# Optimizing a Trainium2 kernel written in Bass

```python
import math
import jax, jax.numpy as jnp
from jax import lax
import numpy as np

D_MODEL = 2048
BATCH = 1
SEQ = 256
DEPTH = 2

HEAD_DIM = 128
A_HEADS = 8
A_WIDTH = A_HEADS * HEAD_DIM
DILATED_BRANCHES = ((128, 1), (512, 4), (2048, 16))
A_QBLOCK = 128
B_WIDTH = D_MODEL - A_WIDTH
B_GROUP = 16
B_GROUPS = B_WIDTH // B_GROUP
B_STATE = 64
DT_MIN = 1e-3
DT_MAX = 1e-1
C_HEADS = D_MODEL // HEAD_DIM
C_WIDTH = C_HEADS * HEAD_DIM
GRID_W = 64
NA_ROWS_MAX = 8
NA_COLS = 16
T5_BUCKETS = 32
T5_MAX_DISTANCE = 1024
D_FF = 4 * D_MODEL
RMS_EPS = 1e-6
NEG_INF = -1e30
N_EVEN = (DEPTH + 1) // 2
N_ODD = DEPTH // 2

kernel_name = "hybrid_dilated_s5_neighbourhood_encoder"

def rmsnorm(x, g):
    x32 = x.astype(jnp.float32)
    y = x32 * lax.rsqrt(jnp.mean(x32 * x32, axis=-1, keepdims=True) + RMS_EPS)
    return (y * g.astype(jnp.float32)).astype(x.dtype)

def t5_bucket(rel):
    half = T5_BUCKETS // 2
    max_exact = half // 2
    n = jnp.abs(rel)
    nf = jnp.maximum(n, 1).astype(jnp.float32)
    large = max_exact + (jnp.log(nf / max_exact) / math.log(T5_MAX_DISTANCE / max_exact)
                         * (half - max_exact)).astype(jnp.int32)
    large = jnp.minimum(large, half - 1)
    return jnp.where(rel > 0, half, 0) + jnp.where(n < max_exact, n, large)

def dilated_branch(q, k, v, t5_table, window, dilation):
    b, h, s, hd = q.shape
    half = window // (2 * dilation)
    L = s // dilation
    nb = -(-L // A_QBLOCK)
    lp = nb * A_QBLOCK
    kb_len = A_QBLOCK + 2 * half
    scale = 1.0 / math.sqrt(hd)

    def strided(t):
        return t.reshape(b, h, L, dilation, hd).transpose(0, 1, 3, 2, 4)

    qs = jnp.pad(strided(q), ((0, 0), (0, 0), (0, 0), (0, lp - L), (0, 0)))
    qs = qs.reshape(b, h, dilation, nb, A_QBLOCK, hd)
    pad_k = ((0, 0), (0, 0), (0, 0), (half, lp - L + half), (0, 0))
    key_idx = jnp.arange(nb)[:, None] * A_QBLOCK + jnp.arange(kb_len)[None, :]
    ks = jnp.pad(strided(k), pad_k)[:, :, :, key_idx]
    vs = jnp.pad(strided(v), pad_k)[:, :, :, key_idx]

    off = jnp.arange(kb_len)[None, :] - half - jnp.arange(A_QBLOCK)[:, None]
    bias = jnp.transpose(t5_table[t5_bucket(off * dilation)], (2, 0, 1)).astype(jnp.float32)
    key_pos = key_idx - half
    valid = (jnp.abs(off) <= half)[None] & ((key_pos >= 0) & (key_pos < L))[:, None, :]

    sc = jnp.einsum('bhrnqc,bhrnkc->bhrnqk', qs, ks) * scale + bias[None, :, None, None]
    sc = jnp.where(valid, sc, NEG_INF)
    m = sc.max(axis=-1)
    p = jnp.exp(sc - m[..., None])
    l = p.sum(axis=-1)
    num = jnp.einsum('bhrnqk,bhrnkc->bhrnqc', p, vs)

    def unstride(t):
        t = t.reshape(b, h, dilation, lp, *t.shape[5:])[:, :, :, :L]
        t = jnp.moveaxis(t, 2, 3)
        return t.reshape(b, h, s, *t.shape[4:])

    return unstride(m), unstride(l), unstride(num)

def dilated_attention(q, k, v, t5_table):
    outs = [dilated_branch(q, k, v, t5_table, w, d) for (w, d) in DILATED_BRANCHES]
    m = jnp.stack([o[0] for o in outs])
    l = jnp.stack([o[1] for o in outs])
    num = jnp.stack([o[2] for o in outs])
    wgt = jnp.exp(m - m.max(axis=0, keepdims=True))
    return (wgt[..., None] * num).sum(0) / (wgt * l).sum(0)[..., None]

def s5_direction(u, lam_re, lam_im, log_step, b_re, b_im, c_re, c_im, reverse):
    f32 = jnp.float32
    step = jnp.exp(log_step.astype(f32))[:, None]
    lr = jnp.minimum(lam_re.astype(f32), -1e-4)
    li = lam_im.astype(f32)
    mag = jnp.exp(lr * step)
    ab_re = mag * jnp.cos(li * step)
    ab_im = mag * jnp.sin(li * step)
    den = lr * lr + li * li
    zr = ((ab_re - 1.0) * lr + ab_im * li) / den
    zi = (ab_im * lr - (ab_re - 1.0) * li) / den
    br = b_re.astype(f32)
    bi = b_im.astype(f32)
    bb_re = zr[..., None] * br - zi[..., None] * bi
    bb_im = zr[..., None] * bi + zi[..., None] * br
    bu_re = jnp.einsum('bsgc,gpc->bsgp', u, bb_re)
    bu_im = jnp.einsum('bsgc,gpc->bsgp', u, bb_im)
    a_re = jnp.broadcast_to(ab_re, bu_re.shape)
    a_im = jnp.broadcast_to(ab_im, bu_im.shape)

    def combine(e1, e2):
        a1r, a1i, b1r, b1i = e1
        a2r, a2i, b2r, b2i = e2
        return (a2r * a1r - a2i * a1i,
                a2r * a1i + a2i * a1r,
                a2r * b1r - a2i * b1i + b2r,
                a2r * b1i + a2i * b1r + b2i)

    _, _, xr, xi = lax.associative_scan(combine, (a_re, a_im, bu_re, bu_im), reverse=reverse, axis=1)
    return (jnp.einsum('bsgp,gcp->bsgc', xr, c_re.astype(f32))
            - jnp.einsum('bsgp,gcp->bsgc', xi, c_im.astype(f32)))

def neighbourhood_attention(q, k, v, rpb):
    b, h, s, hd = q.shape
    rows = s // GRID_W
    kr = min(NA_ROWS_MAX, rows)
    scale = 1.0 / math.sqrt(hd)
    r = jnp.arange(rows)
    c = jnp.arange(GRID_W)
    row_start = jnp.clip(r - kr // 2, 0, rows - kr)
    row_idx = row_start[:, None] + jnp.arange(kr)[None, :]
    col_start = jnp.clip(c - NA_COLS // 2, 0, GRID_W - NA_COLS)
    col_ok = (c[None, :] >= col_start[:, None]) & (c[None, :] < col_start[:, None] + NA_COLS)
    col_off = c[None, :] - c[:, None]
    row_off = row_idx - r[:, None]

    qg = q.reshape(b, h, rows, GRID_W, hd)
    kg = k.reshape(b, h, rows, GRID_W, hd)[:, :, row_idx]
    vg = v.reshape(b, h, rows, GRID_W, hd)[:, :, row_idx]
    bias = rpb[:, (row_off + NA_ROWS_MAX - 1)[:, None, :, None],
               jnp.clip(col_off + NA_COLS - 1, 0, 2 * NA_COLS - 2)[None, :, None, :]]
    sc = jnp.einsum('bhrqc,bhrjkc->bhrqjk', qg, kg) * scale + bias[None].astype(jnp.float32)
    sc = jnp.where(col_ok[:, None, :], sc, NEG_INF)
    p = jax.nn.softmax(sc.reshape(b, h, rows, GRID_W, kr * GRID_W), axis=-1).reshape(sc.shape)
    o = jnp.einsum('bhrqjk,bhrjkc->bhrqc', p, vg)
    return o.reshape(b, h, s, hd)

def mixer_ab(xn, w_in, w_out, t5_table, lam_re, lam_im, log_step, b_re, b_im, c_re, c_im, d_skip, w_glu):
    b, s, _ = xn.shape
    f32 = jnp.float32
    proj = xn @ w_in
    q, k, v, u = jnp.split(proj, [A_WIDTH, 2 * A_WIDTH, 3 * A_WIDTH], axis=-1)

    def heads(t):
        return t.astype(f32).reshape(b, s, A_HEADS, HEAD_DIM).transpose(0, 2, 1, 3)

    o_a = dilated_attention(heads(q), heads(k), heads(v), t5_table)
    o_a = o_a.transpose(0, 2, 1, 3).reshape(b, s, A_WIDTH)

    ug = u.astype(f32).reshape(b, s, B_GROUPS, B_GROUP)
    y = (s5_direction(ug, lam_re[0], lam_im[0], log_step[0], b_re, b_im, c_re[0], c_im[0], False)
         + s5_direction(ug, lam_re[1], lam_im[1], log_step[1], b_re, b_im, c_re[1], c_im[1], True)
         + d_skip.astype(f32).reshape(B_GROUPS, B_GROUP) * ug)
    y = jax.nn.gelu(y.reshape(b, s, B_WIDTH))
    o_b = y * jax.nn.sigmoid((y.astype(xn.dtype) @ w_glu).astype(f32))
    merged = jnp.concatenate([o_a, o_b], axis=-1).astype(xn.dtype)
    return merged @ w_out

def mixer_c(xn, w_qkv, w_out, rpb):
    b, s, _ = xn.shape
    q, k, v = jnp.split(xn @ w_qkv, 3, axis=-1)

    def heads(t):
        return t.astype(jnp.float32).reshape(b, s, C_HEADS, HEAD_DIM).transpose(0, 2, 1, 3)

    o = neighbourhood_attention(heads(q), heads(k), heads(v), rpb)
    o = o.transpose(0, 2, 1, 3).reshape(b, s, C_WIDTH).astype(xn.dtype)
    return o @ w_out

def squared_relu_mlp(xn, w1, w2):
    hdn = jnp.square(jax.nn.relu(xn @ w1))
    return hdn @ w2

def setup_inputs(seed: int = 0) -> dict:
    key = jax.random.key(seed)
    ks = jax.random.split(key, 22)
    f32 = jnp.float32
    nrm = lambda k, shape, sc: (jax.random.normal(k, shape, f32) * sc)
    lam_im_init = jnp.pi * jnp.arange(B_STATE, dtype=f32)
    return {
        "x": nrm(ks[0], (BATCH, SEQ, D_MODEL), 1.0),
        "t5_bias": nrm(ks[1], (T5_BUCKETS, A_HEADS), 0.5),
        "ab_w_in": nrm(ks[2], (N_EVEN, D_MODEL, 3 * A_WIDTH + B_WIDTH), D_MODEL ** -0.5),
        "ab_w_out": nrm(ks[3], (N_EVEN, A_WIDTH + B_WIDTH, D_MODEL), (A_WIDTH + B_WIDTH) ** -0.5),
        "s5_lam_re": -0.5 + nrm(ks[4], (N_EVEN, 2, B_GROUPS, B_STATE), 0.01),
        "s5_lam_im": lam_im_init + nrm(ks[5], (N_EVEN, 2, B_GROUPS, B_STATE), 0.01),
        "s5_log_step": jax.random.uniform(ks[6], (N_EVEN, 2, B_GROUPS), f32,
                                          minval=math.log(DT_MIN), maxval=math.log(DT_MAX)),
        "s5_b_re": nrm(ks[7], (N_EVEN, B_GROUPS, B_STATE, B_GROUP), (2 * B_GROUP) ** -0.5),
        "s5_b_im": nrm(ks[8], (N_EVEN, B_GROUPS, B_STATE, B_GROUP), (2 * B_GROUP) ** -0.5),
        "s5_c_re": nrm(ks[9], (N_EVEN, 2, B_GROUPS, B_GROUP, B_STATE), (2 * B_STATE) ** -0.5),
        "s5_c_im": nrm(ks[10], (N_EVEN, 2, B_GROUPS, B_GROUP, B_STATE), (2 * B_STATE) ** -0.5),
        "s5_d": nrm(ks[11], (N_EVEN, B_WIDTH), 1.0),
        "s5_w_glu": nrm(ks[12], (N_EVEN, B_WIDTH, B_WIDTH), B_WIDTH ** -0.5),
        "c_w_qkv": nrm(ks[13], (N_ODD, D_MODEL, 3 * C_WIDTH), D_MODEL ** -0.5),
        "c_w_out": nrm(ks[14], (N_ODD, C_WIDTH, D_MODEL), C_WIDTH ** -0.5),
        "c_rpb": nrm(ks[15], (N_ODD, C_HEADS, 2 * NA_ROWS_MAX - 1, 2 * NA_COLS - 1), 0.5),
        "norm_mix": 1.0 + nrm(ks[16], (DEPTH, D_MODEL), 0.02),
        "norm_mlp": 1.0 + nrm(ks[17], (DEPTH, D_MODEL), 0.02),
        "mlp_w1": nrm(ks[18], (DEPTH, D_MODEL, D_FF), D_MODEL ** -0.5),
        "mlp_w2": nrm(ks[19], (DEPTH, D_FF, D_MODEL), D_FF ** -0.5),
        "norm_final": 1.0 + nrm(ks[20], (D_MODEL,), 0.02),
    }

def reference(x, t5_bias, ab_w_in, ab_w_out, s5_lam_re, s5_lam_im, s5_log_step, s5_b_re, s5_b_im,
              s5_c_re, s5_c_im, s5_d, s5_w_glu, c_w_qkv, c_w_out, c_rpb, norm_mix, norm_mlp,
              mlp_w1, mlp_w2, norm_final):
    for i in range(DEPTH):
        j = i // 2
        hn = rmsnorm(x, norm_mix[i])
        if i % 2 == 0:
            mix = mixer_ab(hn, ab_w_in[j], ab_w_out[j], t5_bias, s5_lam_re[j], s5_lam_im[j],
                           s5_log_step[j], s5_b_re[j], s5_b_im[j], s5_c_re[j], s5_c_im[j],
                           s5_d[j], s5_w_glu[j])
        else:
            mix = mixer_c(hn, c_w_qkv[j], c_w_out[j], c_rpb[j])
        x = x + mix.astype(x.dtype)
        hn = rmsnorm(x, norm_mlp[i])
        x = x + squared_relu_mlp(hn, mlp_w1[i], mlp_w2[i]).astype(x.dtype)
    return rmsnorm(x, norm_final)


_drawn_inputs = setup_inputs


def setup_inputs(seed=0):
    import zlib

    import numpy as np

    out = dict(_drawn_inputs(seed))
    spreads = {}
    factors = {'s5_lam_re': 8.0,
     's5_b_re': 3.516,
     's5_b_im': 3.508,
     's5_c_re': 3.501,
     's5_c_im': 3.49,
     'norm_mix': 6.109,
     'norm_final': 2.842}
    for name, (base, spread) in spreads.items():
        noise = np.random.default_rng([zlib.crc32(name.encode()), seed]).standard_normal(out[name].shape)
        drawn = base * np.exp(spread * noise) if base else spread * noise
        out[name] = __import__('jax').numpy.asarray(drawn.astype(out[name].dtype))
    for name, factor in factors.items():
        out[name] = (out[name] * factor).astype(out[name].dtype)
    return out
```

```python
from contextlib import ExitStack

import numpy as np

import concourse.bass as bass
from concourse import mybir

F32 = mybir.dt.float32
F32R = mybir.dt.float32r
ALU = mybir.AluOpType
ACT = mybir.ActivationFunctionType
AX_X = mybir.AxisListType.X

P = 128
D = 2048
T = 256
KT = D // P
HD = 128
HA = 8
HC = 16
FF = 4 * D
QUARTER = FF // 4
CH = 16
NST = 64
NG = 64
NPAIR = NG // 2
PT = 4
NT = NPAIR // PT
GRID_W = 64
ROWS = T // GRID_W
RPB_ROWS, RPB_COLS = 15, 31
RPB_PAD = 127
EPS = 1e-6
NEG = -1e30
SCALE = 1.0 / float(np.sqrt(HD))
BLK = 256
SUBK = 4
RAWK = 8
TB = 16
MAGIC = 12582912.0
TWO_PI = 2.0 * np.pi
C1 = 6.28125
C2 = float(np.round((TWO_PI - C1) * 2.0**20) / 2.0**20)
C3 = float(np.float32(TWO_PI - C1 - C2))
GELU_A = 0.044715
GELU_B = float(np.sqrt(2.0 / np.pi))

J_U = 0
J_Q, J_K, J_V = 4, 8, 12
J_GLU = 16
J_OUT0 = J_GLU + 2
J_MLP0 = J_OUT0 + 8
J_QKV1 = J_MLP0 + 64
J_OUT1 = J_QKV1 + 24
J_MLP1 = J_OUT1 + 8
J_END = J_MLP1 + 64


def tile0(j):
    return 2 * j + 2 * min(max(j - J_GLU, 0), 2)


X_BEFORE = [0, 16, 80, 96, 160]


S5_PAIRS = {}
_next = 0
for _j in range(J_Q, J_GLU):
    _n = 3 if _j < J_Q + NPAIR - 2 * (J_GLU - J_Q) else 2
    S5_PAIRS[_j] = list(range(_next, _next + _n))
    _next += _n
SMALL_STEPS = 42


def build(nc, ins, out):
    ctx = ExitStack()
    KB = 1024
    arena = (nc.sbuf_base + 31) // 32 * 32

    def at(name, shape, off, dt=F32):
        return nc.alloc_sbuf_tensor_at(name, shape, dt, offset=arena + int(off))

    with ctx:
        def sem(name):
            return ctx.enter_context(nc.semaphore(name))

        raw = at("raw", [P, 4, RAWK, BLK], 0)
        whl = at("whl", [P, 4, SUBK, 2, BLK], 32 * KB, F32R)
        x = at("x", [P, KT, T], 64 * KB)
        act = at("act", [P, KT, 2, T], 80 * KB, F32R)
        half = at("half", [P, 2, T], 112 * KB)
        ysum = at("ysum", [P, 2, T], 114 * KB)
        ident = at("ident", [P, P], 116 * KB)
        ones = at("ones", [P, P], 116.5 * KB)
        gcol = at("gcol", [P, 88], 117 * KB)
        small = at("small", [P, 64], 117.5 * KB)
        eps_c = small[:, 0:1]
        lstep = small[:, 1:2]
        stat = small[:, 8:32].rearrange("p (a k q) -> p a k q", a=2, k=6)
        U0 = 118 * KB
        q_a = at("q_a", [P, HA, T], U0)
        k_a = at("k_a", [P, HA, T], U0 + 8 * KB)
        v_a = at("v_a", [P, 2, HA * HD], U0 + 16 * KB)
        u = at("u", [P, NT, T], U0 + 24 * KB)
        bt = at("bt", [P, NT, 2, P], U0 + 32 * KB)
        fmat = at("fmat", [P, 2, 2, NPAIR, 2 * CH], U0 + 40 * KB)
        tab0 = at("tab0", [P, 2, 2, NPAIR, TB], U0 + 56 * KB)
        tab1 = at("tab1", [P, 2, 2, NPAIR, TB], U0 + 64 * KB)
        par = at("par", [P, 3, 2, NPAIR], U0 + 72 * KB)
        vs = at("vs", [P, 2, 2, T], U0 + 72.75 * KB)
        tcs = at("tcs", [P, 2, 2, T], U0 + 76.75 * KB)
        pm = at("pm", [P, 2, 2, T], U0 + 80.75 * KB)
        p2 = at("p2", [P, 2, T], U0 + 84.75 * KB)
        xs = at("xs", [P, 2, T], U0 + 86.75 * KB)
        ttmp = at("ttmp", [P, T], U0 + 88.75 * KB)
        ss_a = at("ss_a", [P, 2, 2, T], U0 + 32 * KB)
        bias_a = at("bias_a", [P, 2, 2, T], U0 + 36 * KB)
        cnt_a = at("cnt_a", [P, 2, T], U0 + 40 * KB)
        neg_a = at("neg_a", [P, 2, T], U0 + 42 * KB)
        pt_a = at("pt_a", [P, 2, T], U0 + 44 * KB)
        cnat = at("cnat", [P, 2, 2, NT, 2, NST], U0)
        rows = at("rows", [P, 16, 2 * NST], U0 + 16 * KB)
        t5sb = at("t5sb", [HA, 512], U0 + 24 * KB)
        t5tab = at("t5tab", [32, HA], U0 + 26 * KB)
        onehot = at("onehot", [32, 512], U0 + 27 * KB)
        grow = at("grow", [88, P], U0 + 29 * KB)
        xin = at("xin", [P, 2, D], U0 + 40 * KB)
        bnat = at("bnat", [P, 2, NPAIR, 2 * CH], U0 + 56 * KB)
        zt = at("zt", [P, 2, 3, NPAIR, 2], U0 + 72.75 * KB)
        ctmp = at("ctmp", [P, 2, 2, P], U0 + 74.25 * KB)
        rpbw = at("rpbw", [HC, 7, RPB_PAD], U0 + 76.75 * KB)
        nrm = at("nrm", [P, 4, T], U0 + 80.75 * KB)
        ssum = at("ssum", [P, T], U0 + 84.75 * KB)
        rstd = at("rstd", [P, T], U0 + 85.75 * KB)
        sq = at("sq", [P, T], U0 + 86.75 * KB)
        hid = at("hid", [P, KT, 2, T], U0, F32R)
        hsq = at("hsq", [P, 2, T], U0 + 32 * KB)
        q_c = at("q_c", [P, HC, T], U0)
        k_c = at("k_c", [P, HC, T], U0 + 16 * KB)
        v_c = at("v_c", [P, 2, HC * HD], U0 + 32 * KB)
        ss_c = at("ss_c", [P, 2, 2, T], U0 + 48 * KB)
        bias_c = at("bias_c", [P, 2, 2, T], U0 + 52 * KB)
        neg_c = at("neg_c", [P, 2, T], U0 + 56 * KB)
        pt_c = at("pt_c", [P, 2, T], U0 + 58 * KB)
        xfin = at("xfin", [P, KT, T], U0)
        outs = at("outs", [P, 8, 512], U0 + 16 * KB)

        psum = ctx.enter_context(nc.psum_tensor("psum", [P, 8, 512], F32))

        t5_dram = nc.dram_tensor("t5_rel", [P, HA, 512], F32).ap()
        rpb_dram = nc.dram_tensor("rpb_pad", [GRID_W, HC, 7 * RPB_PAD], F32).ap()

        raw_in = [sem(f"raw_in{s}") for s in range(4)]
        x_in = sem("x_in")
        small_in = sem("small_in")
        rows_in = sem("rows_in")
        b_in, c_in = sem("b_in"), sem("c_in")
        b_zero = sem("b_zero")
        ones_set = sem("ones_set")
        rpb_zero, rpb_in, rpb_out = sem("rpb_zero"), sem("rpb_in"), sem("rpb_out")
        t5_out = sem("t5_out")
        hi_done = sem("hi_done")
        lo_done = sem("lo_done")
        subs_used = sem("subs_used")
        half_done = sem("half_done")
        tiles_out = sem("tiles_out")
        x_tr = sem("x_tr")
        x_ready = sem("x_ready")
        g_tr, g_ready = sem("g_tr"), sem("g_ready")
        t5_mm, t5_ev = sem("t5_mm"), sem("t5_ev")
        sq_done, ssum_done = sem("sq_done"), sem("ssum_done")
        norm_mm, norm_std, norm_rstd = sem("norm_mm"), sem("norm_std"), sem("norm_rstd")
        nrm_done = sem("nrm_done")
        act_hi, act_ready = sem("act_hi"), sem("act_ready")
        resid_sum = sem("resid_sum")
        relu_sum, relu_sq, hid_hi, hid_ready = sem("relu_sum"), sem("relu_sq"), sem("hid_hi"), sem("hid_ready")
        step_v = sem("step_v")
        step_a = sem("step_a")
        par_tr, par_ready = sem("par_tr"), sem("par_ready")
        b_tr, bt_ready = sem("b_tr"), sem("bt_ready")
        c_tr, c_mul, f_ready = sem("c_tr"), sem("c_mul"), sem("f_ready")
        pool_step = sem("pool_step")
        tabs_ready = sem("tabs_ready")
        bu_done, vs_done = sem("bu_done"), sem("vs_done")
        tcs_done, pm_done = sem("tcs_done"), sem("pm_done")
        s5_step = sem("s5_step")
        rot_done, y_mm, y_done = sem("rot_done"), sem("y_mm"), sem("y_done")
        gelu_in, gelu_tanh, gelu_out = sem("gelu_in"), sem("gelu_tanh"), sem("gelu_out")
        y_hi, y_split = sem("y_hi"), sem("y_split")
        glu_sum, glu_tanh, glu_out = sem("glu_sum"), sem("glu_tanh"), sem("glu_out")
        ob_hi, ob_ready = sem("ob_hi"), sem("ob_ready")
        mask_in = sem("mask_in")
        bias_in = [sem("bias_in0"), sem("bias_in1")]
        bias_masked = sem("bias_masked")
        sc_mm, sc_sum, sc_max = sem("sc_mm"), sem("sc_sum"), sem("sc_max")
        exp_done, cnt_done, inv_done, prob_done = sem("exp_done"), sem("cnt_done"), sem("inv_done"), sem("prob_done")
        pt_tr, pt_done, pv_mm, o_hi, o_ready = sem("pt_tr"), sem("pt_done"), sem("pv_mm"), sem("o_hi"), sem("o_ready")
        fin_tr, fin_ev = sem("fin_tr"), sem("fin_ev")
        out_done = sem("out_done")

        block = ctx.enter_context(nc.Block())

        w_in, w_glu, w_out0 = ins["ab_w_in"][0], ins["s5_w_glu"][0], ins["ab_w_out"][0]
        w_qkv, w_out1 = ins["c_w_qkv"][0], ins["c_w_out"][0]
        AW = HA * HD
        STREAM = [
            (J_U, 4, w_in[:, 3 * AW:4 * AW]),
            (J_Q, 12, w_in[:, 0:3 * AW]),
            (J_GLU, 2, w_glu),
            (J_OUT0, 8, w_out0),
        ]

        def mlp_stream(layer, j0):
            w1, w2 = ins["mlp_w1"][layer], ins["mlp_w2"][layer]
            for qu in range(4):
                cols = slice(QUARTER * qu, QUARTER * (qu + 1))
                yield (j0 + 16 * qu, 8, w1[:, cols])
                yield (j0 + 16 * qu + 8, 8, w2[cols, :])

        STREAM += list(mlp_stream(0, J_MLP0))
        STREAM += [(J_QKV1, 24, w_qkv), (J_OUT1, 8, w_out1)]
        STREAM += list(mlp_stream(1, J_MLP1))

        @block.sync
        def _(sp):
            for tt in range(2):
                sp.dma_start(xin[:, tt, :], ins["x"][0, tt * P:(tt + 1) * P, :]).then_inc(x_in, 16)
            for j0, n, w in STREAM:
                wk = w.rearrange("(k p) n -> p k n", p=P)
                if j0 == 0:
                    for r in range(2 * n):
                        if r >= 4:
                            sp.wait_ge(lo_done, 2 * r - 6)
                        src = wk[:, RAWK * (r % 2):RAWK * (r % 2 + 1), r // 2 * BLK:(r // 2 + 1) * BLK]
                        sp.dma_start(raw[:, r % 4], src).then_inc(raw_in[r % 4], 16)
                    continue
                with sp.Fori(0, n // 2) as i:
                    for piece in range(4):
                        sp.wait_ge(lo_done, i * 8 + (4 * j0 + 2 * piece - 6))
                        if j0 == J_GLU:
                            src = wk[:, :, bass.ds(i * (4 * BLK) + piece * BLK, BLK)]
                        else:
                            src = wk[:, RAWK * (piece % 2):RAWK * (piece % 2 + 1),
                                     bass.ds(i * (2 * BLK) + piece // 2 * BLK, BLK)]
                        sp.dma_start(raw[:, piece], src).then_inc(raw_in[piece], 16)
            for g in range(8):
                sp.wait_ge(fin_ev, g + 1)
                sp.dma_start(out[0, (g % 2) * P:(g % 2 + 1) * P, (g // 2) * 512:(g // 2 + 1) * 512],
                             outs[:, g]).then_inc(out_done, 16)
            sp.wait_ge(out_done, 16 * 8)

        @block.gpsimd
        def _(pool):
            pchain = [0]

            def link(instruction):
                pchain[0] += 1
                instruction.then_inc(pool_step, 1)
                pool.wait_ge(pool_step, pchain[0])

            nc.gpsimd.memset(ones[:], 1.0).then_inc(ones_set, 1)
            nc.gpsimd.memset(eps_c, EPS).then_inc(ones_set, 1)
            nc.gpsimd.memset(bnat[:], 0.0).then_inc(b_zero, 1)
            nc.gpsimd.memset(rpbw[:], 0.0).then_inc(rpb_zero, 1)

            def norm_squares(n):
                for kt in range(KT):
                    pool.wait_ge(x_ready, X_BEFORE[n] + kt + 1)
                    if kt == 0:
                        nc.gpsimd.tensor_tensor(ssum[:], x[:, 0], x[:, 0], ALU.mult).then_inc(ssum_done, 1)
                        continue
                    pool.wait_ge(ssum_done, KT * n + kt)
                    nc.gpsimd.tensor_tensor(sq[:], x[:, kt], x[:, kt], ALU.mult).then_inc(sq_done, 1)
                    pool.wait_ge(sq_done, (KT - 1) * n + kt)
                    nc.gpsimd.tensor_tensor(ssum[:], ssum[:], sq[:], ALU.add).then_inc(ssum_done, 1)

            def norm_low(n):
                for kt in range(KT):
                    pool.wait_ge(act_hi, KT * n + kt + 1)
                    nc.gpsimd.tensor_tensor(act[:, kt, 1, :], nrm[:, kt % 4, :], act[:, kt, 0, :].bitcast(F32),
                                            ALU.subtract).then_inc(act_ready, 1)

            norm_squares(0)
            norm_low(0)

            pool.wait_ge(par_ready, 2)
            pool.wait_ge(bt_ready, 4)

            def rot(t, i):
                return t[:, i].rearrange("p d g b -> p (d g) b")

            def angle_add(t, dst, a, b, n):
                ca, sa = rot(t, 0)[:, :, a:a + n], rot(t, 1)[:, :, a:a + n]
                cb = rot(t, 0)[:, :, b:b + 1].to_broadcast([P, 2 * NPAIR, n])
                sb_ = rot(t, 1)[:, :, b:b + 1].to_broadcast([P, 2 * NPAIR, n])
                tmp = p2[:].rearrange("p a t -> p (a t)")[:, 0:2 * NPAIR * n].rearrange("p (g b) -> p g b", b=n)
                co, so = rot(t, 0)[:, :, dst:dst + n], rot(t, 1)[:, :, dst:dst + n]
                link(nc.gpsimd.tensor_tensor(co, ca, cb, ALU.mult))
                link(nc.gpsimd.tensor_tensor(tmp, sa, sb_, ALU.mult))
                link(nc.gpsimd.tensor_tensor(co, co, tmp, ALU.subtract))
                link(nc.gpsimd.tensor_tensor(so, sa, cb, ALU.mult))
                link(nc.gpsimd.tensor_tensor(tmp, ca, sb_, ALU.mult))
                link(nc.gpsimd.tensor_tensor(so, so, tmp, ALU.add))

            for t in (tab0, tab1):
                nc.gpsimd.memset(t[:, 0, :, :, 0], 1.0)
                link(nc.gpsimd.memset(t[:, 1, :, :, 0], 0.0))
            link(nc.gpsimd.tensor_copy(tab0[:, :, :, :, 1], par[:, 1:3]))
            for n in (1, 2, 4):
                angle_add(tab0, n + 1, 1, n, n)
            angle_add(tab0, 9, 1, 8, 7)
            c8, s8 = rot(tab0, 0)[:, :, 8:9], rot(tab0, 1)[:, :, 8:9]
            c16, s16 = rot(tab1, 0)[:, :, 1:2], rot(tab1, 1)[:, :, 1:2]
            tmp = p2[:].rearrange("p a t -> p (a t)")[:, 0:2 * NPAIR].rearrange("p (g b) -> p g b", b=1)
            link(nc.gpsimd.tensor_tensor(c16, c8, c8, ALU.mult))
            link(nc.gpsimd.tensor_tensor(tmp, s8, s8, ALU.mult))
            link(nc.gpsimd.tensor_tensor(c16, c16, tmp, ALU.subtract))
            link(nc.gpsimd.tensor_tensor(s16, s8, c8, ALU.mult))
            link(nc.gpsimd.tensor_tensor(s16, s16, s16, ALU.add))
            for n in (1, 2, 4):
                angle_add(tab1, n + 1, 1, n, n)
            angle_add(tab1, 9, 1, 8, 7)

            pool.wait_ge(rpb_out, 16)
            for pair in range(NPAIR):
                for d in range(2):
                    m = 2 * pair + d
                    if m >= 2:
                        pool.wait_ge(rot_done, m - 1)

                    def outer(i0, i1, dst):
                        a = tab1[:, i1, d, pair, :].unsqueeze(2).to_broadcast([P, TB, TB])
                        b = tab0[:, i0, d, pair, :].unsqueeze(1).to_broadcast([P, TB, TB])
                        return nc.gpsimd.tensor_tensor(dst.rearrange("p (a b) -> p a b", b=TB), a, b, ALU.mult)

                    co, so = tcs[:, m % 2, 0], tcs[:, m % 2, 1]
                    outer(0, 0, co)
                    link(outer(1, 1, ttmp[:]))
                    nc.gpsimd.tensor_tensor(co, co, ttmp[:], ALU.subtract)
                    link(outer(0, 1, so))
                    link(outer(1, 0, ttmp[:]))
                    link(nc.gpsimd.tensor_tensor(so, so, ttmp[:], ALU.add))
                    pool.wait_ge(vs_done, pair + 1)
                    nc.gpsimd.tensor_tensor(pm[:, m % 2], vs[:, pair % 2],
                                            co.unsqueeze(1).to_broadcast([P, 2, T]), ALU.mult).then_inc(pm_done, 1)

            pool.wait_ge(mask_in, 32)
            for h in range(HA):
                pool.wait_ge(bias_in[h % 2], 32 * (h // 2 + 1))
                nc.gpsimd.tensor_tensor(bias_a[:, h % 2], bias_a[:, h % 2], neg_a[:], ALU.add).then_inc(bias_masked, 1)
            norm_squares(1)
            norm_low(1)
            norm_squares(2)
            norm_low(2)
            pool.wait_ge(mask_in, 48)
            for h in range(HC):
                pool.wait_ge(bias_in[h % 2], 32 * HA // 2 + 64 * (h // 2 + 1))
                nc.gpsimd.tensor_tensor(bias_c[:, h % 2], bias_c[:, h % 2], neg_c[:], ALU.add).then_inc(bias_masked, 1)
            norm_squares(3)
            norm_low(3)
            norm_squares(4)

        @block.scalar
        def _(a):
            a.dma_start(ident[:], ins["c_ident"]).then_inc(small_in, 16)
            a.dma_start(onehot[:], ins["c_onehot"]).then_inc(small_in, 16)
            a.dma_start(t5tab[:], ins["t5_bias"]).then_inc(small_in, 16)
            a.dma_start(grow[0:32, :], ins["norm_mix"].rearrange("l (k p) -> (l k) p", p=P)).then_inc(small_in, 16)
            a.dma_start(grow[32:64, :], ins["norm_mlp"].rearrange("l (k p) -> (l k) p", p=P)).then_inc(small_in, 16)
            a.dma_start(grow[64:80, :], ins["norm_final"].rearrange("(k p) -> k p", p=P)).then_inc(small_in, 16)
            a.dma_start(grow[80:88, :], ins["s5_d"][0].rearrange("(k p) -> k p", p=P)).then_inc(small_in, 16)
            for twice in range(2):
                cols = slice(NST * twice, NST * (twice + 1))
                a.dma_start(rows[:, 0, cols], ins["s5_lam_re"][0].rearrange("d g s -> (d g) s")).then_inc(rows_in, 16)
                a.dma_start(rows[:, 1, cols], ins["s5_lam_im"][0].rearrange("d g s -> (d g) s")).then_inc(rows_in, 16)
            a.dma_start(lstep, ins["s5_log_step"].rearrange("a d (g o) -> (a d g) o", o=1)).then_inc(rows_in, 16)
            a.wait_ge(b_zero, 1)
            for i, name in enumerate(("s5_b_re", "s5_b_im")):
                src = ins[name][0].rearrange("(r g) s c -> g s r c", g=2)
                for g in range(2):
                    a.dma_start(bnat[g * NST:(g + 1) * NST, i, :, g * CH:(g + 1) * CH], src[g]).then_inc(b_in, 16)
            a.wait_ge(rpb_zero, 1)
            a.dma_start(rpbw[:, :, 48:48 + RPB_COLS], ins["c_rpb"][0, :, 4:11, :]).then_inc(rpb_in, 16)
            for d in range(2):
                for i, name in enumerate(("s5_c_re", "s5_c_im")):
                    src = ins[name][0, d].rearrange("(t g) c s -> (g c) t s", g=8)
                    for twice in range(2):
                        a.dma_start(cnat[:, d, i, :, twice, :], src).then_inc(c_in, 16)
            a.wait_ge(rpb_in, 16)
            a.dma_start(rpb_dram.rearrange("r h n -> h r n"), rpbw[:].rearrange("h r n -> h (r n)").unsqueeze(1)
                        .to_broadcast([HC, GRID_W, 7 * RPB_PAD])).then_inc(rpb_out, 16)


            def raw_uses(i, j0, jb):
                return i * 16 + 16 * ((j0 + jb) // 2 + 1)

            def high(i, j0, jb, s):
                jp = (j0 + jb) % 2
                piece = 2 * jp + s // 2
                if s % 2 == 0:
                    a.wait_ge(raw_in[piece], raw_uses(i, j0, jb))
                if not (isinstance(i, int) and j0 + 2 * i + jb == 0):
                    a.wait_ge(subs_used, i * 8 + (4 * (j0 + jb) + s - 3))
                nc.scalar.activation(whl[:, s, :, 0, :], raw[:, piece, SUBK * (s % 2):SUBK * (s % 2 + 1), :],
                                     ACT.Copy).then_inc(hi_done, 1)

            def take_halves(i, j0, jb, glu_group=None):
                banks = 2 * ((j0 + jb) % 2 if glu_group is None else glu_group)
                done = 4 * (j0 + jb) + (4 if glu_group is None else 2 * glu_group + 2)
                t = tile0(j0 + jb) + (0 if glu_group is None else 2 * glu_group)
                a.wait_ge(subs_used, i * 8 + done)
                for n in range(2):
                    if t + n >= 2:
                        a.wait_ge(tiles_out, i * 4 + (t + n - 1))
                    nc.scalar.activation(half[:, n], psum[:, banks + n, T:2 * T], ACT.Copy).then_inc(half_done, 1)

            def block_step(i, j0, jb, last=False):
                high(i, j0, jb, 3)
                if not last:
                    for s in range(3):
                        high(i, j0, jb + 1, s)
                take_halves(i, j0, jb)

            def norm(n, base):
                a.wait_ge(norm_mm, n + 1)
                nc.scalar.activation(rstd[:], psum[:, 7, 0:T], ACT.Sqrt, bias=eps_c, scale=1.0 / D).then_inc(norm_std, 1)
                if n == 4:
                    return
                for kt in range(KT):
                    a.wait_ge(nrm_done, KT * n + kt + 1)
                    nc.scalar.activation(act[:, kt, 0, :], nrm[:, kt % 4, :], ACT.Copy).then_inc(act_hi, 1)

            def loop_blocks(j0, n, last=False):
                with a.Fori(0, n // 2 - (1 if last else 0)) as i:
                    block_step(i, j0, 0)
                    block_step(i, j0, 1)
                if last:
                    block_step(n // 2 - 1, j0, 0)
                    block_step(n // 2 - 1, j0, 1, last=True)

            a.wait_ge(rows_in, 16 * 5)
            nc.scalar.activation(lstep, lstep, ACT.Exp).then_inc(step_a, 1)
            a.wait_ge(step_v, 1)
            a.wait_ge(step_a, 1)
            nc.scalar.activation(rows[:, 3], rows[:, 0], ACT.Exp, scale=lstep).then_inc(step_a, 1)
            a.wait_ge(t5_mm, 1)
            nc.scalar.activation(t5sb[:], psum[0:HA, 1, :], ACT.Copy).then_inc(t5_ev, 1)
            a.wait_ge(t5_ev, 1)
            a.dma_start(t5_dram.rearrange("r h n -> h r n"),
                        t5sb[:].unsqueeze(1).to_broadcast([HA, P, 512])).then_inc(t5_out, 16)
            for s in range(3):
                high(0, 0, 0, s)
            a.wait_ge(ones_set, 2)
            norm(0, 0)
            block_step(0, 0, 0)
            for g in range(4):
                a.wait_ge(b_tr, g + 1)
                nc.scalar.activation(bt[:, 2 * g:2 * g + 2].rearrange("p t i s -> p (t i s)"), psum[:, 6 + g % 2, :],
                                     ACT.Copy).then_inc(bt_ready, 1)
            for j in range(1, 4):
                block_step(0, j, 0)

            def take_bu(pair):
                if pair >= NPAIR:
                    return
                a.wait_ge(bu_done, pair + 1)
                if pair >= 2:
                    a.wait_ge(rot_done, 2 * pair - 2)
                elif pair == 0:
                    a.wait_ge(f_ready, 2 * 2 * NT)
                nc.scalar.activation(vs[:, pair % 2].rearrange("p i t -> p (i t)"), psum[:, 4 + pair % 2, :],
                                     ACT.Copy).then_inc(vs_done, 1)

            take_bu(0)
            for j in range(J_Q, J_GLU):
                pairs = S5_PAIRS[j]
                high(0, j, 0, 3)
                if j > J_Q:
                    take_halves(0, j - 1, 0)
                for k in range(3):
                    if k < len(pairs):
                        take_bu(pairs[k] + 1)
                    high(0, j, 1, k)
                    if k < len(pairs) and pairs[k] % PT == PT - 1:
                        t = pairs[k] // PT
                        a.wait_ge(gelu_in, t + 1)
                        nc.scalar.activation(p2[:, 1], p2[:, 0], ACT.Tanh, scale=GELU_B).then_inc(gelu_tanh, 1)
            take_halves(0, J_GLU - 1, 0)
            a.wait_ge(y_done, NT)
            a.dma_start(cnt_a[:], ins["c_cnt"]).then_inc(mask_in, 16)
            a.dma_start(neg_a[:], ins["c_neg_a"]).then_inc(mask_in, 16)
            a.wait_ge(t5_out, 16)
            a.wait_ge(rpb_out, 16)

            def load_bias_a(h):
                for qt in range(2):
                    skew = bass.AP(tensor=t5_dram.tensor, offset=h * 512 + 255 - P * qt, ap=[[HA * 512 - 1, P], [1, T]])
                    a.dma_start(bias_a[:, h % 2, qt, :], skew).then_inc(bias_in[h % 2], 16)

            def load_bias_c(h):
                for r in range(ROWS):
                    skew = bass.AP(tensor=rpb_dram.tensor, offset=(h * 7 + 3 - r) * RPB_PAD + GRID_W - 1,
                                   ap=[[HC * 7 * RPB_PAD - 1, GRID_W], [RPB_PAD, ROWS], [1, GRID_W]])
                    dst = bias_c[GRID_W * (r % 2):GRID_W * (r % 2 + 1), h % 2, r // 2, :]
                    a.dma_start(dst.rearrange("p (r c) -> p r c", r=ROWS), skew).then_inc(bias_in[h % 2], 16)

            def heads(base, count, ss, pt, load_bias, sums):
                def exps(h):
                    for qt in range(2):
                        a.wait_ge(sc_max, base + h + 1)
                        extra = {"accum_out": stat[:, h % 2, 1, qt:qt + 1]} if sums else {}
                        nc.scalar.activation(ss[:, h % 2, qt], ss[:, h % 2, qt], ACT.Exp,
                                             bias=stat[:, h % 2, 0, qt:qt + 1], **extra).then_inc(exp_done, 1)

                exps(0)
                for h in range(count):
                    if h + 2 < count:
                        a.wait_ge(sc_sum, base + h + 1)
                        load_bias(h + 2)
                    if h + 1 < count:
                        exps(h + 1)
                    a.wait_ge(pt_tr, base + h + 1)
                    if h >= 1:
                        a.wait_ge(pv_mm, base + h)
                    nc.scalar.activation(pt[:].rearrange("p k t -> p (k t)"), psum[:, 6, :], ACT.Copy).then_inc(pt_done, 1)
                    a.wait_ge(pv_mm, base + h + 1)
                    nc.scalar.activation(act[:, h, 0, :], psum[:, 7, 0:T], ACT.Copy).then_inc(o_hi, 1)

            load_bias_a(0)
            load_bias_a(1)
            for t in range(NT):
                a.wait_ge(gelu_out, t + 1)
                nc.scalar.activation(act[:, NT + t, 0, :], u[:, t], ACT.Copy).then_inc(y_hi, 1)
            heads(0, HA, ss_a, pt_a, load_bias_a, False)

            def glu_half(jb, g):
                take_halves(0, J_GLU + jb, 0, glu_group=g)
                for n in range(2):
                    f = 4 * jb + 2 * g + n
                    a.wait_ge(tiles_out, tile0(J_GLU + jb) + 2 * g + n + 1)
                    nc.scalar.activation(ysum[:, n], ysum[:, n], ACT.Tanh, scale=0.5).then_inc(glu_tanh, 1)

            for jb in range(2):
                high(0, J_GLU + jb, 0, 3)
                for s in range(3):
                    high(0, J_GLU + jb + 1, 0, s)
                glu_half(jb, 0)
                glu_half(jb, 1)
            for f in range(NT):
                a.wait_ge(glu_out, f + 1)
                nc.scalar.activation(act[:, NT + f, 0, :], u[:, f], ACT.Copy, scale=0.5).then_inc(ob_hi, 1)
            loop_blocks(J_OUT0, 8)
            norm(1, 0)
            for k in range(8):
                loop_blocks(J_MLP0 + 8 * k, 8)
            norm(2, 0)
            a.dma_start(neg_c[:], ins["c_neg_c"]).then_inc(mask_in, 16)
            load_bias_c(0)
            load_bias_c(1)
            loop_blocks(J_QKV1, 24)
            heads(HA, HC, ss_c, pt_c, load_bias_c, True)
            loop_blocks(J_OUT1, 8)
            norm(3, 0)
            for k in range(8):
                loop_blocks(J_MLP1 + 8 * k, 8, last=(k == 7))
            norm(4, 0)
            for g in range(8):
                a.wait_ge(fin_tr, g + 1)
                nc.scalar.activation(outs[:, g], psum[:, g % 4, :], ACT.Copy).then_inc(fin_ev, 1)

        @block.vector
        def _(v):
            vchain = [0]

            def link(instruction):
                vchain[0] += 1
                instruction.then_inc(step_v, 1)
                v.wait_ge(step_v, vchain[0])

            def ts(dst, src, c0, c1, op0=ALU.mult, op1=ALU.add):
                return nc.vector.tensor_scalar(dst, src, c0, c1, op0, op1)

            def tt(dst, s0, s1, op):
                return nc.vector.tensor_tensor(dst, s0, s1, op)

            def stt(dst, s0, c, s1, op0, op1):
                return nc.vector.scalar_tensor_tensor(out=dst, in0=s0, scalar=c, in1=s1, op0=op0, op1=op1)

            R = [rows[:, k] for k in range(16)]
            v.wait_ge(rows_in, 16 * 5)
            link(nc.vector.tensor_scalar(R[0], R[0], -1e-4, None, ALU.min))
            v.wait_ge(step_a, 1)
            link(nc.vector.tensor_scalar(R[2], R[1], lstep, None, ALU.mult))
            link(ts(R[4], R[2], 1.0 / TWO_PI, MAGIC))
            link(nc.vector.tensor_scalar(R[4], R[4], MAGIC, None, ALU.subtract))
            link(stt(R[5], R[4], -C1, R[2], ALU.mult, ALU.add))
            link(stt(R[5], R[4], -C2, R[5], ALU.mult, ALU.add))
            link(stt(R[5], R[4], -C3, R[5], ALU.mult, ALU.add))
            link(nc.vector.tensor_scalar(R[5], R[5], 0.25, None, ALU.mult))
            link(tt(R[6], R[5], R[5], ALU.mult))
            link(nc.vector.tensor_scalar(R[7], R[6], 1.0 / 362880, None, ALU.mult))
            for c in (-1.0 / 5040, 1.0 / 120, -1.0 / 6):
                link(stt(R[7], R[7], c, R[6], ALU.add, ALU.mult))
            link(stt(R[7], R[7], 1.0, R[5], ALU.add, ALU.mult))
            link(nc.vector.tensor_scalar(R[8], R[6], -1.0 / 3628800, None, ALU.mult))
            for c in (1.0 / 40320, -1.0 / 720, 1.0 / 24, -0.5):
                link(stt(R[8], R[8], c, R[6], ALU.add, ALU.mult))
            link(nc.vector.tensor_scalar(R[8], R[8], 1.0, None, ALU.add))
            for s_, c_, s2, c2 in ((7, 8, 11, 8), (11, 8, 13, 14)):
                link(stt(R[s2], R[s_], 2.0, R[c_], ALU.mult, ALU.mult))
                link(stt(R[12], R[s_], -2.0, R[s_], ALU.mult, ALU.mult))
                link(nc.vector.tensor_scalar(R[c2], R[12], 1.0, None, ALU.add))
            v.wait_ge(step_a, 2)
            link(tt(R[9], R[3], R[14], ALU.mult))
            link(nc.vector.tensor_scalar(R[9], R[9], 1.0, None, ALU.subtract))
            link(tt(R[10], R[3], R[13], ALU.mult))
            link(tt(R[12], R[0], R[0], ALU.mult))
            link(tt(R[11], R[1], R[1], ALU.mult))
            link(tt(R[12], R[12], R[11], ALU.add))
            link(nc.vector.reciprocal(R[12], R[12]))
            link(tt(R[5], R[9], R[0], ALU.mult))
            link(tt(R[6], R[10], R[1], ALU.mult))
            link(tt(R[5], R[5], R[6], ALU.add))
            link(tt(R[5], R[5], R[12], ALU.mult))
            link(tt(R[6], R[10], R[0], ALU.mult))
            link(tt(R[7], R[9], R[1], ALU.mult))
            link(tt(R[6], R[6], R[7], ALU.subtract))
            link(tt(R[6], R[6], R[12], ALU.mult))
            link(nc.vector.memset(zt[:], 0.0))
            assert vchain[0] == SMALL_STEPS, vchain[0]

            for g in range(KT // 2):
                v.wait_ge(x_tr, g + 1)
                nc.vector.tensor_copy(x[:, 2 * g:2 * g + 2].rearrange("p k t -> p (k t)"),
                                      psum[:, 4 + g % 4, :]).then_inc(x_ready, 2)
            v.wait_ge(g_tr, 1)
            nc.vector.tensor_copy(gcol[:], psum[:, 0, 0:88]).then_inc(g_ready, 1)

            def low(i, j0, jb, s):
                jp = (j0 + jb) % 2
                piece = 2 * jp + s // 2
                v.wait_ge(hi_done, i * 8 + (4 * (j0 + jb) + s + 1))
                tt(whl[:, s, :, 1, :], raw[:, piece, SUBK * (s % 2):SUBK * (s % 2 + 1), :],
                   whl[:, s, :, 0, :].bitcast(F32), ALU.subtract).then_inc(lo_done, 1)

            def tile_sum(i, j0, jb, n, dst, glu_group=None):
                banks = 2 * ((j0 + jb) % 2 if glu_group is None else glu_group)
                t = tile0(j0 + jb) + (0 if glu_group is None else 2 * glu_group)
                v.wait_ge(half_done, i * 4 + (t + n + 1))
                tt(dst, psum[:, banks + n, 0:T], half[:, n], ALU.add).then_inc(tiles_out, 1)
                return i * 4 + (t + n + 1)

            def store(dst_of):
                def evac(i, j0, jb):
                    for n in range(2):
                        tile_sum(i, j0, jb, n, dst_of(i, j0, jb, n))
                return evac

            def residual(x0):
                def evac(i, j0, jb):
                    v.wait_ge(x_ready, i * 4 + (x0 + 2 * jb))
                    for n in range(2):
                        tile_sum(i, j0, jb, n, ysum[:, n])
                    for n in range(2):
                        v.wait_ge(tiles_out, i * 4 + (tile0(j0 + jb) + n + 1))
                        dst = x[:, bass.ds(i * 4 + (2 * jb + n), 1), :].rearrange("p o t -> p (o t)")
                        tt(dst, dst, ysum[:, n], ALU.add).then_inc(x_ready, 1)
                return evac

            def squared_relu(h0):
                def evac(i, j0, jb):
                    at_ = [i * 4 + (h0 + 2 * jb + n + 1) for n in range(2)]

                    def dst(n, part):
                        return hid[:, bass.ds(i * 4 + (2 * jb + n), 1), part, :].rearrange("p o t -> p (o t)")

                    if not (isinstance(i, int) and i * 4 + h0 + 2 * jb == 0):
                        v.wait_ge(relu_sq, i * 4 + (h0 + 2 * jb))
                        v.wait_ge(hid_ready, i * 4 + (h0 + 2 * jb))
                    for n in range(2):
                        tile_sum(i, j0, jb, n, ysum[:, n])
                    for n in range(2):
                        v.wait_ge(tiles_out, i * 4 + (tile0(j0 + jb) + n + 1))
                        stt(hsq[:, n], ysum[:, n], 0.0, ysum[:, n], ALU.max, ALU.mult).then_inc(relu_sq, 1)
                    for n in range(2):
                        v.wait_ge(relu_sq, at_[n])
                        nc.vector.tensor_copy(dst(n, 0), hsq[:, n]).then_inc(hid_hi, 1)
                    for n in range(2):
                        v.wait_ge(hid_hi, at_[n])
                        tt(dst(n, 1), hsq[:, n], dst(n, 0).bitcast(F32), ALU.subtract).then_inc(hid_ready, 1)
                return evac

            def block_step(i, j0, jb, evac, last=False):
                low(i, j0, jb, 3)
                if not last:
                    for s in range(3):
                        low(i, j0, jb + 1, s)
                evac(i, j0, jb)

            def loop_blocks(j0, n, evac, first=False, last=False):
                if first:
                    block_step(0, j0, 0, evac)
                    block_step(0, j0, 1, evac)
                with v.Fori(1 if first else 0, n // 2 - (1 if last else 0)) as i:
                    block_step(i, j0, 0, evac)
                    block_step(i, j0, 1, evac)
                if last:
                    block_step(n // 2 - 1, j0, 0, evac)
                    block_step(n // 2 - 1, j0, 1, evac, last=True)

            def norm(n, gains):
                v.wait_ge(norm_std, n + 1)
                nc.vector.reciprocal(rstd[:], rstd[:]).then_inc(norm_rstd, 1)
                v.wait_ge(norm_rstd, n + 1)
                for kt in range(KT):
                    if n == 4:
                        dst = xfin[:, kt]
                    else:
                        dst = nrm[:, kt % 4]
                        if kt >= 4:
                            v.wait_ge(act_ready, KT * n + kt - 3)
                    stt(dst, x[:, kt], gcol[:, gains + kt:gains + kt + 1], rstd[:], ALU.mult, ALU.mult) \
                        .then_inc(nrm_done, 1)

            for s in range(3):
                low(0, 0, 0, s)
            v.wait_ge(g_ready, 1)
            norm(0, 0)
            v.wait_ge(t5_out, 16)
            u_store = store(lambda i, j0, jb, n: u[:, 2 * (j0 + jb - J_U) + n])
            block_step(0, 0, 0, u_store)

            v.wait_ge(par_tr, 1)
            pv_ = psum[:, 4, :].rearrange("p (k r g) -> p k r g", k=4, g=2)
            zi_ = psum[:, 5, 0:P].rearrange("p (r g) -> p r g", g=2)
            for g in range(2):
                s_ = slice(NST * g, NST * (g + 1))
                nc.vector.tensor_copy(par[s_].rearrange("p k d r -> p k (d r)"), pv_[s_, 0:3, :, g]).then_inc(par_ready, 1)
            for g in range(2):
                s_ = slice(NST * g, NST * (g + 1))
                zr = pv_[s_, 3, :, g].rearrange("p (d r) -> p d r", d=2)
                zi = zi_[s_, :, g].rearrange("p (d r) -> p d r", d=2)
                for k, src, sign in ((0, zr, 1.0), (1, zi, -1.0), (2, zr, -1.0)):
                    nc.vector.tensor_scalar(zt[s_, :, k, :, g], src, sign, None, ALU.mult).then_inc(par_ready, 1)
            block_step(0, 1, 0, u_store)
            block_step(0, 2, 0, u_store)
            v.wait_ge(par_ready, 8)
            v.wait_ge(x_tr, 8)
            for c in range(2 * NT):
                d, t = c // NT, c % NT
                v.wait_ge(c_tr, c + 1)
                if c:
                    v.wait_ge(f_ready, 2 * c)
                src = psum[:, 4 + c % 2, 0:2 * P].rearrange("p (i r c) -> p i r c", i=2, c=CH)
                for k in range(2):
                    z = zt[:, d, k:k + 2, PT * t:PT * (t + 1), :].rearrange("p i r g -> p i (r g)")
                    tt(ctmp[:, k].rearrange("p i (r c) -> p i r c", c=CH), src,
                       z.unsqueeze(3).to_broadcast([P, 2, 2 * PT, CH]), ALU.mult).then_inc(c_mul, 1)
                for k in range(2):
                    v.wait_ge(c_mul, 2 * c + k + 1)
                    tt(fmat[:, d, k, PT * t:PT * (t + 1), :].rearrange("p r c -> p (r c)"),
                       ctmp[:, k, 0], ctmp[:, k, 1], ALU.add).then_inc(f_ready, 1)
            block_step(0, 3, 0, u_store)

            schain = [0]

            def s5_link(*instructions):
                for instruction in instructions:
                    schain[0] += 1
                    instruction.then_inc(s5_step, 1)
                v.wait_ge(s5_step, schain[0])

            def s5_pair(pair):
                for d in range(2):
                    m = 2 * pair + d
                    sl = m % 2
                    add, sub = (ALU.add, ALU.subtract) if d == 0 else (ALU.subtract, ALU.add)
                    sine = tcs[:, sl, 1].unsqueeze(1).to_broadcast([P, 2, T])
                    cosine = tcs[:, sl, 0].unsqueeze(1).to_broadcast([P, 2, T])
                    v.wait_ge(pm_done, m + 1)
                    s5_link(tt(p2[:], vs[:, pair % 2, ::-1], sine, ALU.mult))
                    s5_link(tt(pm[:, sl, 0], pm[:, sl, 0], p2[:, 0], add),
                            tt(pm[:, sl, 1], pm[:, sl, 1], p2[:, 1], sub))
                    r = par[:, 0, d, pair:pair + 1].to_broadcast([P, T])
                    step = 1 if d == 0 else -1
                    s5_link(*[nc.vector.tensor_tensor_scan(p2[:, i, ::step], r, pm[:, sl, i, ::step], 0.0,
                                                           ALU.mult, ALU.add) for i in range(2)])
                    if m >= 1:
                        v.wait_ge(y_mm, m)
                    s5_link(tt(pm[:, sl], p2[:], cosine, ALU.mult), tt(xs[:], p2[:, ::-1], sine, ALU.mult))
                    tt(xs[:, 0], pm[:, sl, 0], xs[:, 0], sub).then_inc(s5_step, 1)
                    tt(xs[:, 1], pm[:, sl, 1], xs[:, 1], add).then_inc(rot_done, 1)
                    schain[0] += 1
                    v.wait_ge(s5_step, schain[0])
                if pair % PT == PT - 1:
                    t = pair // PT
                    v.wait_ge(y_mm, 2 * pair + 2)
                    stt(u[:, t], u[:, t], gcol[:, 80 + t:81 + t], psum[:, 6 + t % 2, 0:T], ALU.mult, ALU.add) \
                        .then_inc(y_done, 1)
                    v.wait_ge(y_done, t + 1)
                    v.wait_ge(rot_done, 2 * pair + 2)
                    s5_link(tt(p2[:, 0], u[:, t], u[:, t], ALU.mult))
                    s5_link(ts(p2[:, 0], p2[:, 0], GELU_A, 1.0))
                    tt(p2[:, 0], p2[:, 0], u[:, t], ALU.mult).then_inc(gelu_in, 1)
                    v.wait_ge(gelu_tanh, t + 1)
                    s5_link(ts(p2[:, 1], p2[:, 1], 0.5, 0.5))
                    tt(u[:, t], p2[:, 1], u[:, t], ALU.mult).then_inc(gelu_out, 1)
                    v.wait_ge(gelu_out, t + 1)

            q_store = store(lambda i, j0, jb, n: q_a[:, 2 * (j0 + jb - J_Q) + n])
            k_store = store(lambda i, j0, jb, n: k_a[:, 2 * (j0 + jb - J_K) + n])
            v_store = store(lambda i, j0, jb, n: v_a[:, n, BLK * (j0 + jb - J_V):BLK * (j0 + jb - J_V + 1)])
            kinds = [q_store] * 4 + [k_store] * 4 + [v_store] * 4
            for j in range(J_Q, J_GLU):
                pairs = S5_PAIRS[j]
                low(0, j, 0, 3)
                if j > J_Q:
                    kinds[j - 1 - J_Q](0, j - 1, 0)
                for k in range(3):
                    if k < len(pairs):
                        s5_pair(pairs[k])
                    low(0, j, 1, k)
            kinds[-1](0, J_GLU - 1, 0)
            for t in range(NT):
                v.wait_ge(y_hi, t + 1)
                tt(act[:, NT + t, 1, :], u[:, t], act[:, NT + t, 0, :].bitcast(F32), ALU.subtract).then_inc(y_split, 1)

            def heads(base, count, ss, bias, cnt):
                def scores(h):
                    hh, b = base + h, h % 2
                    v.wait_ge(sc_mm, hh + 1)
                    v.wait_ge(bias_masked, hh + 1)
                    if h >= 2:
                        v.wait_ge(pt_tr, hh - 1)
                    stt(ss[:, b].rearrange("p q t -> p (q t)"), psum[:, 4 + b, :], SCALE,
                        bias[:, b].rearrange("p q t -> p (q t)"), ALU.mult, ALU.add).then_inc(sc_sum, 1)
                    v.wait_ge(sc_sum, hh + 1)
                    nc.vector.tensor_reduce(stat[:, b, 0], ss[:, b], AX_X, ALU.max, negate=True).then_inc(sc_max, 1)

                def probs(h):
                    hh, b = base + h, h % 2
                    v.wait_ge(exp_done, 2 * hh + 2)
                    if cnt is not None:
                        for qt in range(2):
                            nc.vector.scalar_tensor_tensor(out=ss[:, b, qt], in0=ss[:, b, qt], scalar=1.0,
                                                           in1=cnt[:, qt], op0=ALU.mult, op1=ALU.mult,
                                                           accum_out=stat[:, b, 1, qt:qt + 1]).then_inc(cnt_done, 1)
                        v.wait_ge(cnt_done, 2 * hh + 2)
                    nc.vector.reciprocal(stat[:, b, 2], stat[:, b, 1]).then_inc(inv_done, 1)
                    v.wait_ge(inv_done, hh + 1)
                    for qt in range(2):
                        last = nc.vector.tensor_scalar(ss[:, b, qt], ss[:, b, qt], stat[:, b, 2, qt:qt + 1],
                                                       None, ALU.mult)
                        last.then_inc(prob_done, 1)

                def out_low(h):
                    v.wait_ge(o_hi, base + h + 1)
                    tt(act[:, h, 1, :], psum[:, 7, 0:T], act[:, h, 0, :].bitcast(F32), ALU.subtract).then_inc(o_ready, 1)

                scores(0)
                for h in range(count):
                    if h + 1 < count:
                        scores(h + 1)
                    if h >= 1:
                        out_low(h - 1)
                    probs(h)
                out_low(count - 1)

            v.wait_ge(mask_in, 32)
            heads(0, HA, ss_a, bias_a, cnt_a)

            for jb in range(2):
                low(0, J_GLU + jb, 0, 3)
                for s in range(3):
                    low(0, J_GLU + jb + 1, 0, s)
                for g in range(2):
                    if jb or g:
                        v.wait_ge(glu_out, 4 * jb + 2 * g)
                    for n in range(2):
                        tile_sum(0, J_GLU + jb, 0, n, ysum[:, n], glu_group=g)
                    for n in range(2):
                        f = 4 * jb + 2 * g + n
                        v.wait_ge(glu_tanh, f + 1)
                        stt(u[:, f], ysum[:, n], 1.0, u[:, f], ALU.add, ALU.mult).then_inc(glu_out, 1)
            for f in range(NT):
                v.wait_ge(ob_hi, f + 1)
                stt(act[:, NT + f, 1, :], u[:, f], 0.5, act[:, NT + f, 0, :].bitcast(F32), ALU.mult, ALU.subtract) \
                    .then_inc(ob_ready, 1)
            loop_blocks(J_OUT0, 8, residual(16))
            norm(1, 32)

            def mlp(j0, x0, h0, last):
                for qu in range(4):
                    v.wait_ge(x_ready, x0 + 16 * qu)
                    loop_blocks(j0 + 16 * qu, 8, squared_relu(h0 + 16 * qu), first=(h0 + qu == 0))
                    v.wait_ge(relu_sq, h0 + 16 * (qu + 1))
                    loop_blocks(j0 + 16 * qu + 8, 8, residual(x0 + 16 * qu), last=(last and qu == 3))

            mlp(J_MLP0, 32, 0, False)
            norm(2, 16)

            def head_major(dst, first):
                return store(lambda i, j0, jb, n: dst[:, bass.ds(i * 4 + (2 * jb + n), 1), :].rearrange("p o t -> p (o t)"))

            loop_blocks(J_QKV1, 8, head_major(q_c, 0))
            loop_blocks(J_QKV1 + 8, 8, head_major(k_c, 0))
            loop_blocks(J_QKV1 + 16, 8, store(lambda i, j0, jb, n: v_c[:, n, bass.ds(i * (2 * BLK) + BLK * jb, BLK)]))
            heads(HA, HC, ss_c, bias_c, None)
            loop_blocks(J_OUT1, 8, residual(96))
            norm(3, 48)
            mlp(J_MLP1, 112, 64, True)
            norm(4, 64)

        @block.tensor
        def _(pe):
            pe.wait_ge(small_in, 16 * 7)
            pe.transpose(psum[:, 0, 0:88], grow[:, :], ident[0:88, 0:88]).then_inc(g_tr, 1)
            pe.matmul(psum[0:HA, 1, :], t5tab[:], onehot[:], start=True, stop=True).then_inc(t5_mm, 1)
            pe.wait_ge(x_in, 32)
            for g in range(KT // 2):
                if g >= 4:
                    pe.wait_ge(x_ready, 2 * (g - 3))
                for k in range(2):
                    for tt_ in range(2):
                        kt = 2 * g + k
                        last = pe.transpose(psum[:, 4 + g % 4, k * T + tt_ * P:k * T + (tt_ + 1) * P],
                                            xin[:, tt_, kt * P:(kt + 1) * P], ident[:])
                last.then_inc(x_tr, 1)

            def norm(n):
                pe.wait_ge(ssum_done, KT * (n + 1))
                pe.matmul(psum[:, 7, 0:T], ones[:], ssum[:], start=True, stop=True).then_inc(norm_mm, 1)

            def block_mm(i, j0, jb, operand, ready, token_major=False, between=None):
                banks = 2 * ((j0 + jb) % 2)
                t = tile0(j0 + jb)
                if t >= 4:
                    pe.wait_ge(tiles_out, i * 4 + (t - 2))
                for s in range(4):
                    pe.wait_ge(lo_done, i * 8 + (4 * (j0 + jb) + s + 1))
                    for k in range(SUBK):
                        kt = SUBK * s + k
                        ready(kt)
                        first, final = kt == 0, kt == KT - 1
                        for n in range(2):
                            cols = slice(n * P, (n + 1) * P)
                            if token_major:
                                w_hi, w_all = whl[:, s, k, 0, :], whl[:, s, k, :, :].rearrange("p h t -> p (h t)")
                                big = (operand[:, kt, 0, cols], w_all)
                                little = (operand[:, kt, 1, cols], w_hi)
                            else:
                                big = (whl[:, s, k, 0, cols], operand[:, kt, :, :].rearrange("p h t -> p (h t)"))
                                little = (whl[:, s, k, 1, cols], operand[:, kt, 0, :])
                            bank = psum[:, banks + n]
                            pe.matmul(bank, *big, start=first, stop=False, skip_group_check=True)
                            last = pe.matmul(bank[:, 0:T], *little, start=False, stop=final, skip_group_check=True)
                    last.then_inc(subs_used, 1)
                    if between:
                        between(s)

            def by_count(semaphore, base, group=2):
                def ready(kt):
                    if kt % group == 0:
                        pe.wait_ge(semaphore, base + kt + group)
                return ready

            def nothing(kt):
                pass

            def loop_blocks(j0, n, operand, ready, token_major=False):
                with pe.Fori(0, n // 2) as i:
                    block_mm(i, j0, 0, operand, ready, token_major)
                    block_mm(i, j0, 1, operand, ready, token_major)

            pe.wait_ge(ones_set, 1)
            pe.wait_ge(x_ready, 16)
            norm(0)
            pe.wait_ge(g_ready, 1)
            pe.wait_ge(t5_ev, 1)
            block_mm(0, 0, 0, act, by_count(act_ready, 0))
            pe.wait_ge(step_v, SMALL_STEPS)
            pe.wait_ge(step_a, 2)
            for k, src in enumerate((3, 14, 13, 5, 6)):
                last = pe.transpose(psum[:, 4 + k // 4, (k % 4) * P:(k % 4 + 1) * P], rows[:, src], ident[:])
            last.then_inc(par_tr, 1)
            pe.wait_ge(b_in, 16 * 4)
            pe.wait_ge(norm_std, 1)
            for g in range(4):
                if g >= 2:
                    pe.wait_ge(bt_ready, g - 1)
                for k in range(4):
                    t, i = 2 * g + k // 2, k % 2
                    last = pe.transpose(psum[:, 6 + g % 2, k * P:(k + 1) * P],
                                        bnat[:, i, PT * t:PT * (t + 1), :].rearrange("p r c -> p (r c)"), ident[:])
                last.then_inc(b_tr, 1)
            block_mm(0, 1, 0, act, nothing)
            block_mm(0, 2, 0, act, nothing)
            pe.wait_ge(c_in, 16 * 8)
            pe.wait_ge(par_ready, 8)
            for c in range(2 * NT):
                d, t = c // NT, c % NT
                if c >= 2:
                    pe.wait_ge(c_mul, 2 * (c - 1))
                for i in range(2):
                    last = pe.transpose(psum[:, 4 + c % 2, i * P:(i + 1) * P],
                                        cnat[:, d, i, t].rearrange("p w s -> p (w s)"), ident[:])
                last.then_inc(c_tr, 1)
            block_mm(0, 3, 0, act, nothing)

            def s5_in(pair):
                if pair >= NPAIR:
                    return
                t, r = pair // PT, slice(32 * (pair % PT), 32 * (pair % PT + 1))
                if pair >= 2:
                    pe.wait_ge(vs_done, pair - 1)
                else:
                    pe.wait_ge(c_mul, 4 * NT)
                for i in range(2):
                    last = pe.matmul(psum[:, 4 + pair % 2, i * T:(i + 1) * T], bt[r, t, i, :], u[r, t, :],
                                     start=True, stop=True)
                last.then_inc(bu_done, 1)

            def s5_out(pair):
                t, r = pair // PT, slice(32 * (pair % PT), 32 * (pair % PT + 1))
                if t >= 2 and pair % PT == 0:
                    pe.wait_ge(y_done, t - 1)
                elif t == 0:
                    pe.wait_ge(bt_ready, 4)
                for d in range(2):
                    pe.wait_ge(rot_done, 2 * pair + d + 1)
                    for i in range(2):
                        last = pe.matmul(psum[r, 6 + t % 2, 0:T], fmat[:, d, i, pair, :], xs[:, i],
                                         start=(d == 0 and i == 0), stop=(d == 1 and i == 1))
                    last.then_inc(y_mm, 1)

            pe.wait_ge(bt_ready, 4)
            pe.wait_ge(f_ready, 4 * NT)
            pe.wait_ge(tiles_out, 8)
            s5_in(0)
            for j in range(J_Q, J_GLU):
                pairs = S5_PAIRS[j]

                def between(s, pairs=pairs):
                    if s < len(pairs):
                        s5_in(pairs[s] + 1)
                        s5_out(pairs[s])

                block_mm(0, j, 0, act, nothing, token_major=(j >= J_V), between=between)

            def heads(base, count, q, k, vv, ss, pt):
                def scores(h):
                    if h >= 2:
                        pe.wait_ge(sc_sum, base + h - 1)
                    for qt in range(2):
                        last = pe.matmul(psum[:, 4 + h % 2, qt * T:(qt + 1) * T], q[:, h, qt * P:(qt + 1) * P],
                                         k[:, h, :], start=True, stop=True)
                    last.then_inc(sc_mm, 1)

                scores(0)
                for h in range(count):
                    if h + 1 < count:
                        scores(h + 1)
                    pe.wait_ge(prob_done, 2 * (base + h) + 2)
                    if h >= 1:
                        pe.wait_ge(pt_done, base + h)
                    for kt in range(2):
                        for qt in range(2):
                            last = pe.transpose(psum[:, 6, kt * T + qt * P:kt * T + (qt + 1) * P],
                                                ss[:, h % 2, qt, kt * P:(kt + 1) * P], ident[:])
                    last.then_inc(pt_tr, 1)
                    pe.wait_ge(pt_done, base + h + 1)
                    if h >= 1:
                        pe.wait_ge(o_ready, base + h)
                    for kt in range(2):
                        last = pe.matmul(psum[:, 7, 0:T], vv[:, kt, h * HD:(h + 1) * HD], pt[:, kt, :],
                                         start=(kt == 0), stop=(kt == 1))
                    last.then_inc(pv_mm, 1)

            pe.wait_ge(tiles_out, tile0(J_GLU))
            pe.wait_ge(y_done, NT)
            heads(0, HA, q_a, k_a, v_a, ss_a, pt_a)
            for jb in range(2):
                for s in range(4):
                    g = s // 2
                    if s % 2 == 0:
                        pe.wait_ge(tiles_out, tile0(J_GLU + jb) + 2 * g - 2)
                    pe.wait_ge(lo_done, 4 * (J_GLU + jb) + s + 1)
                    for k in range(SUBK):
                        kt = SUBK * (s % 2) + k
                        pe.wait_ge(y_split, kt + 1)
                        for n in range(2):
                            cols = slice(n * P, (n + 1) * P)
                            bank = psum[:, 2 * g + n]
                            pe.matmul(bank, whl[:, s, k, 0, cols], act[:, NT + kt].rearrange("p h t -> p (h t)"),
                                      start=(kt == 0), stop=False, skip_group_check=True)
                            last = pe.matmul(bank[:, 0:T], whl[:, s, k, 1, cols], act[:, NT + kt, 0, :],
                                             start=False, stop=(kt == NT - 1), skip_group_check=True)
                    last.then_inc(subs_used, 1)

            def merged(kt):
                if kt < HA:
                    pe.wait_ge(o_ready, kt + 1)
                else:
                    pe.wait_ge(ob_ready, kt - HA + 1)

            loop_blocks(J_OUT0, 8, act, merged)

            def mlp(j0, n, h0):
                norm(n)
                for qu in range(4):
                    loop_blocks(j0 + 16 * qu, 8, act, by_count(act_ready, KT * n))
                    loop_blocks(j0 + 16 * qu + 8, 8, hid, by_count(hid_ready, h0 + 16 * qu, 4))

            mlp(J_MLP0, 1, 0)
            norm(2)
            loop_blocks(J_QKV1, 16, act, by_count(act_ready, 2 * KT))
            loop_blocks(J_QKV1 + 16, 8, act, nothing, token_major=True)
            pe.wait_ge(tiles_out, tile0(J_OUT1))
            heads(HA, HC, q_c, k_c, v_c, ss_c, pt_c)
            loop_blocks(J_OUT1, 8, act, by_count(o_ready, HA, 4))
            mlp(J_MLP1, 3, 64)
            norm(4)
            for g in range(8):
                q4, tt_ = g // 2, g % 2
                pe.wait_ge(nrm_done, 4 * KT + 4 * q4 + 4)
                if g >= 4:
                    pe.wait_ge(fin_ev, g - 3)
                for k in range(4):
                    last = pe.transpose(psum[:, g % 4, k * P:(k + 1) * P],
                                        xfin[:, 4 * q4 + k, tt_ * P:(tt_ + 1) * P], ident[:])
                last.then_inc(fin_tr, 1)


def shape_constants():
    rel = np.arange(T)[None, :] - np.arange(T)[:, None]
    branches = ((128, 1), (512, 4), (2048, 16))
    cnt = sum(((rel % d == 0) & (np.abs(rel) <= w // 2)).astype(np.float32) for w, d in branches)
    c = np.arange(GRID_W)
    start = np.clip(c - 8, 0, GRID_W - 16)
    ok = (c[None, :] >= start[:, None]) & (c[None, :] < start[:, None] + 16)
    ok = np.tile(ok, (ROWS, ROWS))
    d = np.arange(512) - 255
    n = np.abs(d)
    nf = np.maximum(n, 1).astype(np.float32)
    big = 8 + (np.log(nf / np.float32(8)) / np.float32(np.log(1024 / 8)) * np.float32(8)).astype(np.int32)
    bucket = np.where(d > 0, 16, 0) + np.where(n < 8, n, np.minimum(big, 15))
    fold = lambda m: np.ascontiguousarray(m.astype(np.float32).reshape(2, P, T).transpose(1, 0, 2))
    return {
        "c_ident": np.eye(P, dtype=np.float32),
        "c_onehot": (np.arange(32)[:, None] == bucket[None, :]).astype(np.float32),
        "c_cnt": fold(cnt),
        "c_neg_a": fold(np.where(cnt > 0, 0.0, NEG)),
        "c_neg_c": fold(np.where(ok, 0.0, NEG)),
    }


INPUTS = ["x", "t5_bias", "ab_w_in", "ab_w_out", "s5_lam_re", "s5_lam_im", "s5_log_step", "s5_b_re", "s5_b_im",
          "s5_c_re", "s5_c_im", "s5_d", "s5_w_glu", "c_w_qkv", "c_w_out", "c_rpb", "norm_mix", "norm_mlp",
          "mlp_w1", "mlp_w2", "norm_final"]


def kernel(**inputs):
    import concourse.bacc as bacc
    from concourse.bass_utils import run_bass_kernel_spmd

    nc = bacc.Bacc("TRN2", target_bir_lowering=False, num_devices=1)
    arrays = {name: np.ascontiguousarray(inputs[name]) for name in INPUTS} | shape_constants()
    ins = {name: nc.dram_tensor(f"in_{name}", a.shape, F32, kind="ExternalInput").ap() for name, a in arrays.items()}
    out = nc.dram_tensor("out_0", (1, T, D), F32, kind="ExternalOutput").ap()
    build(nc, ins, out)
    result = run_bass_kernel_spmd(nc, [{f"in_{name}": a for name, a in arrays.items()}], core_ids=[0])
    return result.results[0]["out_0"]
```

```python
from contextlib import ExitStack

import numpy as np

import concourse.bass as bass
from concourse import mybir

F32 = mybir.dt.float32
F32R = mybir.dt.float32r
ALU = mybir.AluOpType
ACT = mybir.ActivationFunctionType
AX_X = mybir.AxisListType.X

P = 128
D = 2048
T = 256
KT = D // P
HD = 128
HA = 8
HC = 16
FF = 4 * D
QUARTER = FF // 4
CH = 16
NST = 64
NG = 64
NPAIR = NG // 2
PT = 4
NT = NPAIR // PT
GRID_W = 64
ROWS = T // GRID_W
RPB_ROWS, RPB_COLS = 15, 31
RPB_PAD = 127
EPS = 1e-6
NEG = -1e30
SCALE = 1.0 / float(np.sqrt(HD))
BLK = 256
SUBK = 4
RAWK = 8
TB = 16
MAGIC = 12582912.0
TWO_PI = 2.0 * np.pi
C1 = 6.28125
C2 = float(np.round((TWO_PI - C1) * 2.0**20) / 2.0**20)
C3 = float(np.float32(TWO_PI - C1 - C2))
GELU_A = 0.044715
GELU_B = float(np.sqrt(2.0 / np.pi))

J_U = 0
J_Q, J_K, J_V = 4, 8, 12
J_GLU = 16
J_OUT0 = J_GLU + 2
J_MLP0 = J_OUT0 + 8
J_QKV1 = J_MLP0 + 64
J_OUT1 = J_QKV1 + 24
J_MLP1 = J_OUT1 + 8
J_END = J_MLP1 + 64


def gelu_tile(q):
    t = (q - 5) // PT
    return t if q >= 5 and (q - 5) % PT == 0 and t < NT else None


def tile0(j):
    return 2 * j + 2 * min(max(j - J_GLU, 0), 2)


X_BEFORE = [0, 16, 80, 96, 160]


S5_SLOTS = {}
_next = 0
for _j in range(J_Q, J_GLU):
    _n = 3 if _j < J_Q + (NPAIR + 2) - 2 * (J_GLU - J_Q) else 2
    S5_SLOTS[_j] = list(range(_next, _next + _n))
    _next += _n
SMALL_STEPS = 42


def at_head(o, h, part):
    return o[:, h, part, :] if isinstance(h, int) else o[:, bass.ds(h, 1), part, :].rearrange("p o t -> p (o t)")


def build(nc, ins, out):
    ctx = ExitStack()
    KB = 1024
    arena = (nc.sbuf_base + 31) // 32 * 32

    def at(name, shape, off, dt=F32):
        return nc.alloc_sbuf_tensor_at(name, shape, dt, offset=arena + int(off))

    with ctx:
        def sem(name):
            return ctx.enter_context(nc.semaphore(name))

        raw = at("raw", [P, 4, RAWK, BLK], 0)
        whl = at("whl", [P, 4, SUBK, 2, BLK], 32 * KB, F32R)
        x = at("x", [P, KT, T], 64 * KB)
        act = at("act", [P, KT, 2, T], 80 * KB, F32R)
        half = at("half", [P, 2, T], 112 * KB)
        ysum = at("ysum", [P, 2, T], 114 * KB)
        ident = at("ident", [P, P], 116 * KB)
        ones = at("ones", [P, P], 116.5 * KB)
        gcol = at("gcol", [P, 88], 117 * KB)
        small = at("small", [P, 64], 117.5 * KB)
        eps_c = small[:, 0:1]
        lstep = small[:, 1:2]
        stat = small[:, 8:32].rearrange("p (a k q) -> p a k q", a=2, k=6)
        U0 = 118 * KB
        qk_a = at("qk_a", [P, 2, HA, T], U0)
        v_a = at("v_a", [P, 2, HA * HD], U0 + 16 * KB)
        u = at("u", [P, NT, T], U0 + 24 * KB)
        bt = at("bt", [P, NT, 2, P], U0 + 32 * KB)
        fmat = at("fmat", [P, 2, 2, NPAIR, 2 * CH], U0 + 40 * KB)
        tab0 = at("tab0", [P, 2, 2, NPAIR, TB], U0 + 56 * KB)
        tab1 = at("tab1", [P, 2, 2, NPAIR, T // 2 // TB], U0 + 64 * KB)
        par = at("par", [P, 3, 2, NPAIR], U0 + 68 * KB)
        tcs = at("tcs", [P, 4, 2, T], U0 + 68.75 * KB)
        pm = at("pm", [P, 4, 2, T], U0 + 76.75 * KB)
        p2 = at("p2", [P, 2, 2, T], U0 + 84.75 * KB)
        turned = at("turned", [P, 2, T // 2], U0 + 88.75 * KB)
        ss_a = at("ss_a", [P, 2, 2, T], U0 + 32 * KB)
        bias_a = at("bias_a", [P, 2, 2, T], U0 + 36 * KB)
        cnt_a = at("cnt_a", [P, 2, T], U0 + 40 * KB)
        neg_a = at("neg_a", [P, 2, T], U0 + 42 * KB)
        pt_a = at("pt_a", [P, 2, 2, 2, T], U0 + 44 * KB, F32R)
        qk_s = at("qk_s", [P, 3, 2, 2, T], U0 + 52 * KB, F32R)
        v_s = at("v_s", [P, 3, 2, T], U0 + 64 * KB, F32R)
        cnat = at("cnat", [P, 2, 2, NT, 2, NST], U0)
        rows = at("rows", [P, 16, 2 * NST], U0 + 16 * KB)
        t5sb = at("t5sb", [HA, 512], U0 + 24 * KB)
        t5tab = at("t5tab", [32, HA], U0 + 26 * KB)
        onehot = at("onehot", [32, 512], U0 + 27 * KB)
        grow = at("grow", [88, P], U0 + 29 * KB)
        xin = at("xin", [P, 2, D], U0 + 40 * KB)
        bnat = at("bnat", [P, 2, NPAIR, 2 * CH], U0 + 56 * KB)
        zt = at("zt", [P, 2, 3, NPAIR, 2], U0 + 72.75 * KB)
        ctmp = at("ctmp", [P, 2, 2, P], U0 + 74.25 * KB)
        rpbw = at("rpbw", [HC, 7, RPB_PAD], U0 + 76.75 * KB)
        nrm = at("nrm", [P, 4, T], U0 + 80.75 * KB)
        ssum = at("ssum", [P, T], U0 + 84.75 * KB)
        rstd = at("rstd", [P, T], U0 + 85.75 * KB)
        sq = at("sq", [P, T], U0 + 86.75 * KB)
        hid = at("hid", [P, KT, 2, T], U0, F32R)
        hsq = at("hsq", [P, 2, T], U0 + 32 * KB)
        qk_c = at("qk_c", [P, 2, 2, 2, 2, T], U0, F32R)
        v_c = at("v_c", [P, 2, 2, 2, 2 * HD], U0 + 16 * KB, F32R)
        o_c = at("o_c", [P, HC, 2, T], U0 + 24 * KB, F32R)
        pt_c = at("pt_c", [P, 2, 2, 2, T], U0 + 56 * KB, F32R)
        ss_c = at("ss_c", [P, 2, 2, T], U0 + 64 * KB)
        bias_c = at("bias_c", [P, 2, 2, T], U0 + 68 * KB)
        neg_c = at("neg_c", [P, 2, T], U0 + 72 * KB)
        xfin = at("xfin", [P, KT, T], U0)
        outs = at("outs", [P, 8, 512], U0 + 16 * KB)

        psum = ctx.enter_context(nc.psum_tensor("psum", [P, 8, 512], F32))

        t5_dram = nc.dram_tensor("t5_rel", [P, HA, 512], F32).ap()
        rpb_dram = nc.dram_tensor("rpb_pad", [GRID_W, HC, 7 * RPB_PAD], F32).ap()

        raw_in = [sem(f"raw_in{s}") for s in range(4)]
        x_in = sem("x_in")
        small_in = sem("small_in")
        rows_in = sem("rows_in")
        b_in, c_in = sem("b_in"), sem("c_in")
        b_zero = sem("b_zero")
        ones_set = sem("ones_set")
        rpb_zero, rpb_in, rpb_out = sem("rpb_zero"), sem("rpb_in"), sem("rpb_out")
        t5_out = sem("t5_out")
        hi_done = sem("hi_done")
        lo_done = sem("lo_done")
        subs_used = sem("subs_used")
        half_done = sem("half_done")
        tiles_out = sem("tiles_out")
        x_tr = sem("x_tr")
        x_ready = sem("x_ready")
        g_tr, g_ready = sem("g_tr"), sem("g_ready")
        t5_mm, t5_ev = sem("t5_mm"), sem("t5_ev")
        sq_done, ssum_done = sem("sq_done"), sem("ssum_done")
        norm_mm, norm_std, norm_rstd = sem("norm_mm"), sem("norm_std"), sem("norm_rstd")
        nrm_done = sem("nrm_done")
        act_hi, act_ready = sem("act_hi"), sem("act_ready")
        resid_sum = sem("resid_sum")
        relu_sum, relu_sq, hid_hi, hid_ready = sem("relu_sum"), sem("relu_sq"), sem("hid_hi"), sem("hid_ready")
        step_v = sem("step_v")
        step_a = sem("step_a")
        par_tr, par_ready = sem("par_tr"), sem("par_ready")
        b_tr, bt_ready = sem("b_tr"), sem("bt_ready")
        c_tr, c_mul, f_ready = sem("c_tr"), sem("c_mul"), sem("f_ready")
        pool_step = sem("pool_step")
        bu_done, bu_copied = sem("bu_done"), sem("bu_copied")
        tab_low, tab_turned = sem("tab_low"), sem("tab_turned")
        tcs_done, pm_done = sem("tcs_done"), sem("pm_done")
        sin_in, frame_in, scanned, frame_out = sem("sin_in"), sem("frame_in"), sem("scanned"), sem("frame_out")
        rot_done, y_mm, y_done = sem("rot_done"), sem("y_mm"), sem("y_done")
        gelu_square, gelu_in, gelu_tanh, gelu_out = sem("gelu_square"), sem("gelu_in"), sem("gelu_tanh"), sem("gelu_out")
        y_hi, y_split = sem("y_hi"), sem("y_split")
        glu_sum, glu_tanh, glu_out = sem("glu_sum"), sem("glu_tanh"), sem("glu_out")
        ob_hi, ob_ready = sem("ob_hi"), sem("ob_ready")
        mask_in = sem("mask_in")
        bias_in = [sem("bias_in0"), sem("bias_in1")]
        bias_masked = sem("bias_masked")
        qkv_hi, qkv_ready = sem("qkv_hi"), sem("qkv_ready")
        sc_mm, sc_sum, sc_max = sem("sc_mm"), sem("sc_sum"), sem("sc_max")
        exp_done, cnt_done, inv_done, prob_done = sem("exp_done"), sem("cnt_done"), sem("inv_done"), sem("prob_done")
        head_hi, head_split = sem("head_hi"), sem("head_split")
        pt_tr, pt_hi, pt_ready, pv_mm, o_hi, o_ready = sem("pt_tr"), sem("pt_hi"), sem("pt_ready"), sem("pv_mm"), sem("o_hi"), sem("o_ready")
        fin_tr, fin_ev = sem("fin_tr"), sem("fin_ev")
        out_done = sem("out_done")

        block = ctx.enter_context(nc.Block())

        w_in, w_glu, w_out0 = ins["ab_w_in"][0], ins["s5_w_glu"][0], ins["ab_w_out"][0]
        w_qkv, w_out1 = ins["c_w_qkv"][0], ins["c_w_out"][0]
        AW = HA * HD
        STREAM = [
            (J_U, 4, w_in[:, 3 * AW:4 * AW]),
            (J_Q, 12, w_in[:, 0:3 * AW]),
            (J_GLU, 2, w_glu),
            (J_OUT0, 8, w_out0),
        ]

        def mlp_stream(layer, j0):
            w1, w2 = ins["mlp_w1"][layer], ins["mlp_w2"][layer]
            for qu in range(4):
                cols = slice(QUARTER * qu, QUARTER * (qu + 1))
                yield (j0 + 16 * qu, 8, w1[:, cols])
                yield (j0 + 16 * qu + 8, 8, w2[cols, :])

        STREAM += list(mlp_stream(0, J_MLP0))
        STREAM += [(J_QKV1, 24, w_qkv), (J_OUT1, 8, w_out1)]
        STREAM += list(mlp_stream(1, J_MLP1))

        @block.sync
        def _(sp):
            def load_bias_c(h, b):
                for r in range(ROWS):
                    skew = bass.AP(tensor=rpb_dram.tensor, offset=(3 - r) * RPB_PAD + GRID_W - 1,
                                   ap=[[7 * RPB_PAD, HC], [HC * 7 * RPB_PAD - 1, GRID_W], [RPB_PAD, ROWS], [1, GRID_W]])
                    src = skew[bass.ds(h, 1)].rearrange("o p r c -> (o p) r c")
                    dst = bias_c[GRID_W * (r % 2):GRID_W * (r % 2 + 1), b, r // 2, :]
                    sp.dma_start(dst.rearrange("p (r c) -> p r c", r=ROWS), src).then_inc(bias_in[b], 16)

            for tt in range(2):
                sp.dma_start(xin[:, tt, :], ins["x"][0, tt * P:(tt + 1) * P, :]).then_inc(x_in, 16)
            for j0, n, w in STREAM:
                wk = w.rearrange("(k p) n -> p k n", p=P)
                if j0 == 0:
                    for r in range(2 * n):
                        if r >= 4:
                            sp.wait_ge(lo_done, 2 * r - 6)
                        src = wk[:, RAWK * (r % 2):RAWK * (r % 2 + 1), r // 2 * BLK:(r // 2 + 1) * BLK]
                        sp.dma_start(raw[:, r % 4], src).then_inc(raw_in[r % 4], 16)
                    continue
                if j0 == J_QKV1:
                    sp.wait_ge(rpb_out, 16)
                if j0 == J_QKV1:
                    with sp.Fori(0, n // 6) as i:
                        for p in range(12):
                            block, piece = p // 2, p % 4
                            if p % 6 == 4:
                                sp.wait_ge(sc_sum, i * 4 + (HA + p // 6 * 2))
                                for b in range(2):
                                    load_bias_c(i * 4 + (p // 6 * 2 + b), b)
                            sp.wait_ge(lo_done, i * 24 + (4 * j0 + 2 * p - 6))
                            src = wk[:, RAWK * (p % 2):RAWK * (p % 2 + 1),
                                     bass.ds(i * (2 * BLK) + (block % 3 * D + block // 3 * BLK), BLK)]
                            sp.dma_start(raw[:, piece], src).then_inc(raw_in[piece], 16)
                    continue
                with sp.Fori(0, n // 2) as i:
                    for piece in range(4):
                        sp.wait_ge(lo_done, i * 8 + (4 * j0 + 2 * piece - 6))
                        if j0 == J_GLU:
                            src = wk[:, :, bass.ds(i * (4 * BLK) + piece * BLK, BLK)]
                        else:
                            src = wk[:, RAWK * (piece % 2):RAWK * (piece % 2 + 1),
                                     bass.ds(i * (2 * BLK) + piece // 2 * BLK, BLK)]
                        sp.dma_start(raw[:, piece], src).then_inc(raw_in[piece], 16)
            for g in range(8):
                sp.wait_ge(fin_ev, g + 1)
                sp.dma_start(out[0, (g % 2) * P:(g % 2 + 1) * P, (g // 2) * 512:(g // 2 + 1) * 512],
                             outs[:, g]).then_inc(out_done, 16)
            sp.wait_ge(out_done, 16 * 8)

        @block.gpsimd
        def _(pool):
            pchain = [0]

            def link(instruction):
                pchain[0] += 1
                instruction.then_inc(pool_step, 1)
                pool.wait_ge(pool_step, pchain[0])

            nc.gpsimd.memset(ones[:], 1.0).then_inc(ones_set, 1)
            nc.gpsimd.memset(eps_c, EPS).then_inc(ones_set, 1)
            nc.gpsimd.memset(bnat[:], 0.0).then_inc(b_zero, 1)
            nc.gpsimd.memset(rpbw[:], 0.0).then_inc(rpb_zero, 1)

            def norm_squares(n):
                for kt in range(KT):
                    pool.wait_ge(x_ready, X_BEFORE[n] + kt + 1)
                    if kt == 0:
                        nc.gpsimd.tensor_tensor(ssum[:], x[:, 0], x[:, 0], ALU.mult).then_inc(ssum_done, 1)
                        continue
                    pool.wait_ge(ssum_done, KT * n + kt)
                    nc.gpsimd.tensor_tensor(sq[:], x[:, kt], x[:, kt], ALU.mult).then_inc(sq_done, 1)
                    pool.wait_ge(sq_done, (KT - 1) * n + kt)
                    nc.gpsimd.tensor_tensor(ssum[:], ssum[:], sq[:], ALU.add).then_inc(ssum_done, 1)

            def norm_low(n):
                for kt in range(KT):
                    pool.wait_ge(act_hi, KT * n + kt + 1)
                    nc.gpsimd.tensor_tensor(act[:, kt, 1, :], nrm[:, kt % 4, :], act[:, kt, 0, :].bitcast(F32),
                                            ALU.subtract).then_inc(act_ready, 1)

            norm_squares(0)
            norm_low(0)

            pool.wait_ge(par_ready, 2)
            pool.wait_ge(bt_ready, 4)

            def rot(t, i):
                return t[:, i].rearrange("p d g b -> p (d g) b")

            def angle_add(t, dst, a, b, n, into=None):
                ca, sa = rot(t, 0)[:, :, a:a + n], rot(t, 1)[:, :, a:a + n]
                cb = rot(t, 0)[:, :, b:b + 1].to_broadcast([P, 2 * NPAIR, n])
                sb_ = rot(t, 1)[:, :, b:b + 1].to_broadcast([P, 2 * NPAIR, n])
                tmp = p2[:].rearrange("p s a t -> p (s a t)")[:, 0:2 * NPAIR * n].rearrange("p (g b) -> p g b", b=n)
                co, so = into or (rot(t, 0)[:, :, dst:dst + n], rot(t, 1)[:, :, dst:dst + n])
                link(nc.gpsimd.tensor_tensor(co, ca, cb, ALU.mult))
                link(nc.gpsimd.tensor_tensor(tmp, sa, sb_, ALU.mult))
                link(nc.gpsimd.tensor_tensor(co, co, tmp, ALU.subtract))
                link(nc.gpsimd.tensor_tensor(so, sa, cb, ALU.mult))
                link(nc.gpsimd.tensor_tensor(tmp, ca, sb_, ALU.mult))
                link(nc.gpsimd.tensor_tensor(so, so, tmp, ALU.add))

            for t in (tab0, tab1):
                nc.gpsimd.memset(t[:, 0, :, :, 0], 1.0)
                link(nc.gpsimd.memset(t[:, 1, :, :, 0], 0.0))
            link(nc.gpsimd.tensor_copy(tab0[:, :, :, :, 1], par[:, 1:3]))
            for n in (1, 2, 4):
                angle_add(tab0, n + 1, 1, n, n)
            angle_add(tab0, 9, 1, 8, 7)
            c8, s8 = rot(tab0, 0)[:, :, 8:9], rot(tab0, 1)[:, :, 8:9]
            c16, s16 = rot(tab1, 0)[:, :, 1:2], rot(tab1, 1)[:, :, 1:2]
            tmp = p2[:].rearrange("p s a t -> p (s a t)")[:, 0:2 * NPAIR].rearrange("p (g b) -> p g b", b=1)
            link(nc.gpsimd.tensor_tensor(c16, c8, c8, ALU.mult))
            link(nc.gpsimd.tensor_tensor(tmp, s8, s8, ALU.mult))
            link(nc.gpsimd.tensor_tensor(c16, c16, tmp, ALU.subtract))
            link(nc.gpsimd.tensor_tensor(s16, s8, c8, ALU.mult))
            link(nc.gpsimd.tensor_tensor(s16, s16, s16, ALU.add))
            for n, count in ((1, 1), (2, 2), (4, 3)):
                angle_add(tab1, n + 1, 1, n, count)
            angle_add(tab1, None, 4, 4, 1, into=[par[:, 1 + k].rearrange("p d g -> p (d g)").unsqueeze(2) for k in range(2)])

            pool.wait_ge(rpb_out, 16)
            pool.wait_ge(f_ready, 4 * NT)
            HT = T // 2

            def table_low(m):
                if m >= 2 * NPAIR:
                    return
                pair, d = m // 2, m % 2
                if m >= 4:
                    pool.wait_ge(frame_out, 2 * (m - 3))
                co, so = tcs[:, m % 4, 0], tcs[:, m % 4, 1]

                def outer(i0, i1, dst):
                    a = tab1[:, i1, d, pair, :].unsqueeze(2).to_broadcast([P, HT // TB, TB])
                    b = tab0[:, i0, d, pair, :].unsqueeze(1).to_broadcast([P, HT // TB, TB])
                    return nc.gpsimd.tensor_tensor(dst.rearrange("p (a b) -> p a b", b=TB), a, b, ALU.mult)

                outer(0, 0, co[:, 0:HT])
                outer(1, 1, so[:, HT:T])
                outer(0, 1, so[:, 0:HT])
                link(outer(1, 0, co[:, HT:T]))
                nc.gpsimd.tensor_tensor(co[:, 0:HT], co[:, 0:HT], so[:, HT:T], ALU.subtract).then_inc(tab_low, 1)
                nc.gpsimd.tensor_tensor(so[:, 0:HT], so[:, 0:HT], co[:, HT:T], ALU.add).then_inc(tab_low, 1)

            table_low(0)
            for m in range(2 * NPAIR):
                table_low(m + 1)
                co, so = tcs[:, m % 4, 0], tcs[:, m % 4, 1]
                pool.wait_ge(tab_turned, 4 * (m + 1))
                nc.gpsimd.tensor_tensor(co[:, HT:T], co[:, HT:T], turned[:, 0], ALU.subtract).then_inc(tcs_done, 1)
                nc.gpsimd.tensor_tensor(so[:, HT:T], so[:, HT:T], turned[:, 1], ALU.add).then_inc(tcs_done, 1)
                pool.wait_ge(tcs_done, 2 * (m + 1))
                pool.wait_ge(bu_copied, m // 2 * 2 + 2)
                nc.gpsimd.tensor_tensor(pm[:, m % 4], pm[:, m % 4],
                                        co.unsqueeze(1).to_broadcast([P, 2, T]), ALU.mult).then_inc(pm_done, 1)

            pool.wait_ge(mask_in, 32)
            for h in range(HA):
                pool.wait_ge(bias_in[h % 2], 32 * (h // 2 + 1))
                nc.gpsimd.tensor_tensor(bias_a[:, h % 2], bias_a[:, h % 2], neg_a[:], ALU.add).then_inc(bias_masked, 1)
            norm_squares(1)
            norm_low(1)
            norm_squares(2)
            norm_low(2)
            pool.wait_ge(mask_in, 48)
            for h in range(HC):
                pool.wait_ge(bias_in[h % 2], 32 * HA // 2 + 64 * (h // 2 + 1))
                nc.gpsimd.tensor_tensor(bias_c[:, h % 2], bias_c[:, h % 2], neg_c[:], ALU.add).then_inc(bias_masked, 1)
            norm_squares(3)
            norm_low(3)
            norm_squares(4)

        @block.scalar
        def _(a):
            a.dma_start(ident[:], ins["c_ident"]).then_inc(small_in, 16)
            a.dma_start(onehot[:], ins["c_onehot"]).then_inc(small_in, 16)
            a.dma_start(t5tab[:], ins["t5_bias"]).then_inc(small_in, 16)
            a.dma_start(grow[0:32, :], ins["norm_mix"].rearrange("l (k p) -> (l k) p", p=P)).then_inc(small_in, 16)
            a.dma_start(grow[32:64, :], ins["norm_mlp"].rearrange("l (k p) -> (l k) p", p=P)).then_inc(small_in, 16)
            a.dma_start(grow[64:80, :], ins["norm_final"].rearrange("(k p) -> k p", p=P)).then_inc(small_in, 16)
            a.dma_start(grow[80:88, :], ins["s5_d"][0].rearrange("(k p) -> k p", p=P)).then_inc(small_in, 16)
            for twice in range(2):
                cols = slice(NST * twice, NST * (twice + 1))
                a.dma_start(rows[:, 0, cols], ins["s5_lam_re"][0].rearrange("d g s -> (d g) s")).then_inc(rows_in, 16)
                a.dma_start(rows[:, 1, cols], ins["s5_lam_im"][0].rearrange("d g s -> (d g) s")).then_inc(rows_in, 16)
            a.dma_start(lstep, ins["s5_log_step"].rearrange("a d (g o) -> (a d g) o", o=1)).then_inc(rows_in, 16)
            a.wait_ge(b_zero, 1)
            for i, name in enumerate(("s5_b_re", "s5_b_im")):
                src = ins[name][0].rearrange("(r g) s c -> g s r c", g=2)
                for g in range(2):
                    a.dma_start(bnat[g * NST:(g + 1) * NST, i, :, g * CH:(g + 1) * CH], src[g]).then_inc(b_in, 16)
            a.wait_ge(rpb_zero, 1)
            a.dma_start(rpbw[:, :, 48:48 + RPB_COLS], ins["c_rpb"][0, :, 4:11, :]).then_inc(rpb_in, 16)
            for d in range(2):
                for i, name in enumerate(("s5_c_re", "s5_c_im")):
                    src = ins[name][0, d].rearrange("(t g) c s -> (g c) t s", g=8)
                    for twice in range(2):
                        a.dma_start(cnat[:, d, i, :, twice, :], src).then_inc(c_in, 16)
            a.wait_ge(rpb_in, 16)
            a.dma_start(rpb_dram.rearrange("r h n -> h r n"), rpbw[:].rearrange("h r n -> h (r n)").unsqueeze(1)
                        .to_broadcast([HC, GRID_W, 7 * RPB_PAD])).then_inc(rpb_out, 16)


            def raw_uses(i, j0, jb):
                return i * 16 + 16 * ((j0 + jb) // 2 + 1)

            def high(i, j0, jb, s):
                jp = (j0 + jb) % 2
                piece = 2 * jp + s // 2
                if s % 2 == 0:
                    a.wait_ge(raw_in[piece], raw_uses(i, j0, jb))
                if not (isinstance(i, int) and j0 + 2 * i + jb == 0):
                    a.wait_ge(subs_used, i * 8 + (4 * (j0 + jb) + s - 3))
                nc.scalar.activation(whl[:, s, :, 0, :], raw[:, piece, SUBK * (s % 2):SUBK * (s % 2 + 1), :],
                                     ACT.Copy).then_inc(hi_done, 1)

            def take_halves(i, j0, jb, glu_group=None):
                banks = 2 * ((j0 + jb) % 2 if glu_group is None else glu_group)
                done = 4 * (j0 + jb) + (4 if glu_group is None else 2 * glu_group + 2)
                t = tile0(j0 + jb) + (0 if glu_group is None else 2 * glu_group)
                a.wait_ge(subs_used, i * 8 + done)
                for n in range(2):
                    if t + n >= 2:
                        a.wait_ge(tiles_out, i * 4 + (t + n - 1))
                    nc.scalar.activation(half[:, n], psum[:, banks + n, T:2 * T], ACT.Copy).then_inc(half_done, 1)

            def block_step(i, j0, jb, last=False):
                high(i, j0, jb, 3)
                if not last:
                    for s in range(3):
                        high(i, j0, jb + 1, s)
                take_halves(i, j0, jb)

            def norm(n, base):
                a.wait_ge(norm_mm, n + 1)
                nc.scalar.activation(rstd[:], psum[:, 7, 0:T], ACT.Sqrt, bias=eps_c, scale=1.0 / D).then_inc(norm_std, 1)
                if n == 4:
                    return
                for kt in range(KT):
                    a.wait_ge(nrm_done, KT * n + kt + 1)
                    nc.scalar.activation(act[:, kt, 0, :], nrm[:, kt % 4, :], ACT.Copy).then_inc(act_hi, 1)

            def loop_blocks(j0, n, first=False, last=False):
                with a.Fori(1 if first else 0, n // 2 - (1 if last else 0)) as i:
                    block_step(i, j0, 0)
                    block_step(i, j0, 1)
                if last:
                    block_step(n // 2 - 1, j0, 0)
                    block_step(n // 2 - 1, j0, 1, last=True)

            a.wait_ge(rows_in, 16 * 5)
            nc.scalar.activation(lstep, lstep, ACT.Exp).then_inc(step_a, 1)
            a.wait_ge(step_v, 1)
            a.wait_ge(step_a, 1)
            nc.scalar.activation(rows[:, 3], rows[:, 0], ACT.Exp, scale=lstep).then_inc(step_a, 1)
            a.wait_ge(t5_mm, 1)
            nc.scalar.activation(t5sb[:], psum[0:HA, 1, :], ACT.Copy).then_inc(t5_ev, 1)
            a.wait_ge(t5_ev, 1)
            a.dma_start(t5_dram.rearrange("r h n -> h r n"),
                        t5sb[:].unsqueeze(1).to_broadcast([HA, P, 512])).then_inc(t5_out, 16)
            for s in range(3):
                high(0, 0, 0, s)
            a.wait_ge(ones_set, 2)
            norm(0, 0)
            block_step(0, 0, 0)
            for g in range(4):
                a.wait_ge(b_tr, g + 1)
                nc.scalar.activation(bt[:, 2 * g:2 * g + 2].rearrange("p t i s -> p (t i s)"), psum[:, 6 + g % 2, :],
                                     ACT.Copy).then_inc(bt_ready, 1)
            for j in range(1, 4):
                block_step(0, j, 0)

            def take_bu(pair):
                if pair >= NPAIR:
                    return
                a.wait_ge(bu_done, pair + 1)
                for m in (2 * pair, 2 * pair + 1):
                    if m >= 4:
                        a.wait_ge(y_mm, m - 3)
                    nc.scalar.activation(pm[:, m % 4].rearrange("p i t -> p (i t)"), psum[:, 4 + pair % 2, :],
                                         ACT.Copy).then_inc(bu_copied, 1)

            def table_turn(m):
                if m >= 2 * NPAIR:
                    return
                pair, d = m // 2, m % 2
                a.wait_ge(tab_low, 2 * (m + 1))
                if m >= 1:
                    a.wait_ge(tcs_done, 2 * m)
                c128, s128 = par[:, 1, d, pair:pair + 1], par[:, 2, d, pair:pair + 1]
                co, so = [tcs[:, m % 4, k, 0:T // 2] for k in range(2)]
                for dst, src, by in ((tcs[:, m % 4, 0, T // 2:T], co, c128), (turned[:, 0], so, s128),
                                     (tcs[:, m % 4, 1, T // 2:T], so, c128), (turned[:, 1], co, s128)):
                    nc.scalar.activation(dst, src, ACT.Copy, scale=by).then_inc(tab_turned, 1)

            a.wait_ge(rpb_out, 16)
            take_bu(0)
            table_turn(0)
            for j in range(J_Q, J_GLU):
                slots = S5_SLOTS[j]
                high(0, j, 0, 3)
                if j > J_Q:
                    take_halves(0, j - 1, 0)
                for k in range(3):
                    if k < len(slots):
                        table_turn(2 * slots[k] + 1)
                        t = gelu_tile(slots[k])
                        if t is not None:
                            a.wait_ge(gelu_in, t + 1)
                            inner = psum[:, 6 + t % 2, T:2 * T]
                            nc.scalar.activation(inner, inner, ACT.Tanh, scale=GELU_A * GELU_B).then_inc(gelu_tanh, 1)
                    high(0, j, 1, k)
                    if k < len(slots):
                        take_bu(slots[k] + 1)
                        table_turn(2 * slots[k] + 2)
            take_halves(0, J_GLU - 1, 0)
            a.wait_ge(y_done, NT)
            a.dma_start(cnt_a[:], ins["c_cnt"]).then_inc(mask_in, 16)
            a.dma_start(neg_a[:], ins["c_neg_a"]).then_inc(mask_in, 16)
            a.wait_ge(t5_out, 16)
            a.wait_ge(rpb_out, 16)

            def load_bias_a(h):
                for qt in range(2):
                    skew = bass.AP(tensor=t5_dram.tensor, offset=h * 512 + 255 - P * qt, ap=[[HA * 512 - 1, P], [1, T]])
                    a.dma_start(bias_a[:, h % 2, qt, :], skew).then_inc(bias_in[h % 2], 16)

            def exps(hh, b, ss, sums):
                a.wait_ge(sc_max, hh + 1)
                for qt in range(2):
                    extra = {"accum_out": stat[:, b, 1, qt:qt + 1]} if sums else {}
                    nc.scalar.activation(ss[:, b, qt], ss[:, b, qt], ACT.Exp,
                                         bias=stat[:, b, 0, qt:qt + 1], **extra).then_inc(exp_done, 1)

            def probs_high(hh, b, pt):
                a.wait_ge(pt_tr, hh + 1)
                if not (isinstance(hh, int) and hh < 2):
                    a.wait_ge(pv_mm, hh - 1)
                nc.scalar.activation(pt[:, b, :, 0, :], psum[:, 6 + b].rearrange("p (k t) -> p k t", k=2),
                                     ACT.Copy).then_inc(pt_hi, 1)

            def out_high(hh, b, dst):
                a.wait_ge(pv_mm, hh + 1)
                nc.scalar.activation(dst, psum[:, 6 + b, 0:T], ACT.Copy).then_inc(o_hi, 1)

            def head_high(h):
                if h >= 3:
                    a.wait_ge(pv_mm, h - 2)
                nc.scalar.activation(qk_s[:, h % 3, :, 0], qk_a[:, :, h], ACT.Copy).then_inc(head_hi, 1)
                nc.scalar.activation(v_s[:, h % 3, 0].rearrange("p (k d) -> p k d", k=2),
                                     v_a[:, :, h * HD:(h + 1) * HD], ACT.Copy).then_inc(head_hi, 1)

            load_bias_a(0)
            load_bias_a(1)
            head_high(0)
            for t in range(NT):
                a.wait_ge(gelu_out, t + 1)
                nc.scalar.activation(act[:, NT + t, 0, :], u[:, t], ACT.Copy, scale=0.5).then_inc(y_hi, 1)
            exps(0, 0, ss_a, False)
            head_high(1)

            def head_step(g):
                if g < HA:
                    probs_high(g, g % 2, pt_a)
                if g + 1 < HA:
                    exps(g + 1, (g + 1) % 2, ss_a, False)
                if 1 <= g <= HA:
                    out_high(g - 1, (g - 1) % 2, act[:, g - 1, 0, :])
                if g + 2 < HA:
                    a.wait_ge(sc_sum, g + 1)
                    load_bias_a(g + 2)
                    head_high(g + 2)

            def glu_half(jb, g):
                take_halves(0, J_GLU + jb, 0, glu_group=g)
                for n in range(2):
                    f = 4 * jb + 2 * g + n
                    a.wait_ge(tiles_out, tile0(J_GLU + jb) + 2 * g + n + 1)
                    nc.scalar.activation(ysum[:, n], ysum[:, n], ACT.Tanh, scale=0.5).then_inc(glu_tanh, 1)

            high(0, J_GLU, 0, 3)
            for g in range(8):
                if g < 7:
                    high(0, J_GLU + 1 + g // 4, 0, g % 4)
                head_step(g)
                if g % 2:
                    glu_half(g // 4, g // 2 % 2)
            head_step(8)
            for f in range(NT):
                a.wait_ge(glu_out, f + 1)
                nc.scalar.activation(act[:, NT + f, 0, :], u[:, f], ACT.Copy, scale=0.25).then_inc(ob_hi, 1)
            loop_blocks(J_OUT0, 8)
            norm(1, 0)
            for k in range(8):
                loop_blocks(J_MLP0 + 8 * k, 8)
            norm(2, 0)
            a.dma_start(neg_c[:], ins["c_neg_c"]).then_inc(mask_in, 16)

            def outs_high_c(turn, pair):
                for b in range(2):
                    h = turn * 4 + (2 * pair + b)
                    out_high(h + HA, b, at_head(o_c, h, 0))

            def qkv_blocks(turn, first=False):
                t3 = turn * 3
                for jb in range(6):
                    pair, kind = jb // 3, jb % 3
                    high(t3, J_QKV1, jb, 3)
                    for k in range(3):
                        high(t3, J_QKV1, jb + 1, k)
                        if kind == 2 and k == 1:
                            for b in range(2):
                                exps(turn * 4 + (HA + 2 * pair + b), b, ss_c, True)
                        if kind == 0 and k == 0 and not (first and pair == 0):
                            for b in range(2):
                                probs_high(turn * 4 + (HA + 2 * pair - 2 + b), b, pt_c)
                        if kind == 0 and k == 2 and not (first and pair == 0):
                            outs_high_c(turn, pair - 1)
                    take_halves(t3, J_QKV1, jb)

            qkv_blocks(0, first=True)
            with a.Fori(1, 4) as turn:
                qkv_blocks(turn)
            high(0, J_OUT1, 0, 3)
            for s in range(3):
                high(0, J_OUT1, 1, s)
                if s == 0:
                    for b in range(2):
                        probs_high(HA + HC - 2 + b, b, pt_c)
                if s == 2:
                    outs_high_c(4, -1)
            take_halves(0, J_OUT1, 0)
            block_step(0, J_OUT1, 1)
            loop_blocks(J_OUT1, 8, first=True)
            norm(3, 0)
            for k in range(8):
                loop_blocks(J_MLP1 + 8 * k, 8, last=(k == 7))
            norm(4, 0)
            for g in range(8):
                a.wait_ge(fin_tr, g + 1)
                nc.scalar.activation(outs[:, g], psum[:, g % 4, :], ACT.Copy).then_inc(fin_ev, 1)

        @block.vector
        def _(v):
            vchain = [0]

            def link(instruction):
                vchain[0] += 1
                instruction.then_inc(step_v, 1)
                v.wait_ge(step_v, vchain[0])

            def ts(dst, src, c0, c1, op0=ALU.mult, op1=ALU.add):
                return nc.vector.tensor_scalar(dst, src, c0, c1, op0, op1)

            def tt(dst, s0, s1, op):
                return nc.vector.tensor_tensor(dst, s0, s1, op)

            def stt(dst, s0, c, s1, op0, op1):
                return nc.vector.scalar_tensor_tensor(out=dst, in0=s0, scalar=c, in1=s1, op0=op0, op1=op1)

            R = [rows[:, k] for k in range(16)]
            v.wait_ge(rows_in, 16 * 5)
            link(nc.vector.tensor_scalar(R[0], R[0], -1e-4, None, ALU.min))
            v.wait_ge(step_a, 1)
            link(nc.vector.tensor_scalar(R[2], R[1], lstep, None, ALU.mult))
            link(ts(R[4], R[2], 1.0 / TWO_PI, MAGIC))
            link(nc.vector.tensor_scalar(R[4], R[4], MAGIC, None, ALU.subtract))
            link(stt(R[5], R[4], -C1, R[2], ALU.mult, ALU.add))
            link(stt(R[5], R[4], -C2, R[5], ALU.mult, ALU.add))
            link(stt(R[5], R[4], -C3, R[5], ALU.mult, ALU.add))
            link(nc.vector.tensor_scalar(R[5], R[5], 0.25, None, ALU.mult))
            link(tt(R[6], R[5], R[5], ALU.mult))
            link(nc.vector.tensor_scalar(R[7], R[6], 1.0 / 362880, None, ALU.mult))
            for c in (-1.0 / 5040, 1.0 / 120, -1.0 / 6):
                link(stt(R[7], R[7], c, R[6], ALU.add, ALU.mult))
            link(stt(R[7], R[7], 1.0, R[5], ALU.add, ALU.mult))
            link(nc.vector.tensor_scalar(R[8], R[6], -1.0 / 3628800, None, ALU.mult))
            for c in (1.0 / 40320, -1.0 / 720, 1.0 / 24, -0.5):
                link(stt(R[8], R[8], c, R[6], ALU.add, ALU.mult))
            link(nc.vector.tensor_scalar(R[8], R[8], 1.0, None, ALU.add))
            for s_, c_, s2, c2 in ((7, 8, 11, 8), (11, 8, 13, 14)):
                link(stt(R[s2], R[s_], 2.0, R[c_], ALU.mult, ALU.mult))
                link(stt(R[12], R[s_], -2.0, R[s_], ALU.mult, ALU.mult))
                link(nc.vector.tensor_scalar(R[c2], R[12], 1.0, None, ALU.add))
            v.wait_ge(step_a, 2)
            link(tt(R[9], R[3], R[14], ALU.mult))
            link(nc.vector.tensor_scalar(R[9], R[9], 1.0, None, ALU.subtract))
            link(tt(R[10], R[3], R[13], ALU.mult))
            link(tt(R[12], R[0], R[0], ALU.mult))
            link(tt(R[11], R[1], R[1], ALU.mult))
            link(tt(R[12], R[12], R[11], ALU.add))
            link(nc.vector.reciprocal(R[12], R[12]))
            link(tt(R[5], R[9], R[0], ALU.mult))
            link(tt(R[6], R[10], R[1], ALU.mult))
            link(tt(R[5], R[5], R[6], ALU.add))
            link(tt(R[5], R[5], R[12], ALU.mult))
            link(tt(R[6], R[10], R[0], ALU.mult))
            link(tt(R[7], R[9], R[1], ALU.mult))
            link(tt(R[6], R[6], R[7], ALU.subtract))
            link(tt(R[6], R[6], R[12], ALU.mult))
            link(nc.vector.memset(zt[:], 0.0))
            assert vchain[0] == SMALL_STEPS, vchain[0]

            for g in range(KT // 2):
                v.wait_ge(x_tr, g + 1)
                nc.vector.tensor_copy(x[:, 2 * g:2 * g + 2].rearrange("p k t -> p (k t)"),
                                      psum[:, 4 + g % 4, :]).then_inc(x_ready, 2)
            v.wait_ge(g_tr, 1)
            nc.vector.tensor_copy(gcol[:], psum[:, 0, 0:88]).then_inc(g_ready, 1)

            def low(i, j0, jb, s):
                jp = (j0 + jb) % 2
                piece = 2 * jp + s // 2
                v.wait_ge(hi_done, i * 8 + (4 * (j0 + jb) + s + 1))
                tt(whl[:, s, :, 1, :], raw[:, piece, SUBK * (s % 2):SUBK * (s % 2 + 1), :],
                   whl[:, s, :, 0, :].bitcast(F32), ALU.subtract).then_inc(lo_done, 1)

            def tile_sum(i, j0, jb, n, dst, glu_group=None):
                banks = 2 * ((j0 + jb) % 2 if glu_group is None else glu_group)
                t = tile0(j0 + jb) + (0 if glu_group is None else 2 * glu_group)
                v.wait_ge(half_done, i * 4 + (t + n + 1))
                tt(dst, psum[:, banks + n, 0:T], half[:, n], ALU.add).then_inc(tiles_out, 1)
                return i * 4 + (t + n + 1)

            def store(dst_of):
                def evac(i, j0, jb):
                    for n in range(2):
                        tile_sum(i, j0, jb, n, dst_of(i, j0, jb, n))
                return evac

            def residual(x0):
                def evac(i, j0, jb):
                    v.wait_ge(x_ready, i * 4 + (x0 + 2 * jb))
                    for n in range(2):
                        tile_sum(i, j0, jb, n, ysum[:, n])
                    for n in range(2):
                        v.wait_ge(tiles_out, i * 4 + (tile0(j0 + jb) + n + 1))
                        dst = x[:, bass.ds(i * 4 + (2 * jb + n), 1), :].rearrange("p o t -> p (o t)")
                        tt(dst, dst, ysum[:, n], ALU.add).then_inc(x_ready, 1)
                return evac

            def squared_relu(h0):
                def evac(i, j0, jb):
                    at_ = [i * 4 + (h0 + 2 * jb + n + 1) for n in range(2)]

                    def dst(n, part):
                        return hid[:, bass.ds(i * 4 + (2 * jb + n), 1), part, :].rearrange("p o t -> p (o t)")

                    if not (isinstance(i, int) and i * 4 + h0 + 2 * jb == 0):
                        v.wait_ge(relu_sq, i * 4 + (h0 + 2 * jb))
                        v.wait_ge(hid_ready, i * 4 + (h0 + 2 * jb))
                    for n in range(2):
                        tile_sum(i, j0, jb, n, ysum[:, n])
                    for n in range(2):
                        v.wait_ge(tiles_out, i * 4 + (tile0(j0 + jb) + n + 1))
                        stt(hsq[:, n], ysum[:, n], 0.0, ysum[:, n], ALU.max, ALU.mult).then_inc(relu_sq, 1)
                    for n in range(2):
                        v.wait_ge(relu_sq, at_[n])
                        nc.vector.tensor_copy(dst(n, 0), hsq[:, n]).then_inc(hid_hi, 1)
                    for n in range(2):
                        v.wait_ge(hid_hi, at_[n])
                        tt(dst(n, 1), hsq[:, n], dst(n, 0).bitcast(F32), ALU.subtract).then_inc(hid_ready, 1)
                return evac

            def block_step(i, j0, jb, evac, last=False):
                low(i, j0, jb, 3)
                if not last:
                    for s in range(3):
                        low(i, j0, jb + 1, s)
                evac(i, j0, jb)

            def loop_blocks(j0, n, evac, first=False, last=False):
                if first:
                    block_step(0, j0, 0, evac)
                    block_step(0, j0, 1, evac)
                with v.Fori(1 if first else 0, n // 2 - (1 if last else 0)) as i:
                    block_step(i, j0, 0, evac)
                    block_step(i, j0, 1, evac)
                if last:
                    block_step(n // 2 - 1, j0, 0, evac)
                    block_step(n // 2 - 1, j0, 1, evac, last=True)

            def norm(n, gains):
                v.wait_ge(norm_std, n + 1)
                nc.vector.reciprocal(rstd[:], rstd[:]).then_inc(norm_rstd, 1)
                v.wait_ge(norm_rstd, n + 1)
                for kt in range(KT):
                    if n == 4:
                        dst = xfin[:, kt]
                    else:
                        dst = nrm[:, kt % 4]
                        if kt >= 4:
                            v.wait_ge(act_ready, KT * n + kt - 3)
                    stt(dst, x[:, kt], gcol[:, gains + kt:gains + kt + 1], rstd[:], ALU.mult, ALU.mult) \
                        .then_inc(nrm_done, 1)

            for s in range(3):
                low(0, 0, 0, s)
            v.wait_ge(g_ready, 1)
            norm(0, 0)
            v.wait_ge(t5_out, 16)
            u_store = store(lambda i, j0, jb, n: u[:, 2 * (j0 + jb - J_U) + n])
            block_step(0, 0, 0, u_store)

            v.wait_ge(par_tr, 1)
            pv_ = psum[:, 4, :].rearrange("p (k r g) -> p k r g", k=4, g=2)
            zi_ = psum[:, 5, 0:P].rearrange("p (r g) -> p r g", g=2)
            for g in range(2):
                s_ = slice(NST * g, NST * (g + 1))
                nc.vector.tensor_copy(par[s_].rearrange("p k d r -> p k (d r)"), pv_[s_, 0:3, :, g]).then_inc(par_ready, 1)
            for g in range(2):
                s_ = slice(NST * g, NST * (g + 1))
                zr = pv_[s_, 3, :, g].rearrange("p (d r) -> p d r", d=2)
                zi = zi_[s_, :, g].rearrange("p (d r) -> p d r", d=2)
                for k, src, sign in ((0, zr, 1.0), (1, zi, -1.0), (2, zr, -1.0)):
                    nc.vector.tensor_scalar(zt[s_, :, k, :, g], src, sign, None, ALU.mult).then_inc(par_ready, 1)
            block_step(0, 1, 0, u_store)
            block_step(0, 2, 0, u_store)
            v.wait_ge(par_ready, 8)
            v.wait_ge(x_tr, 8)
            for c in range(2 * NT):
                d, t = c // NT, c % NT
                v.wait_ge(c_tr, c + 1)
                if c:
                    v.wait_ge(f_ready, 2 * c)
                src = psum[:, 4 + c % 2, 0:2 * P].rearrange("p (i r c) -> p i r c", i=2, c=CH)
                for k in range(2):
                    z = zt[:, d, k:k + 2, PT * t:PT * (t + 1), :].rearrange("p i r g -> p i (r g)")
                    tt(ctmp[:, k].rearrange("p i (r c) -> p i r c", c=CH), src,
                       z.unsqueeze(3).to_broadcast([P, 2, 2 * PT, CH]), ALU.mult).then_inc(c_mul, 1)
                for k in range(2):
                    v.wait_ge(c_mul, 2 * c + k + 1)
                    tt(fmat[:, d, k, PT * t:PT * (t + 1), :].rearrange("p r c -> p (r c)"),
                       ctmp[:, k, 0], ctmp[:, k, 1], ALU.add).then_inc(f_ready, 1)
            block_step(0, 3, 0, u_store)

            def terms(m):
                pair, d, sl = m // 2, m % 2, m % 4
                add, sub = (ALU.add, ALU.subtract) if d == 0 else (ALU.subtract, ALU.add)
                cosine, sine = [tcs[:, sl, k].unsqueeze(1).to_broadcast([P, 2, T]) for k in range(2)]
                return pair, d, sl, add, sub, cosine, sine

            def times_sine(m):
                pair, d, sl, add, sub, cosine, sine = terms(m)
                v.wait_ge(pm_done, m + 1)
                tt(p2[:, m % 2], psum[:, 4 + pair % 2].rearrange("p (i t) -> p i t", i=2)[:, ::-1], sine, ALU.mult).then_inc(sin_in, 1)

            def into_frame(m):
                pair, d, sl, add, sub, cosine, sine = terms(m)
                v.wait_ge(sin_in, m + 1)
                tt(pm[:, sl, 0], pm[:, sl, 0], p2[:, m % 2, 0], add).then_inc(frame_in, 1)
                tt(pm[:, sl, 1], pm[:, sl, 1], p2[:, m % 2, 1], sub).then_inc(frame_in, 1)

            def scan(m):
                pair, d, sl, add, sub, cosine, sine = terms(m)
                r = par[:, 0, d, pair:pair + 1].to_broadcast([P, T])
                step = 1 if d == 0 else -1
                v.wait_ge(frame_in, 2 * (m + 1))
                for i in range(2):
                    nc.vector.tensor_tensor_scan(p2[:, m % 2, i, ::step], r, pm[:, sl, i, ::step], 0.0,
                                                 ALU.mult, ALU.add).then_inc(scanned, 1)

            def out_products(m):
                pair, d, sl, add, sub, cosine, sine = terms(m)
                v.wait_ge(scanned, 2 * (m + 1))
                if m >= 1:
                    v.wait_ge(rot_done, 2 * m)
                tt(pm[:, sl], p2[:, m % 2], cosine, ALU.mult).then_inc(frame_out, 1)
                tt(ysum[:], p2[:, m % 2, ::-1], sine, ALU.mult).then_inc(frame_out, 1)

            def out_of_frame(m):
                pair, d, sl, add, sub, cosine, sine = terms(m)
                v.wait_ge(frame_out, 2 * (m + 1))
                tt(pm[:, sl, 0], pm[:, sl, 0], ysum[:, 0], sub).then_inc(rot_done, 1)
                tt(pm[:, sl, 1], pm[:, sl, 1], ysum[:, 1], add).then_inc(rot_done, 1)

            def s5_slot(q):
                t = gelu_tile(q)
                inner = psum[:, 6 + (t or 0) % 2, T:2 * T]
                if t is not None:
                    v.wait_ge(y_mm, 2 * PT * (t + 1))
                    stt(u[:, t], u[:, t], gcol[:, 80 + t:81 + t], psum[:, 6 + t % 2, 0:T], ALU.mult, ALU.add) \
                        .then_inc(y_done, 1)
                for m in (2 * q, 2 * q + 1):
                    if m < 2 * NPAIR:
                        times_sine(m)
                    if t is not None and m % 2 == 0:
                        v.wait_ge(y_done, t + 1)
                        tt(inner, u[:, t], u[:, t], ALU.mult).then_inc(gelu_square, 1)
                    if 1 <= m <= 2 * NPAIR:
                        out_products(m - 1)
                    if t is not None and m % 2 == 0:
                        v.wait_ge(gelu_square, t + 1)
                        stt(inner, inner, 1.0 / GELU_A, u[:, t], ALU.add, ALU.mult).then_inc(gelu_in, 1)
                    if m < 2 * NPAIR:
                        into_frame(m)
                    if 1 <= m <= 2 * NPAIR:
                        out_of_frame(m - 1)
                    if m < 2 * NPAIR:
                        scan(m)
                if t is not None:
                    v.wait_ge(gelu_tanh, t + 1)
                    stt(u[:, t], inner, 1.0, u[:, t], ALU.add, ALU.mult).then_inc(gelu_out, 1)

            q_store = store(lambda i, j0, jb, n: qk_a[:, 0, 2 * (j0 + jb - J_Q) + n])
            k_store = store(lambda i, j0, jb, n: qk_a[:, 1, 2 * (j0 + jb - J_K) + n])
            v_store = store(lambda i, j0, jb, n: v_a[:, n, BLK * (j0 + jb - J_V):BLK * (j0 + jb - J_V + 1)])
            kinds = [q_store] * 4 + [k_store] * 4 + [v_store] * 4
            for j in range(J_Q, J_GLU):
                slots = S5_SLOTS[j]
                low(0, j, 0, 3)
                if j > J_Q:
                    kinds[j - 1 - J_Q](0, j - 1, 0)
                for k in range(3):
                    if k < len(slots):
                        s5_slot(slots[k])
                    low(0, j, 1, k)
            kinds[-1](0, J_GLU - 1, 0)

            def scores(hh, b, ss, bias):
                v.wait_ge(sc_mm, hh + 1)
                v.wait_ge(bias_masked, hh + 1)
                if not (isinstance(hh, int) and hh < 2):
                    v.wait_ge(pt_tr, hh - 1)
                stt(ss[:, b].rearrange("p q t -> p (q t)"), psum[:, 4 + b, :], SCALE,
                    bias[:, b].rearrange("p q t -> p (q t)"), ALU.mult, ALU.add).then_inc(sc_sum, 1)
                v.wait_ge(sc_sum, hh + 1)
                nc.vector.tensor_reduce(stat[:, b, 0], ss[:, b], AX_X, ALU.max, negate=True).then_inc(sc_max, 1)

            def probs(hh, b, ss, cnt):
                v.wait_ge(exp_done, hh * 2 + 2)
                if cnt is not None:
                    for qt in range(2):
                        nc.vector.scalar_tensor_tensor(out=ss[:, b, qt], in0=ss[:, b, qt], scalar=1.0,
                                                       in1=cnt[:, qt], op0=ALU.mult, op1=ALU.mult,
                                                       accum_out=stat[:, b, 1, qt:qt + 1]).then_inc(cnt_done, 1)
                    v.wait_ge(cnt_done, 2 * hh + 2)
                nc.vector.reciprocal(stat[:, b, 2], stat[:, b, 1]).then_inc(inv_done, 1)
                v.wait_ge(inv_done, hh + 1)
                for qt in range(2):
                    nc.vector.tensor_scalar(ss[:, b, qt], ss[:, b, qt], stat[:, b, 2, qt:qt + 1],
                                            None, ALU.mult).then_inc(prob_done, 1)

            def probs_low(hh, b, pt):
                v.wait_ge(pt_hi, hh + 1)
                tt(pt[:, b, :, 1, :], psum[:, 6 + b].rearrange("p (k t) -> p k t", k=2),
                   pt[:, b, :, 0, :].bitcast(F32), ALU.subtract).then_inc(pt_ready, 1)

            def out_low(hh, b, dst, high_half):
                v.wait_ge(o_hi, hh + 1)
                tt(dst, psum[:, 6 + b, 0:T], high_half.bitcast(F32), ALU.subtract).then_inc(o_ready, 1)

            def head_low(h):
                v.wait_ge(head_hi, 2 * h + 2)
                tt(qk_s[:, h % 3, :, 1], qk_a[:, :, h], qk_s[:, h % 3, :, 0].bitcast(F32), ALU.subtract) \
                    .then_inc(head_split, 1)
                tt(v_s[:, h % 3, 1].rearrange("p (k d) -> p k d", k=2), v_a[:, :, h * HD:(h + 1) * HD],
                   v_s[:, h % 3, 0].rearrange("p (k d) -> p k d", k=2).bitcast(F32), ALU.subtract) \
                    .then_inc(head_split, 1)

            def head_step(g):
                if g + 1 < HA:
                    scores(g + 1, (g + 1) % 2, ss_a, bias_a)
                if g < HA:
                    probs_low(g, g % 2, pt_a)
                if 1 <= g <= HA:
                    out_low(g - 1, (g - 1) % 2, act[:, g - 1, 1, :], act[:, g - 1, 0, :])
                if g + 1 < HA:
                    probs(g + 1, (g + 1) % 2, ss_a, cnt_a)
                if g + 2 < HA:
                    head_low(g + 2)

            head_low(0)
            for t in range(NT):
                v.wait_ge(y_hi, t + 1)
                stt(act[:, NT + t, 1, :], u[:, t], 0.5, act[:, NT + t, 0, :].bitcast(F32), ALU.mult, ALU.subtract) \
                    .then_inc(y_split, 1)
            v.wait_ge(mask_in, 32)
            scores(0, 0, ss_a, bias_a)
            head_low(1)
            probs(0, 0, ss_a, cnt_a)

            low(0, J_GLU, 0, 3)
            for g in range(8):
                if g < 7:
                    low(0, J_GLU + 1 + g // 4, 0, g % 4)
                head_step(g)
                if g % 2:
                    jb, half_block = g // 4, g // 2 % 2
                    if g > 1:
                        v.wait_ge(glu_out, g - 1)
                    for n in range(2):
                        tile_sum(0, J_GLU + jb, 0, n, ysum[:, n], glu_group=half_block)
                    for n in range(2):
                        f = g - 1 + n
                        v.wait_ge(glu_tanh, f + 1)
                        stt(u[:, f], ysum[:, n], 1.0, u[:, f], ALU.add, ALU.mult).then_inc(glu_out, 1)
            head_step(8)
            for f in range(NT):
                v.wait_ge(ob_hi, f + 1)
                stt(act[:, NT + f, 1, :], u[:, f], 0.25, act[:, NT + f, 0, :].bitcast(F32), ALU.mult, ALU.subtract) \
                    .then_inc(ob_ready, 1)
            loop_blocks(J_OUT0, 8, residual(16))
            norm(1, 32)

            def mlp(j0, x0, h0, last):
                for qu in range(4):
                    v.wait_ge(x_ready, x0 + 16 * qu)
                    loop_blocks(j0 + 16 * qu, 8, squared_relu(h0 + 16 * qu), first=(h0 + qu == 0))
                    v.wait_ge(relu_sq, h0 + 16 * (qu + 1))
                    loop_blocks(j0 + 16 * qu + 8, 8, residual(x0 + 16 * qu), last=(last and qu == 3))

            mlp(J_MLP0, 32, 0, False)
            norm(2, 16)

            def split_store(turn, jb):
                pair, kind = jb // 3, jb % 3
                t3, at_ = turn * 3, [turn * 12 + (2 * jb + n + 1) for n in range(2)]

                def dst(n, part):
                    return v_c[:, pair, n, part, :] if kind == 2 else qk_c[:, pair, kind, n, part, :]

                if not (isinstance(turn, int) and jb == 0):
                    v.wait_ge(qkv_ready, turn * 12 + 2 * jb)
                for n in range(2):
                    tile_sum(t3, J_QKV1, jb, n, ysum[:, n])
                for n in range(2):
                    v.wait_ge(tiles_out, t3 * 4 + (tile0(J_QKV1 + jb) + n + 1))
                    nc.vector.tensor_copy(dst(n, 0), ysum[:, n]).then_inc(qkv_hi, 1)
                for n in range(2):
                    v.wait_ge(qkv_hi, at_[n])
                    tt(dst(n, 1), ysum[:, n], dst(n, 0).bitcast(F32), ALU.subtract).then_inc(qkv_ready, 1)

            def outs_low_c(turn, pair):
                for b in range(2):
                    h = turn * 4 + (2 * pair + b)
                    out_low(h + HA, b, at_head(o_c, h, 1), at_head(o_c, h, 0))

            def qkv_blocks(turn, first=False):
                t3 = turn * 3
                for jb in range(6):
                    pair, kind = jb // 3, jb % 3
                    head = [turn * 4 + (HA + 2 * pair + b) for b in range(2)]
                    low(t3, J_QKV1, jb, 3)
                    for k in range(3):
                        low(t3, J_QKV1, jb + 1, k)
                        for b in range(2):
                            if kind == 2 and k == 1:
                                scores(head[b], b, ss_c, bias_c)
                            if kind == 2 and k == 2:
                                probs(head[b], b, ss_c, None)
                            if kind == 0 and k == 0 and not (first and pair == 0):
                                probs_low(head[b] - 2, b, pt_c)
                        if kind == 0 and k == 2 and not (first and pair == 0):
                            outs_low_c(turn, pair - 1)
                    split_store(turn, jb)

            qkv_blocks(0, first=True)
            with v.Fori(1, 4) as turn:
                qkv_blocks(turn)
            evac_out1 = residual(96)
            low(0, J_OUT1, 0, 3)
            for s in range(3):
                low(0, J_OUT1, 1, s)
                if s == 0:
                    for b in range(2):
                        probs_low(HA + HC - 2 + b, b, pt_c)
                if s == 2:
                    outs_low_c(4, -1)
            evac_out1(0, J_OUT1, 0)
            block_step(0, J_OUT1, 1, evac_out1)
            with v.Fori(1, 4) as i:
                block_step(i, J_OUT1, 0, evac_out1)
                block_step(i, J_OUT1, 1, evac_out1)
            norm(3, 48)
            mlp(J_MLP1, 112, 64, True)
            norm(4, 64)

        @block.tensor
        def _(pe):
            pe.wait_ge(small_in, 16 * 7)
            pe.transpose(psum[:, 0, 0:88], grow[:, :], ident[0:88, 0:88]).then_inc(g_tr, 1)
            pe.matmul(psum[0:HA, 1, :], t5tab[:], onehot[:], start=True, stop=True).then_inc(t5_mm, 1)
            pe.wait_ge(x_in, 32)
            for g in range(KT // 2):
                if g >= 4:
                    pe.wait_ge(x_ready, 2 * (g - 3))
                for k in range(2):
                    for tt_ in range(2):
                        kt = 2 * g + k
                        last = pe.transpose(psum[:, 4 + g % 4, k * T + tt_ * P:k * T + (tt_ + 1) * P],
                                            xin[:, tt_, kt * P:(kt + 1) * P], ident[:])
                last.then_inc(x_tr, 1)

            def norm(n):
                pe.wait_ge(ssum_done, KT * (n + 1))
                pe.matmul(psum[:, 7, 0:T], ones[:], ssum[:], start=True, stop=True).then_inc(norm_mm, 1)

            def block_mm(i, j0, jb, operand, ready, token_major=False, between=None):
                banks = 2 * ((j0 + jb) % 2)
                t = tile0(j0 + jb)
                if t >= 4:
                    pe.wait_ge(tiles_out, i * 4 + (t - 2))
                for s in range(4):
                    pe.wait_ge(lo_done, i * 8 + (4 * (j0 + jb) + s + 1))
                    for k in range(SUBK):
                        kt = SUBK * s + k
                        ready(kt)
                        first, final = kt == 0, kt == KT - 1
                        for n in range(2):
                            cols = slice(n * P, (n + 1) * P)
                            if token_major:
                                w_hi, w_all = whl[:, s, k, 0, :], whl[:, s, k, :, :].rearrange("p h t -> p (h t)")
                                big = (operand[:, kt, 0, cols], w_all)
                                little = (operand[:, kt, 1, cols], w_hi)
                            else:
                                big = (whl[:, s, k, 0, cols], operand[:, kt, :, :].rearrange("p h t -> p (h t)"))
                                little = (whl[:, s, k, 1, cols], operand[:, kt, 0, :])
                            bank = psum[:, banks + n]
                            pe.matmul(bank, *big, start=first, stop=False, skip_group_check=True)
                            last = pe.matmul(bank[:, 0:T], *little, start=False, stop=final, skip_group_check=True)
                    last.then_inc(subs_used, 1)
                    if between:
                        between(s)

            def by_count(semaphore, base, group=2):
                def ready(kt):
                    if kt % group == 0:
                        pe.wait_ge(semaphore, base + kt + group)
                return ready

            def nothing(kt):
                pass

            def loop_blocks(j0, n, operand, ready, token_major=False):
                with pe.Fori(0, n // 2) as i:
                    block_mm(i, j0, 0, operand, ready, token_major)
                    block_mm(i, j0, 1, operand, ready, token_major)

            pe.wait_ge(ones_set, 1)
            pe.wait_ge(x_ready, 16)
            norm(0)
            pe.wait_ge(g_ready, 1)
            pe.wait_ge(t5_ev, 1)
            block_mm(0, 0, 0, act, by_count(act_ready, 0))
            pe.wait_ge(step_v, SMALL_STEPS)
            pe.wait_ge(step_a, 2)
            for k, src in enumerate((3, 14, 13, 5, 6)):
                last = pe.transpose(psum[:, 4 + k // 4, (k % 4) * P:(k % 4 + 1) * P], rows[:, src], ident[:])
            last.then_inc(par_tr, 1)
            pe.wait_ge(b_in, 16 * 4)
            pe.wait_ge(norm_std, 1)
            for g in range(4):
                if g >= 2:
                    pe.wait_ge(bt_ready, g - 1)
                for k in range(4):
                    t, i = 2 * g + k // 2, k % 2
                    last = pe.transpose(psum[:, 6 + g % 2, k * P:(k + 1) * P],
                                        bnat[:, i, PT * t:PT * (t + 1), :].rearrange("p r c -> p (r c)"), ident[:])
                last.then_inc(b_tr, 1)
            block_mm(0, 1, 0, act, nothing)
            block_mm(0, 2, 0, act, nothing)
            pe.wait_ge(c_in, 16 * 8)
            pe.wait_ge(par_ready, 8)
            for c in range(2 * NT):
                d, t = c // NT, c % NT
                if c >= 2:
                    pe.wait_ge(c_mul, 2 * (c - 1))
                for i in range(2):
                    last = pe.transpose(psum[:, 4 + c % 2, i * P:(i + 1) * P],
                                        cnat[:, d, i, t].rearrange("p w s -> p (w s)"), ident[:])
                last.then_inc(c_tr, 1)
            block_mm(0, 3, 0, act, nothing)

            def s5_in(pair):
                if pair >= NPAIR:
                    return
                t, r = pair // PT, slice(32 * (pair % PT), 32 * (pair % PT + 1))
                if pair >= 2:
                    pe.wait_ge(frame_in, 4 * (pair - 1))
                else:
                    pe.wait_ge(c_mul, 4 * NT)
                for i in range(2):
                    last = pe.matmul(psum[:, 4 + pair % 2, i * T:(i + 1) * T], bt[r, t, i, :], u[r, t, :],
                                     start=True, stop=True)
                last.then_inc(bu_done, 1)

            def s5_out(m):
                if not 0 <= m < 2 * NPAIR:
                    return
                pair, d = m // 2, m % 2
                t, r = pair // PT, slice(32 * (pair % PT), 32 * (pair % PT + 1))
                if t >= 2 and m % (2 * PT) == 0:
                    pe.wait_ge(y_done, t - 1)
                pe.wait_ge(rot_done, 2 * (m + 1))
                for i in range(2):
                    last = pe.matmul(psum[r, 6 + t % 2, 0:T], fmat[:, d, i, pair, :], pm[:, m % 4, i],
                                     start=(d == 0 and i == 0), stop=(d == 1 and i == 1))
                last.then_inc(y_mm, 1)

            pe.wait_ge(bt_ready, 4)
            pe.wait_ge(f_ready, 4 * NT)
            pe.wait_ge(tiles_out, 8)
            s5_in(0)
            for j in range(J_Q, J_GLU):
                slots = S5_SLOTS[j]

                def between(s, slots=slots):
                    if s < len(slots):
                        s5_in(slots[s] + 1)
                        s5_out(2 * slots[s] - 1)
                        s5_out(2 * slots[s])

                block_mm(0, j, 0, act, nothing, token_major=(j >= J_V), between=between)

            def exact(dst, products):
                for c, (w, m) in enumerate(products):
                    for p, (wp, mp) in enumerate(((0, 0), (0, 1), (1, 0))):
                        last = pe.matmul(dst, w(wp), m(mp), start=(c == 0 and p == 0),
                                         stop=(c == len(products) - 1 and p == 2), skip_group_check=True)
                return last

            def scores(hh, b, q, k):
                if not (isinstance(hh, int) and hh < 2):
                    pe.wait_ge(sc_sum, hh - 1)
                for qt in range(2):
                    last = exact(psum[:, 4 + b, qt * T:(qt + 1) * T],
                                 [(lambda part: q(part)[:, qt * P:(qt + 1) * P], k)])
                last.then_inc(sc_mm, 1)

            def transposes(hh, b, ss):
                pe.wait_ge(prob_done, hh * 2 + 2)
                if not (isinstance(hh, int) and hh < 2):
                    pe.wait_ge(o_ready, hh - 1)
                for kt in range(2):
                    for qt in range(2):
                        last = pe.transpose(psum[:, 6 + b, kt * T + qt * P:kt * T + (qt + 1) * P],
                                            ss[:, b, qt, kt * P:(kt + 1) * P], ident[:])
                last.then_inc(pt_tr, 1)

            def output(hh, b, values, pt):
                pe.wait_ge(pt_ready, hh + 1)
                exact(psum[:, 6 + b, 0:T],
                      [(lambda part, kt=kt: values(kt, part), lambda part, kt=kt: pt[:, b, kt, part, :])
                       for kt in range(2)]).then_inc(pv_mm, 1)

            def scores_a(h):
                pe.wait_ge(head_split, 2 * h + 2)
                scores(h, h % 2, lambda part: qk_s[:, h % 3, 0, part], lambda part: qk_s[:, h % 3, 1, part])

            def output_a(h):
                output(h, h % 2, lambda kt, part: v_s[:, h % 3, part, kt * P:(kt + 1) * P], pt_a)

            pe.wait_ge(tiles_out, tile0(J_GLU))
            pe.wait_ge(y_done, NT)
            scores_a(0)
            for g in range(8):
                jb, s = g // 4, g % 4
                half_block = s // 2
                if s % 2 == 0:
                    pe.wait_ge(tiles_out, tile0(J_GLU + jb) + 2 * half_block - 2)
                pe.wait_ge(lo_done, 4 * (J_GLU + jb) + s + 1)
                for k in range(SUBK):
                    kt = SUBK * (s % 2) + k
                    pe.wait_ge(y_split, kt + 1)
                    for n in range(2):
                        cols = slice(n * P, (n + 1) * P)
                        bank = psum[:, 2 * half_block + n]
                        pe.matmul(bank, whl[:, s, k, 0, cols], act[:, NT + kt].rearrange("p h t -> p (h t)"),
                                  start=(kt == 0), stop=False, skip_group_check=True)
                        last = pe.matmul(bank[:, 0:T], whl[:, s, k, 1, cols], act[:, NT + kt, 0, :],
                                         start=False, stop=(kt == NT - 1), skip_group_check=True)
                last.then_inc(subs_used, 1)
                if g + 1 < HA:
                    scores_a(g + 1)
                transposes(g, g % 2, ss_a)
                if g >= 1:
                    output_a(g - 1)
            output_a(HA - 1)

            def merged(kt):
                if kt < HA:
                    pe.wait_ge(o_ready, kt + 1)
                else:
                    pe.wait_ge(ob_ready, kt - HA + 1)

            loop_blocks(J_OUT0, 8, act, merged)

            def mlp(j0, n, h0):
                norm(n)
                for qu in range(4):
                    loop_blocks(j0 + 16 * qu, 8, act, by_count(act_ready, KT * n))
                    loop_blocks(j0 + 16 * qu + 8, 8, hid, by_count(hid_ready, h0 + 16 * qu, 4))

            mlp(J_MLP0, 1, 0)
            norm(2)

            def scores_c(turn, pair):
                pe.wait_ge(qkv_ready, turn * 12 + (6 * pair + 4))
                for b in range(2):
                    scores(turn * 4 + (HA + 2 * pair + b), b,
                           lambda part: qk_c[:, pair, 0, b, part], lambda part: qk_c[:, pair, 1, b, part])

            def transposes_c(turn, pair):
                for b in range(2):
                    transposes(turn * 4 + (HA + 2 * pair + b), b, ss_c)

            def outputs_c(turn, slot, back):
                pe.wait_ge(qkv_ready, turn * 12 + (6 * back + 6))
                for b in range(2):
                    output(turn * 4 + (HA + 2 * back + b), b,
                           lambda kt, part: v_c[:, slot, kt, part, b * HD:(b + 1) * HD], pt_c)

            def qkv_blocks(turn, first=False):
                for jb in range(6):
                    pair, kind = jb // 3, jb % 3

                    def between(s):
                        if kind == 2 and s == 1:
                            scores_c(turn, pair)
                        if kind == 0 and s == 0 and not (first and pair == 0):
                            transposes_c(turn, pair - 1)
                        if kind == 0 and s == 2 and not (first and pair == 0):
                            outputs_c(turn, 1 - pair, pair - 1)

                    ready = by_count(act_ready, 2 * KT) if first and jb == 0 else nothing
                    block_mm(turn * 3, J_QKV1, jb, act, ready, token_major=(kind == 2), between=between)

            qkv_blocks(0, first=True)
            with pe.Fori(1, 4) as turn:
                qkv_blocks(turn)

            def last_outputs(s):
                if s == 0:
                    transposes_c(4, -1)
                if s == 2:
                    outputs_c(4, 1, -1)

            heads_ready = by_count(o_ready, HA, 2)
            block_mm(0, J_OUT1, 0, o_c, heads_ready, between=last_outputs)
            block_mm(0, J_OUT1, 1, o_c, nothing)
            with pe.Fori(1, 4) as i:
                block_mm(i, J_OUT1, 0, o_c, nothing)
                block_mm(i, J_OUT1, 1, o_c, nothing)
            mlp(J_MLP1, 3, 64)
            norm(4)
            for g in range(8):
                q4, tt_ = g // 2, g % 2
                pe.wait_ge(nrm_done, 4 * KT + 4 * q4 + 4)
                if g >= 4:
                    pe.wait_ge(fin_ev, g - 3)
                for k in range(4):
                    last = pe.transpose(psum[:, g % 4, k * P:(k + 1) * P],
                                        xfin[:, 4 * q4 + k, tt_ * P:(tt_ + 1) * P], ident[:])
                last.then_inc(fin_tr, 1)


def shape_constants():
    rel = np.arange(T)[None, :] - np.arange(T)[:, None]
    branches = ((128, 1), (512, 4), (2048, 16))
    cnt = sum(((rel % d == 0) & (np.abs(rel) <= w // 2)).astype(np.float32) for w, d in branches)
    c = np.arange(GRID_W)
    start = np.clip(c - 8, 0, GRID_W - 16)
    ok = (c[None, :] >= start[:, None]) & (c[None, :] < start[:, None] + 16)
    ok = np.tile(ok, (ROWS, ROWS))
    d = np.arange(512) - 255
    n = np.abs(d)
    nf = np.maximum(n, 1).astype(np.float32)
    big = 8 + (np.log(nf / np.float32(8)) / np.float32(np.log(1024 / 8)) * np.float32(8)).astype(np.int32)
    bucket = np.where(d > 0, 16, 0) + np.where(n < 8, n, np.minimum(big, 15))
    fold = lambda m: np.ascontiguousarray(m.astype(np.float32).reshape(2, P, T).transpose(1, 0, 2))
    return {
        "c_ident": np.eye(P, dtype=np.float32),
        "c_onehot": (np.arange(32)[:, None] == bucket[None, :]).astype(np.float32),
        "c_cnt": fold(cnt),
        "c_neg_a": fold(np.where(cnt > 0, 0.0, NEG)),
        "c_neg_c": fold(np.where(ok, 0.0, NEG)),
    }


INPUTS = ["x", "t5_bias", "ab_w_in", "ab_w_out", "s5_lam_re", "s5_lam_im", "s5_log_step", "s5_b_re", "s5_b_im",
          "s5_c_re", "s5_c_im", "s5_d", "s5_w_glu", "c_w_qkv", "c_w_out", "c_rpb", "norm_mix", "norm_mlp",
          "mlp_w1", "mlp_w2", "norm_final"]


def kernel(**inputs):
    import concourse.bacc as bacc
    from concourse.bass_utils import run_bass_kernel_spmd

    nc = bacc.Bacc("TRN2", target_bir_lowering=False, num_devices=1)
    arrays = {name: np.ascontiguousarray(inputs[name]) for name in INPUTS} | shape_constants()
    ins = {name: nc.dram_tensor(f"in_{name}", a.shape, F32, kind="ExternalInput").ap() for name, a in arrays.items()}
    out = nc.dram_tensor("out_0", (1, T, D), F32, kind="ExternalOutput").ap()
    build(nc, ins, out)
    result = run_bass_kernel_spmd(nc, [{f"in_{name}": a for name, a in arrays.items()}], core_ids=[0])
    return result.results[0]["out_0"]
```

```python
from contextlib import ExitStack

import numpy as np

import concourse.bass as bass
from concourse import mybir

F32 = mybir.dt.float32
F32R = mybir.dt.float32r
ALU = mybir.AluOpType
ACT = mybir.ActivationFunctionType
AX_X = mybir.AxisListType.X

P = 128
D = 2048
T = 256
KT = D // P
HD = 128
HA = 8
HC = 16
FF = 4 * D
QUARTER = FF // 4
CH = 16
NST = 64
NG = 64
NPAIR = NG // 2
PT = 4
NT = NPAIR // PT
GRID_W = 64
ROWS = T // GRID_W
RPB_COLS = 31
RPB_PAD = 127
EPS = 1e-6
NEG = -1e30
SCALE = 1.0 / float(np.sqrt(HD))
BLK = 256
SUBK = 4
RAWK = 8
TB = 16
MAGIC = 12582912.0
TWO_PI = 2.0 * np.pi
C1 = 6.28125
C2 = float(np.round((TWO_PI - C1) * 2.0**20) / 2.0**20)
C3 = float(np.float32(TWO_PI - C1 - C2))
GELU_A = 0.044715
GELU_B = float(np.sqrt(2.0 / np.pi))

J_U = 0
J_Q, J_K, J_V = 4, 8, 12
J_GLU = 16
J_OUT0 = J_GLU + 2
J_MLP0 = J_OUT0 + 8
J_QKV1 = J_MLP0 + 64
J_OUT1 = J_QKV1 + 24
J_MLP1 = J_OUT1 + 8
J_END = J_MLP1 + 64


def gelu_tile(q):
    t = (q - 5) // PT
    return t if q >= 5 and (q - 5) % PT == 0 and t < NT else None


def tile0(j):
    return 2 * j + 2 * min(max(j - J_GLU, 0), 2)


X_BEFORE = [0, 16, 80, 96, 160]


S5_SLOTS = {}
_next = 0
for _j in range(J_Q, J_GLU):
    _n = 3 if _j < J_Q + (NPAIR + 2) - 2 * (J_GLU - J_Q) else 2
    S5_SLOTS[_j] = list(range(_next, _next + _n))
    _next += _n
SMALL_STEPS = 56


def at_head(o, h, part):
    return o[:, h, part, :] if isinstance(h, int) else o[:, bass.ds(h, 1), part, :].rearrange("p o t -> p (o t)")


def build(nc, ins, out):
    ctx = ExitStack()
    KB = 1024
    arena = (nc.sbuf_base + 31) // 32 * 32

    def at(name, shape, off, dt=F32):
        return nc.alloc_sbuf_tensor_at(name, shape, dt, offset=arena + int(off))

    with ctx:
        def sem(name):
            return ctx.enter_context(nc.semaphore(name))

        raw = at("raw", [P, 4, RAWK, BLK], 0)
        whl = at("whl", [P, 4, SUBK, 2, BLK], 32 * KB, F32R)
        x = at("x", [P, KT, T], 64 * KB)
        xn = at("xn", [P, 2, D], 64 * KB)
        act = at("act", [P, KT, 2, T], 80 * KB, F32R)
        half = at("half", [P, 2, T], 112 * KB)
        ysum = at("ysum", [P, 2, T], 114 * KB)
        ident = at("ident", [P, P], 116 * KB)
        ones = at("ones", [P, P], 116.5 * KB)
        gcol = at("gcol", [P, 88], 117 * KB)
        small = at("small", [P, 64], 117.5 * KB)
        eps_c = small[:, 0:1]
        lstep = small[:, 1:2]
        tok = small[:, 2:6]
        stat = small[:, 8:32].rearrange("p (a k q) -> p a k q", a=2, k=6)
        U0 = 118 * KB
        qk_a = at("qk_a", [P, 2, HA, T], U0)
        v_a = at("v_a", [P, 2, HA * HD], U0 + 16 * KB)
        u = at("u", [P, NT, T], U0 + 24 * KB)
        bt = at("bt", [P, NT, 2, P], U0 + 32 * KB)
        fmat = at("fmat", [P, 2, 2, NPAIR, 2 * CH], U0 + 40 * KB)
        tab0 = at("tab0", [P, 2, 2, NPAIR, TB], U0 + 56 * KB)
        tab1 = at("tab1", [P, 2, 2, NPAIR, T // 2 // TB], U0 + 64 * KB)
        par = at("par", [P, 3, 2, NPAIR], U0 + 68 * KB)
        tcs = at("tcs", [P, 4, 2, T], U0 + 68.75 * KB)
        pm = at("pm", [P, 4, 2, T], U0 + 76.75 * KB)
        p2 = at("p2", [P, 2, 2, T], U0 + 84.75 * KB)
        turned = at("turned", [P, 2, T // 2], U0 + 88.75 * KB)
        ss_a = at("ss_a", [P, 2, 2, T], U0 + 32 * KB)
        bias_a = at("bias_a", [P, 2, 2, T], U0 + 36 * KB)
        cnt_a = at("cnt_a", [P, 2, T], U0 + 40 * KB)
        neg_a = at("neg_a", [P, 2, T], U0 + 42 * KB)
        pt_a = at("pt_a", [P, 2, 2, 2, T], U0 + 44 * KB, F32R)
        qk_s = at("qk_s", [P, 3, 2, 2, T], U0 + 52 * KB, F32R)
        v_s = at("v_s", [P, 3, 2, T], U0 + 64 * KB, F32R)
        cnat = at("cnat", [P, 2, 2, NT, 2, NST], U0)
        rows = at("rows", [P, 16, 2 * NST], U0 + 16 * KB)
        t5sb = at("t5sb", [HA, 512], U0 + 70.5 * KB)
        t5tab = at("t5tab", [32, HA], U0 + 88.75 * KB)
        onehot = at("onehot", [32, 512], U0 + 86.75 * KB)
        grow = at("grow", [88, P], U0 + 69 * KB)
        xin = at("xin", [P, 2, D], U0 + 40 * KB)
        bnat = at("bnat", [P, 2, NPAIR, 2 * CH], U0 + 56 * KB)
        zt = at("zt", [P, 2, 3, NPAIR, 2], U0 + 72.75 * KB)
        ctmp = at("ctmp", [P, 2, 2, P], U0 + 74.25 * KB)
        rpbw = at("rpbw", [HC, 7, RPB_PAD], U0 + 76.75 * KB)
        ssum = at("ssum", [P, T], U0 + 84.75 * KB)
        rstd = at("rstd", [P, T], U0 + 85.75 * KB)
        sq = at("sq", [P, T], U0 + 86.75 * KB)
        rsq = at("rsq", [P, T], U0 + 87.75 * KB)
        hid = at("hid", [P, KT, 2, T], U0, F32R)
        hsq = at("hsq", [P, 2, T], U0 + 32 * KB)
        qk_c = at("qk_c", [P, 2, 2, 2, 2, T], U0, F32R)
        v_c = at("v_c", [P, 2, 2, 2, 2 * HD], U0 + 16 * KB, F32R)
        o_c = at("o_c", [P, HC, 2, T], U0 + 24 * KB, F32R)
        pt_c = at("pt_c", [P, 2, 2, 2, T], U0 + 56 * KB, F32R)
        ss_c = at("ss_c", [P, 2, 2, T], U0 + 64 * KB)
        bias_c = at("bias_c", [P, 2, 2, T], U0 + 68 * KB)
        neg_c = at("neg_c", [P, 2, T], U0 + 72 * KB)
        xfin = at("xfin", [P, KT, T], U0)
        outs = at("outs", [P, 8, 512], U0 + 16 * KB)

        psum = ctx.enter_context(nc.psum_tensor("psum", [P, 8, 512], F32))

        t5_dram = nc.dram_tensor("t5_rel", [P, HA, 512], F32).ap()
        rpb_dram = nc.dram_tensor("rpb_pad", [GRID_W, HC, 7 * RPB_PAD], F32).ap()

        raw_in = [sem(f"raw_in{s}") for s in range(4)]
        x_in = [sem("x_in0"), sem("x_in1")]
        ident_in, gain_in, t5_in = sem("ident_in"), sem("gain_in"), sem("t5_in")
        tok_sq, tok_std, tok_inv, xn_done = sem("tok_sq"), sem("tok_std"), sem("tok_inv"), sem("xn_done")
        xn_tr = sem("xn_tr")
        rows_in = sem("rows_in")
        b_in, c_in = sem("b_in"), sem("c_in")
        b_zero = sem("b_zero")
        ones_set = sem("ones_set")
        rpb_zero, rpb_in, rpb_out = sem("rpb_zero"), sem("rpb_in"), sem("rpb_out")
        t5_out = sem("t5_out")
        hi_done = sem("hi_done")
        lo_done = sem("lo_done")
        subs_used = sem("subs_used")
        half_done = sem("half_done")
        tiles_out = sem("tiles_out")
        x_tr = sem("x_tr")
        x_ready = sem("x_ready")
        g_tr, g_ready = sem("g_tr"), sem("g_ready")
        t5_mm, t5_ev = sem("t5_mm"), sem("t5_ev")
        sq_done, ssum_done = sem("sq_done"), sem("ssum_done")
        norm_mm, norm_std, norm_rstd = sem("norm_mm"), sem("norm_std"), sem("norm_rstd")
        rsq_done = sem("rsq_done")
        final_done = sem("final_done")
        act_hi, act_ready = sem("act_hi"), sem("act_ready")
        relu_scaled, relu_sq, hid_hi, hid_ready = sem("relu_scaled"), sem("relu_sq"), sem("hid_hi"), sem("hid_ready")
        lam_inv = sem("lam_inv")
        small_step = sem("small_step")
        step_a = sem("step_a")
        par_tr, par_ready = sem("par_tr"), sem("par_ready")
        b_tr, bt_ready = sem("b_tr"), sem("bt_ready")
        c_tr, c_mul, f_ready = sem("c_tr"), sem("c_mul"), sem("f_ready")
        pool_step = sem("pool_step")
        bu_done, bu_copied = sem("bu_done"), sem("bu_copied")
        tab_low, tab_turned = sem("tab_low"), sem("tab_turned")
        tcs_done, pm_done = sem("tcs_done"), sem("pm_done")
        sin_in, frame_in, scanned, frame_out = sem("sin_in"), sem("frame_in"), sem("scanned"), sem("frame_out")
        rot_done, y_mm, y_done = sem("rot_done"), sem("y_mm"), sem("y_done")
        gelu_square, gelu_in, gelu_tanh, gelu_out = sem("gelu_square"), sem("gelu_in"), sem("gelu_tanh"), sem("gelu_out")
        y_hi, y_split = sem("y_hi"), sem("y_split")
        glu_tanh, glu_out = sem("glu_tanh"), sem("glu_out")
        ob_hi, ob_ready = sem("ob_hi"), sem("ob_ready")
        mask_in = sem("mask_in")
        bias_in = [sem("bias_in0"), sem("bias_in1")]
        bias_masked = sem("bias_masked")
        qkv_scaled, qkv_hi, qkv_ready = sem("qkv_scaled"), sem("qkv_hi"), sem("qkv_ready")
        sc_mm, sc_sum, sc_max = sem("sc_mm"), sem("sc_sum"), sem("sc_max")
        exp_done, cnt_done, inv_done, prob_done = sem("exp_done"), sem("cnt_done"), sem("inv_done"), sem("prob_done")
        head_hi, head_split = sem("head_hi"), sem("head_split")
        pt_tr, pt_hi, pt_ready, pv_mm, o_hi, o_ready = sem("pt_tr"), sem("pt_hi"), sem("pt_ready"), sem("pv_mm"), sem("o_hi"), sem("o_ready")
        fin_tr = sem("fin_tr")
        fin_ev = [sem("fin_ev0"), sem("fin_ev1")]
        out_done = sem("out_done")

        block = ctx.enter_context(nc.Block())

        w_in, w_glu, w_out0 = ins["ab_w_in"][0], ins["s5_w_glu"][0], ins["ab_w_out"][0]
        w_qkv, w_out1 = ins["c_w_qkv"][0], ins["c_w_out"][0]
        AW = HA * HD
        STREAM = [
            (J_U, 4, w_in[:, 3 * AW:4 * AW]),
            (J_Q, 12, w_in[:, 0:3 * AW]),
            (J_GLU, 2, w_glu),
            (J_OUT0, 8, w_out0),
        ]

        def mlp_stream(layer, j0):
            w1, w2 = ins["mlp_w1"][layer], ins["mlp_w2"][layer]
            for qu in range(4):
                cols = slice(QUARTER * qu, QUARTER * (qu + 1))
                yield (j0 + 16 * qu, 8, w1[:, cols])
                yield (j0 + 16 * qu + 8, 8, w2[cols, :])

        STREAM += list(mlp_stream(0, J_MLP0))
        STREAM += [(J_QKV1, 24, w_qkv), (J_OUT1, 8, w_out1)]
        STREAM += list(mlp_stream(1, J_MLP1))

        @block.sync
        def _(sp):
            def load_bias_c(h, b):
                for r in range(ROWS):
                    skew = bass.AP(tensor=rpb_dram.tensor, offset=(3 - r) * RPB_PAD + GRID_W - 1,
                                   ap=[[7 * RPB_PAD, HC], [HC * 7 * RPB_PAD - 1, GRID_W], [RPB_PAD, ROWS], [1, GRID_W]])
                    src = skew[bass.ds(h, 1)].rearrange("o p r c -> (o p) r c")
                    dst = bias_c[GRID_W * (r % 2):GRID_W * (r % 2 + 1), b, r // 2, :]
                    sp.dma_start(dst.rearrange("p (r c) -> p r c", r=ROWS), src).then_inc(bias_in[b], 16)

            def load_b():
                sp.wait_ge(b_zero, 1)
                for i, name in enumerate(("s5_b_re", "s5_b_im")):
                    src = ins[name][0].rearrange("(r g) s c -> g s r c", g=2)
                    for g in range(2):
                        sp.dma_start(bnat[g * NST:(g + 1) * NST, i, :, g * CH:(g + 1) * CH], src[g]).then_inc(b_in, 16)

            def load_c():
                sp.wait_ge(rpb_zero, 1)
                sp.dma_start(rpbw[:, :, 48:48 + RPB_COLS], ins["c_rpb"][0, :, 4:11, :]).then_inc(rpb_in, 16)
                for d in range(2):
                    for i, name in enumerate(("s5_c_re", "s5_c_im")):
                        src = ins[name][0, d].rearrange("(t g) c s -> (g c) t s", g=8)
                        for twice in range(2):
                            sp.dma_start(cnat[:, d, i, :, twice, :], src).then_inc(c_in, 16)

            def store_rpb():
                sp.wait_ge(rpb_in, 16)
                sp.dma_start(rpb_dram.rearrange("r h n -> h r n"), rpbw[:].rearrange("h r n -> h (r n)").unsqueeze(1)
                            .to_broadcast([HC, GRID_W, 7 * RPB_PAD])).then_inc(rpb_out, 16)

            for tt in range(2):
                sp.dma_start(xin[:, tt, :], ins["x"][0, tt * P:(tt + 1) * P, :]).then_inc(x_in[tt], 16)
            for j0, n, w in STREAM:
                wk = w.rearrange("(k p) n -> p k n", p=P)
                if j0 == 0:
                    for r in range(2 * n):
                        if r == 1:
                            sp.wait_ge(rows_in, 16 * 5)
                        if r == 4:
                            load_b()
                        if r == 6:
                            load_c()
                        if r == 7:
                            store_rpb()
                        if r >= 4:
                            sp.wait_ge(lo_done, 2 * r - 6)
                        src = wk[:, RAWK * (r % 2):RAWK * (r % 2 + 1), r // 2 * BLK:(r // 2 + 1) * BLK]
                        sp.dma_start(raw[:, r % 4], src).then_inc(raw_in[r % 4], 16)
                    continue
                if j0 == J_QKV1:
                    sp.wait_ge(rpb_out, 16)
                if j0 == J_QKV1:
                    with sp.Fori(0, n // 6) as i:
                        for p in range(12):
                            block, piece = p // 2, p % 4
                            if p % 6 == 4:
                                sp.wait_ge(sc_sum, i * 4 + (HA + p // 6 * 2))
                                for b in range(2):
                                    load_bias_c(i * 4 + (p // 6 * 2 + b), b)
                            sp.wait_ge(lo_done, i * 24 + (4 * j0 + 2 * p - 6))
                            src = wk[:, RAWK * (p % 2):RAWK * (p % 2 + 1),
                                     bass.ds(i * (2 * BLK) + (block % 3 * D + block // 3 * BLK), BLK)]
                            sp.dma_start(raw[:, piece], src).then_inc(raw_in[piece], 16)
                    continue
                with sp.Fori(0, n // 2) as i:
                    for piece in range(4):
                        sp.wait_ge(lo_done, i * 8 + (4 * j0 + 2 * piece - 6))
                        if j0 == J_GLU:
                            src = wk[:, :, bass.ds(i * (4 * BLK) + piece * BLK, BLK)]
                        else:
                            src = wk[:, RAWK * (piece % 2):RAWK * (piece % 2 + 1),
                                     bass.ds(i * (2 * BLK) + piece // 2 * BLK, BLK)]
                        sp.dma_start(raw[:, piece], src).then_inc(raw_in[piece], 16)
            for g in range(8):
                sp.wait_ge(fin_ev[g % 2], g // 2 + 1)
                sp.dma_start(out[0, (g % 2) * P:(g % 2 + 1) * P, (g // 2) * 512:(g // 2 + 1) * 512],
                             outs[:, g]).then_inc(out_done, 16)
            sp.wait_ge(out_done, 16 * 8)

        @block.gpsimd
        def _(pool):
            pchain = [0]

            def link(instruction):
                pchain[0] += 1
                instruction.then_inc(pool_step, 1)
                pool.wait_ge(pool_step, pchain[0])

            nc.gpsimd.memset(ones[:], 1.0).then_inc(ones_set, 1)
            nc.gpsimd.memset(eps_c, EPS).then_inc(ones_set, 1)
            nc.gpsimd.memset(bnat[:], 0.0).then_inc(b_zero, 1)
            nc.gpsimd.memset(rpbw[:], 0.0).then_inc(rpb_zero, 1)

            small_chain = [0]

            def small_link(instruction):
                small_chain[0] += 1
                instruction.then_inc(small_step, 1)
                pool.wait_ge(small_step, small_chain[0])

            def ts(dst, src, c0, c1, op0=ALU.mult, op1=ALU.add):
                return nc.gpsimd.tensor_scalar(dst, src, c0, c1, op0, op1)

            def tt(dst, s0, s1, op):
                return nc.gpsimd.tensor_tensor(dst, s0, s1, op)

            def stt(dst, s0, c, s1, op0, op1):
                small_link(nc.gpsimd.tensor_scalar(rows[:, 9], s0, c, None, op0))
                return nc.gpsimd.tensor_tensor(dst, rows[:, 9], s1, op1)

            R = [rows[:, k] for k in range(16)]
            pool.wait_ge(rows_in, 16 * 5)
            small_link(nc.gpsimd.tensor_scalar(R[0], R[0], -1e-4, None, ALU.min))
            small_link(tt(R[15], R[0], R[0], ALU.mult))
            small_link(tt(R[9], R[1], R[1], ALU.mult))
            small_link(tt(R[15], R[15], R[9], ALU.add))
            pool.wait_ge(step_a, 1)
            small_link(nc.gpsimd.tensor_scalar(R[2], R[1], lstep, None, ALU.mult))
            small_link(ts(R[4], R[2], 1.0 / TWO_PI, MAGIC))
            small_link(nc.gpsimd.tensor_scalar(R[4], R[4], MAGIC, None, ALU.subtract))
            small_link(stt(R[5], R[4], -C1, R[2], ALU.mult, ALU.add))
            small_link(stt(R[5], R[4], -C2, R[5], ALU.mult, ALU.add))
            small_link(stt(R[5], R[4], -C3, R[5], ALU.mult, ALU.add))
            small_link(nc.gpsimd.tensor_scalar(R[5], R[5], 0.25, None, ALU.mult))
            small_link(tt(R[6], R[5], R[5], ALU.mult))
            small_link(nc.gpsimd.tensor_scalar(R[7], R[6], 1.0 / 362880, None, ALU.mult))
            for c in (-1.0 / 5040, 1.0 / 120, -1.0 / 6):
                small_link(stt(R[7], R[7], c, R[6], ALU.add, ALU.mult))
            small_link(stt(R[7], R[7], 1.0, R[5], ALU.add, ALU.mult))
            small_link(nc.gpsimd.tensor_scalar(R[8], R[6], -1.0 / 3628800, None, ALU.mult))
            for c in (1.0 / 40320, -1.0 / 720, 1.0 / 24, -0.5):
                small_link(stt(R[8], R[8], c, R[6], ALU.add, ALU.mult))
            small_link(nc.gpsimd.tensor_scalar(R[8], R[8], 1.0, None, ALU.add))
            for s_, c_, s2, c2 in ((7, 8, 11, 8), (11, 8, 13, 14)):
                small_link(stt(R[s2], R[s_], 2.0, R[c_], ALU.mult, ALU.mult))
                small_link(stt(R[12], R[s_], -2.0, R[s_], ALU.mult, ALU.mult))
                small_link(nc.gpsimd.tensor_scalar(R[c2], R[12], 1.0, None, ALU.add))
            pool.wait_ge(step_a, 2)
            small_link(tt(R[9], R[3], R[14], ALU.mult))
            small_link(nc.gpsimd.tensor_scalar(R[9], R[9], 1.0, None, ALU.subtract))
            small_link(tt(R[10], R[3], R[13], ALU.mult))
            pool.wait_ge(lam_inv, 1)
            small_link(tt(R[5], R[9], R[0], ALU.mult))
            small_link(tt(R[6], R[10], R[1], ALU.mult))
            small_link(tt(R[5], R[5], R[6], ALU.add))
            small_link(tt(R[5], R[5], R[15], ALU.mult))
            small_link(tt(R[6], R[10], R[0], ALU.mult))
            small_link(tt(R[7], R[9], R[1], ALU.mult))
            small_link(tt(R[6], R[6], R[7], ALU.subtract))
            small_link(tt(R[6], R[6], R[15], ALU.mult))
            small_link(nc.gpsimd.memset(zt[:], 0.0))
            assert small_chain[0] == SMALL_STEPS, small_chain[0]

            def norm_squares(n):
                for kt in range(KT):
                    pool.wait_ge(x_ready, X_BEFORE[n] + kt + 1)
                    if kt == 0:
                        nc.gpsimd.tensor_tensor(ssum[:], x[:, 0], x[:, 0], ALU.mult).then_inc(ssum_done, 1)
                        continue
                    pool.wait_ge(ssum_done, KT * (n - 1) + kt)
                    nc.gpsimd.tensor_tensor(sq[:], x[:, kt], x[:, kt], ALU.mult).then_inc(sq_done, 1)
                    pool.wait_ge(sq_done, (KT - 1) * (n - 1) + kt)
                    nc.gpsimd.tensor_tensor(ssum[:], ssum[:], sq[:], ALU.add).then_inc(ssum_done, 1)

            pool.wait_ge(par_ready, 2)
            pool.wait_ge(bt_ready, 4)

            def rot(t, i):
                return t[:, i].rearrange("p d g b -> p (d g) b")

            def angle_add(t, dst, a, b, n, into=None):
                ca, sa = rot(t, 0)[:, :, a:a + n], rot(t, 1)[:, :, a:a + n]
                cb = rot(t, 0)[:, :, b:b + 1].to_broadcast([P, 2 * NPAIR, n])
                sb_ = rot(t, 1)[:, :, b:b + 1].to_broadcast([P, 2 * NPAIR, n])
                tmp = p2[:].rearrange("p s a t -> p (s a t)")[:, 0:2 * NPAIR * n].rearrange("p (g b) -> p g b", b=n)
                co, so = into or (rot(t, 0)[:, :, dst:dst + n], rot(t, 1)[:, :, dst:dst + n])
                link(nc.gpsimd.tensor_tensor(co, ca, cb, ALU.mult))
                link(nc.gpsimd.tensor_tensor(tmp, sa, sb_, ALU.mult))
                link(nc.gpsimd.tensor_tensor(co, co, tmp, ALU.subtract))
                link(nc.gpsimd.tensor_tensor(so, sa, cb, ALU.mult))
                link(nc.gpsimd.tensor_tensor(tmp, ca, sb_, ALU.mult))
                link(nc.gpsimd.tensor_tensor(so, so, tmp, ALU.add))

            for t in (tab0, tab1):
                nc.gpsimd.memset(t[:, 0, :, :, 0], 1.0)
                link(nc.gpsimd.memset(t[:, 1, :, :, 0], 0.0))
            link(nc.gpsimd.tensor_copy(tab0[:, :, :, :, 1], par[:, 1:3]))
            for n in (1, 2, 4):
                angle_add(tab0, n + 1, 1, n, n)
            angle_add(tab0, 9, 1, 8, 7)
            c8, s8 = rot(tab0, 0)[:, :, 8:9], rot(tab0, 1)[:, :, 8:9]
            c16, s16 = rot(tab1, 0)[:, :, 1:2], rot(tab1, 1)[:, :, 1:2]
            tmp = p2[:].rearrange("p s a t -> p (s a t)")[:, 0:2 * NPAIR].rearrange("p (g b) -> p g b", b=1)
            link(nc.gpsimd.tensor_tensor(c16, c8, c8, ALU.mult))
            link(nc.gpsimd.tensor_tensor(tmp, s8, s8, ALU.mult))
            link(nc.gpsimd.tensor_tensor(c16, c16, tmp, ALU.subtract))
            link(nc.gpsimd.tensor_tensor(s16, s8, c8, ALU.mult))
            link(nc.gpsimd.tensor_tensor(s16, s16, s16, ALU.add))
            for n, count in ((1, 1), (2, 2), (4, 3)):
                angle_add(tab1, n + 1, 1, n, count)
            angle_add(tab1, None, 4, 4, 1, into=[par[:, 1 + k].rearrange("p d g -> p (d g)").unsqueeze(2) for k in range(2)])

            pool.wait_ge(t5_out, 16)
            HT = T // 2

            def table_low(m):
                if m >= 2 * NPAIR:
                    return
                pair, d = m // 2, m % 2
                if m == 2:
                    pool.wait_ge(f_ready, 4 * NT)
                if m >= 4:
                    pool.wait_ge(frame_out, 2 * (m - 3))
                co, so = tcs[:, m % 4, 0], tcs[:, m % 4, 1]

                def outer(i0, i1, dst):
                    a = tab1[:, i1, d, pair, :].unsqueeze(2).to_broadcast([P, HT // TB, TB])
                    b = tab0[:, i0, d, pair, :].unsqueeze(1).to_broadcast([P, HT // TB, TB])
                    return nc.gpsimd.tensor_tensor(dst.rearrange("p (a b) -> p a b", b=TB), a, b, ALU.mult)

                outer(0, 0, co[:, 0:HT])
                outer(1, 1, so[:, HT:T])
                outer(0, 1, so[:, 0:HT])
                link(outer(1, 0, co[:, HT:T]))
                nc.gpsimd.tensor_tensor(co[:, 0:HT], co[:, 0:HT], so[:, HT:T], ALU.subtract).then_inc(tab_low, 1)
                nc.gpsimd.tensor_tensor(so[:, 0:HT], so[:, 0:HT], co[:, HT:T], ALU.add).then_inc(tab_low, 1)

            table_low(0)
            for m in range(2 * NPAIR):
                table_low(m + 1)
                co, so = tcs[:, m % 4, 0], tcs[:, m % 4, 1]
                pool.wait_ge(tab_turned, 4 * (m + 1))
                nc.gpsimd.tensor_tensor(co[:, HT:T], co[:, HT:T], turned[:, 0], ALU.subtract).then_inc(tcs_done, 1)
                nc.gpsimd.tensor_tensor(so[:, HT:T], so[:, HT:T], turned[:, 1], ALU.add).then_inc(tcs_done, 1)
                pool.wait_ge(tcs_done, 2 * (m + 1))
                pool.wait_ge(bu_copied, m // 2 * 2 + 2)
                nc.gpsimd.tensor_tensor(pm[:, m % 4], pm[:, m % 4],
                                        co.unsqueeze(1).to_broadcast([P, 2, T]), ALU.mult).then_inc(pm_done, 1)

            def head_low(h):
                pool.wait_ge(head_hi, 2 * h + 2)
                tt(qk_s[:, h % 3, :, 1], qk_a[:, :, h], qk_s[:, h % 3, :, 0].bitcast(F32), ALU.subtract) \
                    .then_inc(head_split, 1)
                tt(v_s[:, h % 3, 1].rearrange("p (k d) -> p k d", k=2), v_a[:, :, h * HD:(h + 1) * HD],
                   v_s[:, h % 3, 0].rearrange("p (k d) -> p k d", k=2).bitcast(F32), ALU.subtract) \
                    .then_inc(head_split, 1)

            for h in range(HA):

                head_low(h)
                pool.wait_ge(mask_in, 32)
                pool.wait_ge(bias_in[h % 2], 32 * (h // 2 + 1))
                nc.gpsimd.tensor_tensor(bias_a[:, h % 2], bias_a[:, h % 2], neg_a[:], ALU.add).then_inc(bias_masked, 1)
            norm_squares(1)
            norm_squares(2)
            pool.wait_ge(mask_in, 48)
            for h in range(HC):
                pool.wait_ge(bias_in[h % 2], 32 * HA // 2 + 64 * (h // 2 + 1))
                nc.gpsimd.tensor_tensor(bias_c[:, h % 2], bias_c[:, h % 2], neg_c[:], ALU.add).then_inc(bias_masked, 1)
            norm_squares(3)
            norm_squares(4)

        @block.scalar
        def _(a):
            a.dma_start(ident[:], ins["c_ident"]).then_inc(ident_in, 16)
            a.dma_start(grow[0:32, :], ins["norm_mix"].rearrange("l (k p) -> (l k) p", p=P)).then_inc(gain_in, 16)
            a.dma_start(grow[32:64, :], ins["norm_mlp"].rearrange("l (k p) -> (l k) p", p=P)).then_inc(gain_in, 16)
            a.dma_start(grow[64:80, :], ins["norm_final"].rearrange("(k p) -> k p", p=P)).then_inc(gain_in, 16)
            a.dma_start(grow[80:88, :], ins["s5_d"][0].rearrange("(k p) -> k p", p=P)).then_inc(gain_in, 16)
            for twice in range(2):
                cols = slice(NST * twice, NST * (twice + 1))
                a.dma_start(rows[:, 0, cols], ins["s5_lam_re"][0].rearrange("d g s -> (d g) s")).then_inc(rows_in, 16)
                a.dma_start(rows[:, 1, cols], ins["s5_lam_im"][0].rearrange("d g s -> (d g) s")).then_inc(rows_in, 16)
            a.dma_start(lstep, ins["s5_log_step"].rearrange("a d (g o) -> (a d g) o", o=1)).then_inc(rows_in, 16)

            a.wait_ge(ones_set, 2)
            for tt in range(2):
                a.wait_ge(x_in[tt], 16)
                nc.scalar.activation(xn[:, tt], xin[:, tt], ACT.Square, accum_out=tok[:, tt:tt + 1]).then_inc(tok_sq, 1)
            a.wait_ge(tok_sq, 2)
            nc.scalar.activation(tok[:, 0:2], tok[:, 0:2], ACT.Sqrt, bias=eps_c, scale=1.0 / D).then_inc(tok_std, 1)

            a.wait_ge(rows_in, 16 * 5)
            nc.scalar.activation(lstep, lstep, ACT.Exp).then_inc(step_a, 1)
            a.wait_ge(small_step, 1)
            a.wait_ge(step_a, 1)
            nc.scalar.activation(rows[:, 3], rows[:, 0], ACT.Exp, scale=lstep).then_inc(step_a, 1)

            def raw_uses(i, j0, jb):
                return i * 16 + 16 * ((j0 + jb) // 2 + 1)

            def high(i, j0, jb, s):
                jp = (j0 + jb) % 2
                piece = 2 * jp + s // 2
                if s % 2 == 0:
                    a.wait_ge(raw_in[piece], raw_uses(i, j0, jb))
                if not (isinstance(i, int) and j0 + 2 * i + jb == 0):
                    a.wait_ge(subs_used, i * 8 + (4 * (j0 + jb) + s - 3))
                nc.scalar.activation(whl[:, s, :, 0, :], raw[:, piece, SUBK * (s % 2):SUBK * (s % 2 + 1), :],
                                     ACT.Copy).then_inc(hi_done, 1)

            def take_halves(i, j0, jb, glu_group=None):
                banks = 2 * ((j0 + jb) % 2 if glu_group is None else glu_group)
                done = 4 * (j0 + jb) + (4 if glu_group is None else 2 * glu_group + 2)
                t = tile0(j0 + jb) + (0 if glu_group is None else 2 * glu_group)
                a.wait_ge(subs_used, i * 8 + done)
                for n in range(2):
                    if t + n >= 2:
                        a.wait_ge(tiles_out, i * 4 + (t + n - 1))
                    nc.scalar.activation(half[:, n], psum[:, banks + n, T:2 * T], ACT.Copy).then_inc(half_done, 1)

            def block_step(i, j0, jb, last=False):
                high(i, j0, jb, 3)
                if not last:
                    for s in range(3):
                        high(i, j0, jb + 1, s)
                take_halves(i, j0, jb)

            def input_high(n, gains):
                for kt in range(KT):
                    a.wait_ge(x_ready, X_BEFORE[n] + kt + 1)
                    nc.scalar.activation(act[:, kt, 0, :], x[:, kt], ACT.Copy,
                                         scale=gcol[:, gains + kt:gains + kt + 1]).then_inc(act_hi, 1)

            def rms(n):
                a.wait_ge(norm_mm, n)
                nc.scalar.activation(rstd[:], psum[:, 7, 0:T], ACT.Sqrt, bias=eps_c, scale=1.0 / D).then_inc(norm_std, 1)
                if n == 2:
                    nc.scalar.activation(tok[:, 0:2], psum[:, 7, T:T + 2], ACT.Sqrt, bias=eps_c,
                                         scale=1.0 / D).then_inc(tok_std, 1)

            def mlp(n, j0, gains, last=False):
                input_high(n, gains)
                high(0, j0, 0, 3)
                rms(n)
                for s in range(3):
                    high(0, j0, 1, s)
                take_halves(0, j0, 0)
                block_step(0, j0, 1)
                loop_blocks(j0, 8, first=True)
                for k in range(1, 8):
                    loop_blocks(j0 + 8 * k, 8, last=(last and k == 7))

            def loop_blocks(j0, n, first=False, last=False):
                with a.Fori(1 if first else 0, n // 2 - (1 if last else 0)) as i:
                    block_step(i, j0, 0)
                    block_step(i, j0, 1)
                if last:
                    block_step(n // 2 - 1, j0, 0)
                    block_step(n // 2 - 1, j0, 1, last=True)

            for s in range(3):
                high(0, 0, 0, s)
            a.dma_start(onehot[:], ins["c_onehot"]).then_inc(t5_in, 16)
            a.dma_start(t5tab[:], ins["t5_bias"]).then_inc(t5_in, 16)
            for kt in range(KT):
                a.wait_ge(xn_tr, kt // 2 + 1)
                if kt == 0:
                    a.wait_ge(g_ready, 1)
                nc.scalar.activation(act[:, kt, 0, :], psum[:, 4 + kt // 2 % 4, kt % 2 * T:(kt % 2 + 1) * T], ACT.Copy,
                                     scale=gcol[:, kt:kt + 1]).then_inc(act_hi, 1)

            def take_b(g):
                a.wait_ge(b_tr, g + 1)
                nc.scalar.activation(bt[:, 2 * g:2 * g + 2].rearrange("p t i s -> p (t i s)"), psum[:, 6 + g % 2, :],
                                     ACT.Copy).then_inc(bt_ready, 1)

            high(0, 0, 0, 3)
            high(0, 1, 0, 0)
            take_b(0)
            take_b(1)
            high(0, 1, 0, 1)
            take_b(2)
            take_b(3)
            high(0, 1, 0, 2)
            take_halves(0, 0, 0)
            block_step(0, 1, 0)
            a.wait_ge(t5_mm, 1)
            nc.scalar.activation(t5sb[:], psum[0:HA, 7, :], ACT.Copy).then_inc(t5_ev, 1)
            a.wait_ge(t5_ev, 1)
            a.dma_start(t5_dram.rearrange("r h n -> h r n"),
                        t5sb[:].unsqueeze(1).to_broadcast([HA, P, 512])).then_inc(t5_out, 16)
            block_step(0, 2, 0)
            block_step(0, 3, 0)

            def take_bu(pair):
                if pair >= NPAIR:
                    return
                a.wait_ge(bu_done, pair + 1)
                for m in (2 * pair, 2 * pair + 1):
                    if m >= 4:
                        a.wait_ge(y_mm, m - 3)
                    nc.scalar.activation(pm[:, m % 4].rearrange("p i t -> p (i t)"), psum[:, 4 + pair % 2, :],
                                         ACT.Copy).then_inc(bu_copied, 1)

            def table_turn(m):
                if m >= 2 * NPAIR:
                    return
                pair, d = m // 2, m % 2
                a.wait_ge(tab_low, 2 * (m + 1))
                if m >= 1:
                    a.wait_ge(tcs_done, 2 * m)
                c128, s128 = par[:, 1, d, pair:pair + 1], par[:, 2, d, pair:pair + 1]
                co, so = [tcs[:, m % 4, k, 0:T // 2] for k in range(2)]
                for dst, src, by in ((tcs[:, m % 4, 0, T // 2:T], co, c128), (turned[:, 0], so, s128),
                                     (tcs[:, m % 4, 1, T // 2:T], so, c128), (turned[:, 1], co, s128)):
                    nc.scalar.activation(dst, src, ACT.Copy, scale=by).then_inc(tab_turned, 1)

            a.wait_ge(rpb_out, 16)
            take_bu(0)
            table_turn(0)
            for j in range(J_Q, J_GLU):
                slots = S5_SLOTS[j]
                for k in range(3):
                    if k < len(slots):
                        table_turn(2 * slots[k] + 1)
                        t = gelu_tile(slots[k])
                        if t is not None:
                            a.wait_ge(gelu_in, t + 1)
                            inner = psum[:, 6 + t % 2, T:2 * T]
                            nc.scalar.activation(inner, inner, ACT.Tanh, scale=GELU_A * GELU_B).then_inc(gelu_tanh, 1)
                    if k == 0:
                        high(0, j, 0, 3)
                        if j > J_Q:
                            take_halves(0, j - 1, 0)
                    high(0, j, 1, k)
                    if k < len(slots):
                        take_bu(slots[k] + 1)
                        table_turn(2 * slots[k] + 2)
            take_halves(0, J_GLU - 1, 0)
            a.wait_ge(y_done, NT)
            a.dma_start(cnt_a[:], ins["c_cnt"]).then_inc(mask_in, 16)
            a.dma_start(neg_a[:], ins["c_neg_a"]).then_inc(mask_in, 16)
            a.wait_ge(t5_out, 16)
            a.wait_ge(rpb_out, 16)

            def load_bias_a(h):
                for qt in range(2):
                    skew = bass.AP(tensor=t5_dram.tensor, offset=h * 512 + 255 - P * qt, ap=[[HA * 512 - 1, P], [1, T]])
                    a.dma_start(bias_a[:, h % 2, qt, :], skew).then_inc(bias_in[h % 2], 16)

            def exps(hh, b, ss, sums):
                a.wait_ge(sc_max, hh + 1)
                for qt in range(2):
                    extra = {"accum_out": stat[:, b, 1, qt:qt + 1]} if sums else {}
                    nc.scalar.activation(ss[:, b, qt], ss[:, b, qt], ACT.Exp,
                                         bias=stat[:, b, 0, qt:qt + 1], **extra).then_inc(exp_done, 1)

            def probs_high(hh, b, pt):
                a.wait_ge(pt_tr, hh + 1)
                if not (isinstance(hh, int) and hh < 2):
                    a.wait_ge(pv_mm, hh - 1)
                nc.scalar.activation(pt[:, b, :, 0, :], psum[:, 6 + b].rearrange("p (k t) -> p k t", k=2),
                                     ACT.Copy).then_inc(pt_hi, 1)

            def out_high(hh, b, dst):
                a.wait_ge(pv_mm, hh + 1)
                nc.scalar.activation(dst, psum[:, 6 + b, 0:T], ACT.Copy).then_inc(o_hi, 1)

            def head_high(h):
                if h >= 3:
                    a.wait_ge(pv_mm, h - 2)
                nc.scalar.activation(qk_s[:, h % 3, :, 0], qk_a[:, :, h], ACT.Copy).then_inc(head_hi, 1)
                nc.scalar.activation(v_s[:, h % 3, 0].rearrange("p (k d) -> p k d", k=2),
                                     v_a[:, :, h * HD:(h + 1) * HD], ACT.Copy).then_inc(head_hi, 1)

            load_bias_a(0)
            load_bias_a(1)
            head_high(0)
            for t in range(NT):
                a.wait_ge(gelu_out, t + 1)
                nc.scalar.activation(act[:, NT + t, 0, :], u[:, t], ACT.Copy, scale=0.5).then_inc(y_hi, 1)
            exps(0, 0, ss_a, False)
            head_high(1)

            def head_step(g):
                if g < HA:
                    probs_high(g, g % 2, pt_a)
                if g + 1 < HA:
                    exps(g + 1, (g + 1) % 2, ss_a, False)
                if 1 <= g <= HA:
                    out_high(g - 1, (g - 1) % 2, act[:, g - 1, 0, :])
                if g + 2 < HA:
                    head_high(g + 2)
                    a.wait_ge(sc_sum, g + 1)
                    load_bias_a(g + 2)

            def gate_tanh(g):
                for f in (g - 2, g - 1):
                    a.wait_ge(tiles_out, tile0(J_GLU) + f + 1)
                    nc.scalar.activation(ysum[:, f % 2], ysum[:, f % 2], ACT.Tanh, scale=0.5).then_inc(glu_tanh, 1)

            high(0, J_GLU, 0, 3)
            for g in range(9):
                if g < 7:
                    high(0, J_GLU + 1 + g // 4, 0, g % 4)
                head_step(g)
                if g % 2:
                    take_halves(0, J_GLU + g // 4, 0, glu_group=g // 2 % 2)
                elif g:
                    gate_tanh(g)
            for f in range(NT):
                a.wait_ge(glu_out, f + 1)
                nc.scalar.activation(act[:, NT + f, 0, :], u[:, f], ACT.Copy, scale=0.25).then_inc(ob_hi, 1)
            loop_blocks(J_OUT0, 8)
            mlp(1, J_MLP0, 32)
            input_high(2, 16)
            a.dma_start(neg_c[:], ins["c_neg_c"]).then_inc(mask_in, 16)

            def outs_high_c(turn, pair):
                for b in range(2):
                    h = turn * 4 + (2 * pair + b)
                    out_high(h + HA, b, at_head(o_c, h, 0))

            def qkv_blocks(turn, first=False):
                t3 = turn * 3
                for jb in range(6):
                    pair, kind = jb // 3, jb % 3
                    high(t3, J_QKV1, jb, 3)
                    if first and jb == 0:
                        rms(2)
                    for k in range(3):
                        high(t3, J_QKV1, jb + 1, k)
                        if kind == 2 and k == 1:
                            for b in range(2):
                                exps(turn * 4 + (HA + 2 * pair + b), b, ss_c, True)
                        if kind == 0 and k == 0 and not (first and pair == 0):
                            for b in range(2):
                                probs_high(turn * 4 + (HA + 2 * pair - 2 + b), b, pt_c)
                        if kind == 0 and k == 2 and not (first and pair == 0):
                            outs_high_c(turn, pair - 1)
                    take_halves(t3, J_QKV1, jb)

            qkv_blocks(0, first=True)
            with a.Fori(1, 4) as turn:
                qkv_blocks(turn)
            high(0, J_OUT1, 0, 3)
            for s in range(3):
                high(0, J_OUT1, 1, s)
                if s == 0:
                    for b in range(2):
                        probs_high(HA + HC - 2 + b, b, pt_c)
                if s == 2:
                    outs_high_c(4, -1)
            take_halves(0, J_OUT1, 0)
            block_step(0, J_OUT1, 1)
            loop_blocks(J_OUT1, 8, first=True)
            mlp(3, J_MLP1, 48, last=True)
            a.wait_ge(norm_mm, 4)
            nc.scalar.activation(tok[:, 0:2], psum[:, 3, 0:2], ACT.Sqrt, bias=eps_c, scale=1.0 / D).then_inc(tok_std, 1)
            a.wait_ge(tok_inv, 3)
            for g in range(0, 8, 2):
                a.wait_ge(fin_tr, g + 1)
                nc.scalar.activation(outs[:, g], psum[:, (4 + g) % 8, :], ACT.Copy, scale=tok[:, 2:3]) \
                    .then_inc(fin_ev[0], 1)

        @block.vector
        def _(v):
            def ts(dst, src, c0, c1, op0=ALU.mult, op1=ALU.add):
                return nc.vector.tensor_scalar(dst, src, c0, c1, op0, op1)

            def tt(dst, s0, s1, op):
                return nc.vector.tensor_tensor(dst, s0, s1, op)

            def stt(dst, s0, c, s1, op0, op1):
                return nc.vector.scalar_tensor_tensor(out=dst, in0=s0, scalar=c, in1=s1, op0=op0, op1=op1)

            v.wait_ge(small_step, 4)
            nc.vector.reciprocal(rows[:, 15], rows[:, 15]).then_inc(lam_inv, 1)

            v.wait_ge(tok_std, 1)
            nc.vector.reciprocal(tok[:, 2:4], tok[:, 0:2]).then_inc(tok_inv, 1)
            v.wait_ge(tok_inv, 1)
            for tt_ in range(2):
                nc.vector.tensor_scalar(xn[:, tt_], xin[:, tt_], tok[:, 2 + tt_:3 + tt_], None, ALU.mult) \
                    .then_inc(xn_done, 1)
            v.wait_ge(g_tr, 1)
            nc.vector.tensor_copy(gcol[:], psum[:, 0, 0:88]).then_inc(g_ready, 1)

            def low(i, j0, jb, s):
                jp = (j0 + jb) % 2
                piece = 2 * jp + s // 2
                v.wait_ge(hi_done, i * 8 + (4 * (j0 + jb) + s + 1))
                tt(whl[:, s, :, 1, :], raw[:, piece, SUBK * (s % 2):SUBK * (s % 2 + 1), :],
                   whl[:, s, :, 0, :].bitcast(F32), ALU.subtract).then_inc(lo_done, 1)

            def tile_sum(i, j0, jb, n, dst, glu_group=None):
                banks = 2 * ((j0 + jb) % 2 if glu_group is None else glu_group)
                t = tile0(j0 + jb) + (0 if glu_group is None else 2 * glu_group)
                v.wait_ge(half_done, i * 4 + (t + n + 1))
                tt(dst, psum[:, banks + n, 0:T], half[:, n], ALU.add).then_inc(tiles_out, 1)
                return i * 4 + (t + n + 1)

            def store(dst_of):
                def evac(i, j0, jb):
                    for n in range(2):
                        tile_sum(i, j0, jb, n, dst_of(i, j0, jb, n))
                return evac

            def residual(x0):
                def evac(i, j0, jb):
                    v.wait_ge(x_ready, i * 4 + (x0 + 2 * jb))
                    for n in range(2):
                        tile_sum(i, j0, jb, n, ysum[:, n])
                    for n in range(2):
                        v.wait_ge(tiles_out, i * 4 + (tile0(j0 + jb) + n + 1))
                        dst = x[:, bass.ds(i * 4 + (2 * jb + n), 1), :].rearrange("p o t -> p (o t)")
                        tt(dst, dst, ysum[:, n], ALU.add).then_inc(x_ready, 1)
                return evac

            def squared_relu(h0):
                def evac(i, j0, jb):
                    at_ = [i * 4 + (h0 + 2 * jb + n + 1) for n in range(2)]

                    def dst(n, part):
                        return hid[:, bass.ds(i * 4 + (2 * jb + n), 1), part, :].rearrange("p o t -> p (o t)")

                    if not (isinstance(i, int) and i * 4 + h0 + 2 * jb == 0):
                        v.wait_ge(relu_sq, i * 4 + (h0 + 2 * jb))
                        v.wait_ge(hid_ready, i * 4 + (h0 + 2 * jb))
                    for n in range(2):
                        tile_sum(i, j0, jb, n, ysum[:, n])
                    for n in range(2):
                        v.wait_ge(tiles_out, i * 4 + (tile0(j0 + jb) + n + 1))
                        tt(hsq[:, n], ysum[:, n], rsq[:], ALU.mult).then_inc(relu_scaled, 1)
                    for n in range(2):
                        v.wait_ge(relu_scaled, at_[n])
                        stt(hsq[:, n], ysum[:, n], 0.0, hsq[:, n], ALU.max, ALU.mult).then_inc(relu_sq, 1)
                    for n in range(2):
                        v.wait_ge(relu_sq, at_[n])
                        nc.vector.tensor_copy(dst(n, 0), hsq[:, n]).then_inc(hid_hi, 1)
                    for n in range(2):
                        v.wait_ge(hid_hi, at_[n])
                        tt(dst(n, 1), hsq[:, n], dst(n, 0).bitcast(F32), ALU.subtract).then_inc(hid_ready, 1)
                return evac

            def block_step(i, j0, jb, evac, last=False):
                low(i, j0, jb, 3)
                if not last:
                    for s in range(3):
                        low(i, j0, jb + 1, s)
                evac(i, j0, jb)

            def loop_blocks(j0, n, evac, first=False, last=False):
                with v.Fori(1 if first else 0, n // 2 - (1 if last else 0)) as i:
                    block_step(i, j0, 0, evac)
                    block_step(i, j0, 1, evac)
                if last:
                    block_step(n // 2 - 1, j0, 0, evac)
                    block_step(n // 2 - 1, j0, 1, evac, last=True)

            def input_low(n, gains):
                for kt in range(KT):
                    v.wait_ge(act_hi, KT * n + kt + 1)
                    stt(act[:, kt, 1, :], x[:, kt], gcol[:, gains + kt:gains + kt + 1],
                        act[:, kt, 0, :].bitcast(F32), ALU.mult, ALU.subtract).then_inc(act_ready, 1)

            def inverse_rms(n):
                v.wait_ge(norm_std, n)
                nc.vector.reciprocal(rstd[:], rstd[:]).then_inc(norm_rstd, 1)
                v.wait_ge(norm_rstd, n)
                if n in (1, 3):
                    tt(rsq[:], rstd[:], rstd[:], ALU.mult).then_inc(rsq_done, 1)
                    v.wait_ge(rsq_done, (n + 1) // 2)
                if n == 2:
                    v.wait_ge(tok_std, 2)
                    nc.vector.reciprocal(tok[:, 2:4], tok[:, 0:2]).then_inc(tok_inv, 1)
                    v.wait_ge(tok_inv, 2)

            for s in range(3):
                low(0, 0, 0, s)
            v.wait_ge(g_ready, 1)
            for kt in range(KT):
                v.wait_ge(act_hi, 2 * (kt // 2 + 1))
                stt(act[:, kt, 1, :], psum[:, 4 + kt // 2 % 4, kt % 2 * T:(kt % 2 + 1) * T], gcol[:, kt:kt + 1],
                    act[:, kt, 0, :].bitcast(F32), ALU.mult, ALU.subtract).then_inc(act_ready, 1)

            u_store = store(lambda i, j0, jb, n: u[:, 2 * (j0 + jb - J_U) + n])
            low(0, 0, 0, 3)

            for s in range(3):
                low(0, 1, 0, s)
            u_store(0, 0, 0)
            low(0, 1, 0, 3)
            for s in range(3):
                low(0, 2, 0, s)

            v.wait_ge(par_tr, 1)
            pv_ = psum[:, 4, :].rearrange("p (k r g) -> p k r g", k=4, g=2)
            zi_ = psum[:, 5, 0:P].rearrange("p (r g) -> p r g", g=2)
            for g in range(2):
                s_ = slice(NST * g, NST * (g + 1))
                nc.vector.tensor_copy(par[s_].rearrange("p k d r -> p k (d r)"), pv_[s_, 0:3, :, g]).then_inc(par_ready, 1)
            for g in range(2):
                s_ = slice(NST * g, NST * (g + 1))
                zr = pv_[s_, 3, :, g].rearrange("p (d r) -> p d r", d=2)
                zi = zi_[s_, :, g].rearrange("p (d r) -> p d r", d=2)
                for k, src, sign in ((0, zr, 1.0), (1, zi, -1.0), (2, zr, -1.0)):
                    nc.vector.tensor_scalar(zt[s_, :, k, :, g], src, sign, None, ALU.mult).then_inc(par_ready, 1)

            u_store(0, 1, 0)
            for g in range(KT // 2):
                v.wait_ge(x_tr, g + 1)
                nc.vector.tensor_copy(x[:, 2 * g:2 * g + 2].rearrange("p k t -> p (k t)"),
                                      psum[:, 4 + g % 4, :]).then_inc(x_ready, 2)
            def c_times_z(c):
                d, t = c // NT, c % NT
                v.wait_ge(c_tr, c + 1)
                if c:
                    v.wait_ge(f_ready, 2 * c)
                src = psum[:, 4 + c % 2, 0:2 * P].rearrange("p (i r c) -> p i r c", i=2, c=CH)
                for k in range(2):
                    z = zt[:, d, k:k + 2, PT * t:PT * (t + 1), :].rearrange("p i r g -> p i (r g)")
                    tt(ctmp[:, k].rearrange("p i (r c) -> p i r c", c=CH), src,
                       z.unsqueeze(3).to_broadcast([P, 2, 2 * PT, CH]), ALU.mult).then_inc(c_mul, 1)
                for k in range(2):
                    v.wait_ge(c_mul, 2 * c + k + 1)
                    tt(fmat[:, d, k, PT * t:PT * (t + 1), :].rearrange("p r c -> p (r c)"),
                       ctmp[:, k, 0], ctmp[:, k, 1], ALU.add).then_inc(f_ready, 1)

            low(0, 2, 0, 3)
            v.wait_ge(par_ready, 8)
            v.wait_ge(x_tr, 8)
            for j in (2, 3):
                for k in range(3):
                    low(0, j + 1, 0, k)
                    c_times_z(8 * (j - 2) + 2 * k)
                    c_times_z(8 * (j - 2) + 2 * k + 1)
                u_store(0, j, 0)
                if j == 2:
                    low(0, 3, 0, 3)
                c_times_z(8 * (j - 2) + 6)
                c_times_z(8 * (j - 2) + 7)

            def terms(m):
                pair, d, sl = m // 2, m % 2, m % 4
                add, sub = (ALU.add, ALU.subtract) if d == 0 else (ALU.subtract, ALU.add)
                cosine, sine = [tcs[:, sl, k].unsqueeze(1).to_broadcast([P, 2, T]) for k in range(2)]
                return pair, d, sl, add, sub, cosine, sine

            def times_sine(m):
                pair, d, sl, add, sub, cosine, sine = terms(m)
                v.wait_ge(pm_done, m + 1)
                tt(p2[:, m % 2], psum[:, 4 + pair % 2].rearrange("p (i t) -> p i t", i=2)[:, ::-1], sine, ALU.mult).then_inc(sin_in, 1)

            def into_frame(m):
                pair, d, sl, add, sub, cosine, sine = terms(m)
                v.wait_ge(sin_in, m + 1)
                tt(pm[:, sl, 0], pm[:, sl, 0], p2[:, m % 2, 0], add).then_inc(frame_in, 1)
                tt(pm[:, sl, 1], pm[:, sl, 1], p2[:, m % 2, 1], sub).then_inc(frame_in, 1)

            def scan(m):
                pair, d, sl, add, sub, cosine, sine = terms(m)
                r = par[:, 0, d, pair:pair + 1].to_broadcast([P, T])
                step = 1 if d == 0 else -1
                v.wait_ge(frame_in, 2 * (m + 1))
                for i in range(2):
                    nc.vector.tensor_tensor_scan(p2[:, m % 2, i, ::step], r, pm[:, sl, i, ::step], 0.0,
                                                 ALU.mult, ALU.add).then_inc(scanned, 1)

            def out_products(m):
                pair, d, sl, add, sub, cosine, sine = terms(m)
                v.wait_ge(scanned, 2 * (m + 1))
                if m >= 1:
                    v.wait_ge(rot_done, 2 * m)
                tt(pm[:, sl], p2[:, m % 2], cosine, ALU.mult).then_inc(frame_out, 1)
                tt(ysum[:], p2[:, m % 2, ::-1], sine, ALU.mult).then_inc(frame_out, 1)

            def out_of_frame(m):
                pair, d, sl, add, sub, cosine, sine = terms(m)
                v.wait_ge(frame_out, 2 * (m + 1))
                tt(pm[:, sl, 0], pm[:, sl, 0], ysum[:, 0], sub).then_inc(rot_done, 1)
                tt(pm[:, sl, 1], pm[:, sl, 1], ysum[:, 1], add).then_inc(rot_done, 1)

            def s5_slot(q):
                t = gelu_tile(q)
                inner = psum[:, 6 + (t or 0) % 2, T:2 * T]
                if t is not None:
                    v.wait_ge(y_mm, 2 * PT * (t + 1))
                    stt(u[:, t], u[:, t], gcol[:, 80 + t:81 + t], psum[:, 6 + t % 2, 0:T], ALU.mult, ALU.add) \
                        .then_inc(y_done, 1)
                for m in (2 * q, 2 * q + 1):
                    if m < 2 * NPAIR:
                        times_sine(m)
                    if t is not None and m % 2 == 0:
                        v.wait_ge(y_done, t + 1)
                        tt(inner, u[:, t], u[:, t], ALU.mult).then_inc(gelu_square, 1)
                    if 1 <= m <= 2 * NPAIR:
                        out_products(m - 1)
                    if t is not None and m % 2 == 0:
                        v.wait_ge(gelu_square, t + 1)
                        stt(inner, inner, 1.0 / GELU_A, u[:, t], ALU.add, ALU.mult).then_inc(gelu_in, 1)
                    if m < 2 * NPAIR:
                        into_frame(m)
                    if 1 <= m <= 2 * NPAIR:
                        out_of_frame(m - 1)
                    if m < 2 * NPAIR:
                        scan(m)
                if t is not None:
                    v.wait_ge(gelu_tanh, t + 1)
                    stt(u[:, t], inner, 1.0, u[:, t], ALU.add, ALU.mult).then_inc(gelu_out, 1)

            q_store = store(lambda i, j0, jb, n: qk_a[:, 0, 2 * (j0 + jb - J_Q) + n])
            k_store = store(lambda i, j0, jb, n: qk_a[:, 1, 2 * (j0 + jb - J_K) + n])
            v_store = store(lambda i, j0, jb, n: v_a[:, n, BLK * (j0 + jb - J_V):BLK * (j0 + jb - J_V + 1)])
            kinds = [q_store] * 4 + [k_store] * 4 + [v_store] * 4
            for j in range(J_Q, J_GLU):
                slots = S5_SLOTS[j]
                for k in range(3):
                    if k < len(slots):
                        s5_slot(slots[k])
                    if k == 0:
                        low(0, j, 0, 3)
                        if j > J_Q:
                            kinds[j - 1 - J_Q](0, j - 1, 0)
                    low(0, j, 1, k)
            kinds[-1](0, J_GLU - 1, 0)

            def scores(hh, b, ss, bias):
                v.wait_ge(sc_mm, hh + 1)
                v.wait_ge(bias_masked, hh + 1)
                if not (isinstance(hh, int) and hh < 2):
                    v.wait_ge(pt_tr, hh - 1)
                stt(ss[:, b].rearrange("p q t -> p (q t)"), psum[:, 4 + b, :], SCALE,
                    bias[:, b].rearrange("p q t -> p (q t)"), ALU.mult, ALU.add).then_inc(sc_sum, 1)
                v.wait_ge(sc_sum, hh + 1)
                nc.vector.tensor_reduce(stat[:, b, 0], ss[:, b], AX_X, ALU.max, negate=True).then_inc(sc_max, 1)

            def probs(hh, b, ss, cnt):
                v.wait_ge(exp_done, hh * 2 + 2)
                if cnt is not None:
                    for qt in range(2):
                        nc.vector.scalar_tensor_tensor(out=ss[:, b, qt], in0=ss[:, b, qt], scalar=1.0,
                                                       in1=cnt[:, qt], op0=ALU.mult, op1=ALU.mult,
                                                       accum_out=stat[:, b, 1, qt:qt + 1]).then_inc(cnt_done, 1)
                    v.wait_ge(cnt_done, 2 * hh + 2)
                nc.vector.reciprocal(stat[:, b, 2], stat[:, b, 1]).then_inc(inv_done, 1)
                v.wait_ge(inv_done, hh + 1)
                for qt in range(2):
                    nc.vector.tensor_scalar(ss[:, b, qt], ss[:, b, qt], stat[:, b, 2, qt:qt + 1],
                                            None, ALU.mult).then_inc(prob_done, 1)

            def probs_low(hh, b, pt):
                v.wait_ge(pt_hi, hh + 1)
                tt(pt[:, b, :, 1, :], psum[:, 6 + b].rearrange("p (k t) -> p k t", k=2),
                   pt[:, b, :, 0, :].bitcast(F32), ALU.subtract).then_inc(pt_ready, 1)

            def out_low(hh, b, dst, high_half):
                v.wait_ge(o_hi, hh + 1)
                tt(dst, psum[:, 6 + b, 0:T], high_half.bitcast(F32), ALU.subtract).then_inc(o_ready, 1)

            def head_step(g):
                if g + 1 < HA:
                    scores(g + 1, (g + 1) % 2, ss_a, bias_a)
                if g < HA:
                    probs_low(g, g % 2, pt_a)
                if 1 <= g <= HA:
                    out_low(g - 1, (g - 1) % 2, act[:, g - 1, 1, :], act[:, g - 1, 0, :])
                if g + 1 < HA:
                    probs(g + 1, (g + 1) % 2, ss_a, cnt_a)

            for t in range(NT):
                v.wait_ge(y_hi, t + 1)
                stt(act[:, NT + t, 1, :], u[:, t], 0.5, act[:, NT + t, 0, :].bitcast(F32), ALU.mult, ALU.subtract) \
                    .then_inc(y_split, 1)
            v.wait_ge(mask_in, 32)
            scores(0, 0, ss_a, bias_a)
            probs(0, 0, ss_a, cnt_a)

            low(0, J_GLU, 0, 3)
            for g in range(9):
                if g < 7:
                    low(0, J_GLU + 1 + g // 4, 0, g % 4)
                head_step(g)
                if g % 2:
                    if g > 1:
                        v.wait_ge(glu_out, g - 1)
                    for n in range(2):
                        tile_sum(0, J_GLU + g // 4, 0, n, ysum[:, n], glu_group=g // 2 % 2)
                elif g:
                    for f in (g - 2, g - 1):
                        v.wait_ge(glu_tanh, f + 1)
                        stt(u[:, f], ysum[:, f % 2], 1.0, u[:, f], ALU.add, ALU.mult).then_inc(glu_out, 1)
            for f in range(NT):
                v.wait_ge(ob_hi, f + 1)
                stt(act[:, NT + f, 1, :], u[:, f], 0.25, act[:, NT + f, 0, :].bitcast(F32), ALU.mult, ALU.subtract) \
                    .then_inc(ob_ready, 1)
            loop_blocks(J_OUT0, 8, residual(16))

            def mlp(n, j0, gains, x0, h0, last=False):
                input_low(n, gains)
                evac = squared_relu(h0)
                v.wait_ge(x_ready, x0)
                low(0, j0, 0, 3)
                inverse_rms(n)
                for s in range(3):
                    low(0, j0, 1, s)
                evac(0, j0, 0)
                block_step(0, j0, 1, evac)
                for qu in range(4):
                    if qu:
                        v.wait_ge(x_ready, x0 + 16 * qu)
                        evac = squared_relu(h0 + 16 * qu)
                    loop_blocks(j0 + 16 * qu, 8, evac, first=(qu == 0))
                    v.wait_ge(relu_sq, h0 + 16 * (qu + 1))
                    loop_blocks(j0 + 16 * qu + 8, 8, residual(x0 + 16 * qu), last=(last and qu == 3))

            mlp(1, J_MLP0, 32, 32, 0)
            input_low(2, 16)

            def split_store(turn, jb):
                pair, kind = jb // 3, jb % 3
                t3, at_ = turn * 3, [turn * 12 + (2 * jb + n + 1) for n in range(2)]

                def dst(n, part):
                    return v_c[:, pair, n, part, :] if kind == 2 else qk_c[:, pair, kind, n, part, :]

                if not (isinstance(turn, int) and jb == 0):
                    v.wait_ge(qkv_ready, turn * 12 + 2 * jb)
                for n in range(2):
                    tile_sum(t3, J_QKV1, jb, n, ysum[:, n])
                for n in range(2):
                    v.wait_ge(tiles_out, t3 * 4 + (tile0(J_QKV1 + jb) + n + 1))
                    if kind == 2:
                        scaled = nc.vector.tensor_scalar(ysum[:, n], ysum[:, n], tok[:, 2 + n:3 + n], None, ALU.mult)
                    else:
                        scaled = tt(ysum[:, n], ysum[:, n], rstd[:], ALU.mult)
                    scaled.then_inc(qkv_scaled, 1)
                for n in range(2):
                    v.wait_ge(qkv_scaled, at_[n])
                    nc.vector.tensor_copy(dst(n, 0), ysum[:, n]).then_inc(qkv_hi, 1)
                for n in range(2):
                    v.wait_ge(qkv_hi, at_[n])
                    tt(dst(n, 1), ysum[:, n], dst(n, 0).bitcast(F32), ALU.subtract).then_inc(qkv_ready, 1)

            def outs_low_c(turn, pair):
                for b in range(2):
                    h = turn * 4 + (2 * pair + b)
                    out_low(h + HA, b, at_head(o_c, h, 1), at_head(o_c, h, 0))

            def qkv_blocks(turn, first=False):
                t3 = turn * 3
                for jb in range(6):
                    pair, kind = jb // 3, jb % 3
                    head = [turn * 4 + (HA + 2 * pair + b) for b in range(2)]
                    low(t3, J_QKV1, jb, 3)
                    if first and jb == 0:
                        inverse_rms(2)
                    for k in range(3):
                        low(t3, J_QKV1, jb + 1, k)
                        for b in range(2):
                            if kind == 2 and k == 1:
                                scores(head[b], b, ss_c, bias_c)
                            if kind == 2 and k == 2:
                                probs(head[b], b, ss_c, None)
                            if kind == 0 and k == 0 and not (first and pair == 0):
                                probs_low(head[b] - 2, b, pt_c)
                        if kind == 0 and k == 2 and not (first and pair == 0):
                            outs_low_c(turn, pair - 1)
                    split_store(turn, jb)

            qkv_blocks(0, first=True)
            with v.Fori(1, 4) as turn:
                qkv_blocks(turn)
            evac_out1 = residual(96)
            low(0, J_OUT1, 0, 3)
            for s in range(3):
                low(0, J_OUT1, 1, s)
                if s == 0:
                    for b in range(2):
                        probs_low(HA + HC - 2 + b, b, pt_c)
                if s == 2:
                    outs_low_c(4, -1)
            evac_out1(0, J_OUT1, 0)
            block_step(0, J_OUT1, 1, evac_out1)
            with v.Fori(1, 4) as i:
                block_step(i, J_OUT1, 0, evac_out1)
                block_step(i, J_OUT1, 1, evac_out1)
            mlp(3, J_MLP1, 48, 112, 64, last=True)
            for kt in range(KT):
                v.wait_ge(x_ready, X_BEFORE[4] + kt + 1)
                nc.vector.tensor_scalar(xfin[:, kt], x[:, kt], gcol[:, 64 + kt:65 + kt], None, ALU.mult) \
                    .then_inc(final_done, 1)
            v.wait_ge(tok_std, 3)
            nc.vector.reciprocal(tok[:, 2:4], tok[:, 0:2]).then_inc(tok_inv, 1)
            v.wait_ge(tok_inv, 3)
            for g in range(1, 8, 2):
                v.wait_ge(fin_tr, g + 1)
                nc.vector.tensor_scalar(outs[:, g], psum[:, (4 + g) % 8, :], tok[:, 3:4], None, ALU.mult) \
                    .then_inc(fin_ev[1], 1)

        @block.tensor
        def _(pe):
            pe.wait_ge(ident_in, 16)
            pe.wait_ge(gain_in, 16 * 4)
            pe.transpose(psum[:, 0, 0:88], grow[:, :], ident[0:88, 0:88]).then_inc(g_tr, 1)

            def transpose_x(src, g):
                for k in range(2):
                    for tt_ in range(2):
                        kt = 2 * g + k
                        last = pe.transpose(psum[:, 4 + g % 4, k * T + tt_ * P:k * T + (tt_ + 1) * P],
                                            src[:, tt_, kt * P:(kt + 1) * P], ident[:])
                return last

            pe.wait_ge(xn_done, 2)
            for g in range(KT // 2):
                if g >= 4:
                    pe.wait_ge(act_ready, 2 * (g - 3))
                transpose_x(xn, g).then_inc(xn_tr, 1)

            def norm(n):
                pe.wait_ge(ssum_done, KT * n)
                if n == 2:
                    for tt_ in range(2):
                        pe.matmul(psum[:, 7, T + tt_:T + tt_ + 1], ssum[:, tt_ * P:(tt_ + 1) * P], ones[:, 0:1],
                                  start=True, stop=True)
                pe.matmul(psum[:, 7, 0:T], ones[:], ssum[:], start=True, stop=True).then_inc(norm_mm, 1)

            def block_mm(i, j0, jb, operand, ready, token_major=False, between=None):
                banks = 2 * ((j0 + jb) % 2)
                t = tile0(j0 + jb)
                if t >= 4:
                    pe.wait_ge(tiles_out, i * 4 + (t - 2))
                for s in range(4):
                    pe.wait_ge(lo_done, i * 8 + (4 * (j0 + jb) + s + 1))
                    for k in range(SUBK):
                        kt = SUBK * s + k
                        ready(kt)
                        first, final = kt == 0, kt == KT - 1
                        for n in range(2):
                            cols = slice(n * P, (n + 1) * P)
                            if token_major:
                                w_hi, w_all = whl[:, s, k, 0, :], whl[:, s, k, :, :].rearrange("p h t -> p (h t)")
                                big = (operand[:, kt, 0, cols], w_all)
                                little = (operand[:, kt, 1, cols], w_hi)
                            else:
                                big = (whl[:, s, k, 0, cols], operand[:, kt, :, :].rearrange("p h t -> p (h t)"))
                                little = (whl[:, s, k, 1, cols], operand[:, kt, 0, :])
                            bank = psum[:, banks + n]
                            pe.matmul(bank, *big, start=first, stop=False, skip_group_check=True)
                            last = pe.matmul(bank[:, 0:T], *little, start=False, stop=final, skip_group_check=True)
                    last.then_inc(subs_used, 1)
                    if between:
                        between(s)

            def by_count(semaphore, base, group=2):
                def ready(kt):
                    if kt % group == 0:
                        pe.wait_ge(semaphore, base + kt + group)
                return ready

            def nothing(kt):
                pass

            def loop_blocks(j0, n, operand, ready, token_major=False):
                with pe.Fori(0, n // 2) as i:
                    block_mm(i, j0, 0, operand, ready, token_major)
                    block_mm(i, j0, 1, operand, ready, token_major)

            pe.wait_ge(g_ready, 1)

            def transpose_par():
                pe.wait_ge(act_ready, KT)
                pe.wait_ge(small_step, SMALL_STEPS)
                pe.wait_ge(step_a, 2)
                for k, src in enumerate((3, 14, 13, 5, 6)):
                    last = pe.transpose(psum[:, 4 + k // 4, (k % 4) * P:(k % 4 + 1) * P], rows[:, src], ident[:])
                last.then_inc(par_tr, 1)

            def transpose_b(g):
                pe.wait_ge(b_in, 16 * 4)
                if g < 2:
                    pe.wait_ge(act_ready, KT)
                else:
                    pe.wait_ge(bt_ready, g - 1)
                for k in range(4):
                    t, i = 2 * g + k // 2, k % 2
                    last = pe.transpose(psum[:, 6 + g % 2, k * P:(k + 1) * P],
                                        bnat[:, i, PT * t:PT * (t + 1), :].rearrange("p r c -> p (r c)"), ident[:])
                last.then_inc(b_tr, 1)

            def transpose_c(c):
                d, t = c // NT, c % NT
                pe.wait_ge(c_in, 16 * 8)
                pe.wait_ge(x_ready, KT)
                if c >= 2:
                    pe.wait_ge(c_mul, 2 * (c - 1))
                for i in range(2):
                    last = pe.transpose(psum[:, 4 + c % 2, i * P:(i + 1) * P],
                                        cnat[:, d, i, t].rearrange("p w s -> p (w s)"), ident[:])
                last.then_inc(c_tr, 1)

            def between_first(s):
                if s in (1, 2):
                    transpose_b(2 * (s - 1))
                    transpose_b(2 * (s - 1) + 1)

            block_mm(0, 0, 0, act, by_count(act_ready, 0), between=between_first)
            block_mm(0, 1, 0, act, nothing, between=lambda s: transpose_par() if s == 2 else None)
            pe.wait_ge(t5_in, 32)
            pe.wait_ge(bt_ready, 4)
            pe.matmul(psum[:HA, 7, :], t5tab[:], onehot[:], start=True, stop=True).then_inc(t5_mm, 1)
            for g in range(KT // 2):
                if g >= 4:
                    pe.wait_ge(x_ready, 2 * (g - 3))
                elif g == 3:
                    pe.wait_ge(t5_ev, 1)
                elif g == 2:
                    pe.wait_ge(bt_ready, 4)
                else:
                    pe.wait_ge(par_ready, 8)
                transpose_x(xin, g).then_inc(x_tr, 1)
            for j in (2, 3):
                def between_c(s, j=j):
                    transpose_c(8 * (j - 2) + 2 * s)
                    transpose_c(8 * (j - 2) + 2 * s + 1)

                block_mm(0, j, 0, act, nothing, between=between_c)

            def s5_in(pair):
                if pair >= NPAIR:
                    return
                t, r = pair // PT, slice(32 * (pair % PT), 32 * (pair % PT + 1))
                if pair >= 2:
                    pe.wait_ge(frame_in, 4 * (pair - 1))
                else:
                    pe.wait_ge(c_mul, 4 * NT)
                for i in range(2):
                    last = pe.matmul(psum[:, 4 + pair % 2, i * T:(i + 1) * T], bt[r, t, i, :], u[r, t, :],
                                     start=True, stop=True)
                last.then_inc(bu_done, 1)

            def s5_out(m):
                if not 0 <= m < 2 * NPAIR:
                    return
                pair, d = m // 2, m % 2
                t, r = pair // PT, slice(32 * (pair % PT), 32 * (pair % PT + 1))
                if t >= 2 and m % (2 * PT) == 0:
                    pe.wait_ge(y_done, t - 1)
                pe.wait_ge(rot_done, 2 * (m + 1))
                for i in range(2):
                    last = pe.matmul(psum[r, 6 + t % 2, 0:T], fmat[:, d, i, pair, :], pm[:, m % 4, i],
                                     start=(d == 0 and i == 0), stop=(d == 1 and i == 1))
                last.then_inc(y_mm, 1)

            pe.wait_ge(bt_ready, 4)
            pe.wait_ge(f_ready, 4 * NT)
            pe.wait_ge(tiles_out, 8)
            s5_in(0)
            for j in range(J_Q, J_GLU):
                slots = S5_SLOTS[j]

                def between(s, slots=slots):
                    if s < len(slots):
                        s5_in(slots[s] + 1)
                        s5_out(2 * slots[s] - 1)
                        s5_out(2 * slots[s])

                block_mm(0, j, 0, act, nothing, token_major=(j >= J_V), between=between)

            def exact(dst, products):
                for c, (w, m) in enumerate(products):
                    for p, (wp, mp) in enumerate(((0, 0), (0, 1), (1, 0))):
                        last = pe.matmul(dst, w(wp), m(mp), start=(c == 0 and p == 0),
                                         stop=(c == len(products) - 1 and p == 2), skip_group_check=True)
                return last

            def scores(hh, b, q, k):
                if not (isinstance(hh, int) and hh < 2):
                    pe.wait_ge(sc_sum, hh - 1)
                for qt in range(2):
                    last = exact(psum[:, 4 + b, qt * T:(qt + 1) * T],
                                 [(lambda part: q(part)[:, qt * P:(qt + 1) * P], k)])
                last.then_inc(sc_mm, 1)

            def transposes(hh, b, ss):
                pe.wait_ge(prob_done, hh * 2 + 2)
                if not (isinstance(hh, int) and hh < 2):
                    pe.wait_ge(o_ready, hh - 1)
                for kt in range(2):
                    for qt in range(2):
                        last = pe.transpose(psum[:, 6 + b, kt * T + qt * P:kt * T + (qt + 1) * P],
                                            ss[:, b, qt, kt * P:(kt + 1) * P], ident[:])
                last.then_inc(pt_tr, 1)

            def output(hh, b, values, pt):
                pe.wait_ge(pt_ready, hh + 1)
                exact(psum[:, 6 + b, 0:T],
                      [(lambda part, kt=kt: values(kt, part), lambda part, kt=kt: pt[:, b, kt, part, :])
                       for kt in range(2)]).then_inc(pv_mm, 1)

            def scores_a(h):
                pe.wait_ge(head_split, 2 * h + 2)
                scores(h, h % 2, lambda part: qk_s[:, h % 3, 0, part], lambda part: qk_s[:, h % 3, 1, part])

            def output_a(h):
                output(h, h % 2, lambda kt, part: v_s[:, h % 3, part, kt * P:(kt + 1) * P], pt_a)

            pe.wait_ge(tiles_out, tile0(J_GLU))
            pe.wait_ge(y_done, NT)
            scores_a(0)
            for g in range(8):
                jb, s = g // 4, g % 4
                half_block = s // 2
                if s % 2 == 0:
                    pe.wait_ge(tiles_out, tile0(J_GLU + jb) + 2 * half_block - 2)
                pe.wait_ge(lo_done, 4 * (J_GLU + jb) + s + 1)
                for k in range(SUBK):
                    kt = SUBK * (s % 2) + k
                    pe.wait_ge(y_split, kt + 1)
                    for n in range(2):
                        cols = slice(n * P, (n + 1) * P)
                        bank = psum[:, 2 * half_block + n]
                        pe.matmul(bank, whl[:, s, k, 0, cols], act[:, NT + kt].rearrange("p h t -> p (h t)"),
                                  start=(kt == 0), stop=False, skip_group_check=True)
                        last = pe.matmul(bank[:, 0:T], whl[:, s, k, 1, cols], act[:, NT + kt, 0, :],
                                         start=False, stop=(kt == NT - 1), skip_group_check=True)
                last.then_inc(subs_used, 1)
                if g + 1 < HA:
                    scores_a(g + 1)
                transposes(g, g % 2, ss_a)
                if g >= 1:
                    output_a(g - 1)
            output_a(HA - 1)

            def merged(kt):
                if kt < HA:
                    pe.wait_ge(o_ready, kt + 1)
                else:
                    pe.wait_ge(ob_ready, kt - HA + 1)

            loop_blocks(J_OUT0, 8, act, merged)

            def mlp(j0, n, h0):
                def squares(s):
                    if s == 1:
                        norm(n)

                block_mm(0, j0, 0, act, by_count(act_ready, KT * n), between=squares)
                block_mm(0, j0, 1, act, nothing)
                with pe.Fori(1, 4) as i:
                    block_mm(i, j0, 0, act, nothing)
                    block_mm(i, j0, 1, act, nothing)
                for qu in range(4):
                    if qu:
                        loop_blocks(j0 + 16 * qu, 8, act, nothing)
                    loop_blocks(j0 + 16 * qu + 8, 8, hid, by_count(hid_ready, h0 + 16 * qu, 4))

            mlp(J_MLP0, 1, 0)

            def scores_c(turn, pair):
                pe.wait_ge(qkv_ready, turn * 12 + (6 * pair + 4))
                for b in range(2):
                    scores(turn * 4 + (HA + 2 * pair + b), b,
                           lambda part: qk_c[:, pair, 0, b, part], lambda part: qk_c[:, pair, 1, b, part])

            def transposes_c(turn, pair):
                for b in range(2):
                    transposes(turn * 4 + (HA + 2 * pair + b), b, ss_c)

            def outputs_c(turn, slot, back):
                pe.wait_ge(qkv_ready, turn * 12 + (6 * back + 6))
                for b in range(2):
                    output(turn * 4 + (HA + 2 * back + b), b,
                           lambda kt, part: v_c[:, slot, kt, part, b * HD:(b + 1) * HD], pt_c)

            def qkv_blocks(turn, first=False):
                for jb in range(6):
                    pair, kind = jb // 3, jb % 3

                    def between(s):
                        if first and jb == 0 and s == 1:
                            norm(2)
                        if kind == 2 and s == 1:
                            scores_c(turn, pair)
                        if kind == 0 and s == 0 and not (first and pair == 0):
                            transposes_c(turn, pair - 1)
                        if kind == 0 and s == 2 and not (first and pair == 0):
                            outputs_c(turn, 1 - pair, pair - 1)

                    ready = by_count(act_ready, 2 * KT) if first and jb == 0 else nothing
                    block_mm(turn * 3, J_QKV1, jb, act, ready, token_major=(kind == 2), between=between)

            qkv_blocks(0, first=True)
            with pe.Fori(1, 4) as turn:
                qkv_blocks(turn)

            def last_outputs(s):
                if s == 0:
                    transposes_c(4, -1)
                if s == 2:
                    outputs_c(4, 1, -1)

            heads_ready = by_count(o_ready, HA, 2)
            block_mm(0, J_OUT1, 0, o_c, heads_ready, between=last_outputs)
            block_mm(0, J_OUT1, 1, o_c, nothing)
            with pe.Fori(1, 4) as i:
                block_mm(i, J_OUT1, 0, o_c, nothing)
                block_mm(i, J_OUT1, 1, o_c, nothing)
            mlp(J_MLP1, 3, 64)
            for g in range(8):
                q4, tt_ = g // 2, g % 2
                pe.wait_ge(final_done, 4 * q4 + 4)
                if g == 4:
                    pe.wait_ge(tiles_out, tile0(J_END))
                if g == 7:
                    pe.wait_ge(ssum_done, KT * 4)
                    for h in range(2):
                        last = pe.matmul(psum[:, 3, h:h + 1], ssum[:, h * P:(h + 1) * P], ones[:, 0:1],
                                         start=True, stop=True)
                    last.then_inc(norm_mm, 1)
                    pe.wait_ge(tok_std, 3)
                for k in range(4):
                    last = pe.transpose(psum[:, (4 + g) % 8, k * P:(k + 1) * P],
                                        xfin[:, 4 * q4 + k, tt_ * P:(tt_ + 1) * P], ident[:])
                last.then_inc(fin_tr, 1)


def shape_constants():
    rel = np.arange(T)[None, :] - np.arange(T)[:, None]
    branches = ((128, 1), (512, 4), (2048, 16))
    cnt = sum(((rel % d == 0) & (np.abs(rel) <= w // 2)).astype(np.float32) for w, d in branches)
    c = np.arange(GRID_W)
    start = np.clip(c - 8, 0, GRID_W - 16)
    ok = (c[None, :] >= start[:, None]) & (c[None, :] < start[:, None] + 16)
    ok = np.tile(ok, (ROWS, ROWS))
    d = np.arange(512) - 255
    n = np.abs(d)
    nf = np.maximum(n, 1).astype(np.float32)
    big = 8 + (np.log(nf / np.float32(8)) / np.float32(np.log(1024 / 8)) * np.float32(8)).astype(np.int32)
    bucket = np.where(d > 0, 16, 0) + np.where(n < 8, n, np.minimum(big, 15))
    fold = lambda m: np.ascontiguousarray(m.astype(np.float32).reshape(2, P, T).transpose(1, 0, 2))
    return {
        "c_ident": np.eye(P, dtype=np.float32),
        "c_onehot": (np.arange(32)[:, None] == bucket[None, :]).astype(np.float32),
        "c_cnt": fold(cnt),
        "c_neg_a": fold(np.where(cnt > 0, 0.0, NEG)),
        "c_neg_c": fold(np.where(ok, 0.0, NEG)),
    }


INPUTS = ["x", "t5_bias", "ab_w_in", "ab_w_out", "s5_lam_re", "s5_lam_im", "s5_log_step", "s5_b_re", "s5_b_im",
          "s5_c_re", "s5_c_im", "s5_d", "s5_w_glu", "c_w_qkv", "c_w_out", "c_rpb", "norm_mix", "norm_mlp",
          "mlp_w1", "mlp_w2", "norm_final"]


def kernel(**inputs):
    import concourse.bacc as bacc
    from concourse.bass_utils import run_bass_kernel_spmd

    nc = bacc.Bacc("TRN2", target_bir_lowering=False, num_devices=1)
    arrays = {name: np.ascontiguousarray(inputs[name]) for name in INPUTS} | shape_constants()
    ins = {name: nc.dram_tensor(f"in_{name}", a.shape, F32, kind="ExternalInput").ap() for name, a in arrays.items()}
    out = nc.dram_tensor("out_0", (1, T, D), F32, kind="ExternalOutput").ap()
    build(nc, ins, out)
    result = run_bass_kernel_spmd(nc, [{f"in_{name}": a for name, a in arrays.items()}], core_ids=[0])
    return result.results[0]["out_0"]
```
